# Optimizing a Trainium2 kernel written in Bass

```python
import jax
import jax.numpy as jnp
from jax import lax
import numpy as np

D_MODEL = 1024
BATCH = 1
SEQ = 256
DEPTH = 2

F32 = jnp.float32
NORM_EPS = 1e-6
PLE_DIM = 256
A_HEADS = 8
A_KV_HEADS = 2
HEAD_DIM = 64
ROPE_DIM = HEAD_DIM // 4
ROPE_THETA = 500000.0
IDX_HEADS = 4
IDX_DIM = 64
TOPK_MAX = 256
Q_BLOCK = 128
LRU_WIDTH = 512
LRU_BLOCKS = 8
CONV_W = 4
LRU_C = 8.0
EVEN_IN = A_HEADS * HEAD_DIM + 2 * A_KV_HEADS * HEAD_DIM + IDX_HEADS * IDX_DIM + IDX_DIM + IDX_HEADS + 2 * LRU_WIDTH
EVEN_MIX = A_HEADS * HEAD_DIM + LRU_WIDTH
SSD_INNER = 2 * D_MODEL
SSD_HEAD_DIM = 64
SSD_HEADS = SSD_INNER // SSD_HEAD_DIM
SSD_GROUPS = 4
SSD_STATE = 128
SSD_CHUNK = 128
SSD_CONV_CH = SSD_INNER + 2 * SSD_GROUPS * SSD_STATE
ODD_IN = SSD_INNER + SSD_CONV_CH + SSD_HEADS
D_FF = 3584
N_EXPERTS = 8
TOP_K = 2

kernel_name = 'hybrid_dsa_rglru_ssd_moe_ple'

def _split(u, widths):
    out, start = [], 0
    for w in widths:
        out.append(u[..., start:start + w])
        start += w
    return out

def rmsnorm(x, g):
    xf = x.astype(F32)
    y = xf * lax.rsqrt(jnp.mean(xf * xf, axis=-1, keepdims=True) + NORM_EPS)
    return (y * g.astype(F32)).astype(x.dtype)

def partial_rope(x, pos):
    half = ROPE_DIM // 2
    inv = ROPE_THETA ** (-jnp.arange(half, dtype=F32) / half)
    ang = pos.astype(F32)[:, None] * inv[None, :]
    cos = jnp.cos(ang)[None, :, None, :]
    sin = jnp.sin(ang)[None, :, None, :]
    xr = x[..., :ROPE_DIM].astype(F32)
    x1, x2 = xr[..., :half], xr[..., half:]
    rot = jnp.concatenate([x1 * cos - x2 * sin, x1 * sin + x2 * cos], axis=-1).astype(x.dtype)
    return jnp.concatenate([rot, x[..., ROPE_DIM:]], axis=-1)

def causal_dwconv(x, w, b):
    c = x.shape[-1]
    y = lax.conv_general_dilated(x, w[:, None, :], window_strides=(1,), padding=[(CONV_W - 1, 0)],
                                 dimension_numbers=('NWC', 'WIO', 'NWC'), feature_group_count=c)
    return y + b

def swiglu(h, wg, wu, wd):
    return (jax.nn.silu(h @ wg) * (h @ wu)) @ wd

def dsa_mixer(q, k, v, qi, ki, wi):
    bsz, seq = q.shape[0], q.shape[1]
    n_sel = min(TOPK_MAX, seq // 4)
    n_blk = seq // Q_BLOCK
    groups = A_HEADS // A_KV_HEADS
    kpos = jnp.arange(seq)
    wi = wi.astype(F32) * IDX_HEADS ** -0.5

    def block(j):
        t0 = j * Q_BLOCK
        qb = lax.dynamic_slice_in_dim(q, t0, Q_BLOCK, axis=1)
        qib = lax.dynamic_slice_in_dim(qi, t0, Q_BLOCK, axis=1)
        wib = lax.dynamic_slice_in_dim(wi, t0, Q_BLOCK, axis=1)
        tpos = t0 + jnp.arange(Q_BLOCK)
        s_idx = jnp.einsum('bthd,bsd->bths', qib, ki, preferred_element_type=F32) * IDX_DIM ** -0.5
        score = jnp.einsum('bth,bths->bts', wib, jax.nn.relu(s_idx))
        causal = kpos[None, :] <= tpos[:, None]
        score = jnp.where(causal[None], score, -jnp.inf)
        _, sel = lax.top_k(score, n_sel)
        valid = sel <= tpos[None, :, None]
        kg = jax.vmap(lambda kk, ii: kk[ii])(k, sel)
        vg = jax.vmap(lambda vv, ii: vv[ii])(v, sel)
        qg = qb.reshape(bsz, Q_BLOCK, A_KV_HEADS, groups, HEAD_DIM)
        logits = jnp.einsum('btkgd,btskd->btkgs', qg, kg, preferred_element_type=F32) * HEAD_DIM ** -0.5
        logits = jnp.where(valid[:, :, None, None, :], logits, -jnp.inf)
        probs = jax.nn.softmax(logits, axis=-1).astype(v.dtype)
        o = jnp.einsum('btkgs,btskd->btkgd', probs, vg)
        return o.reshape(bsz, Q_BLOCK, A_HEADS * HEAD_DIM)

    out = lax.map(block, jnp.arange(n_blk))
    return jnp.moveaxis(out, 0, 1).reshape(bsz, seq, A_HEADS * HEAD_DIM)

def rglru_mixer(xg, xr, conv_w, conv_b, wa, ba, wx, bx, lam):
    bsz, seq, width = xr.shape
    xc = causal_dwconv(xr, conv_w, conv_b)
    xb = xc.reshape(bsz, seq, LRU_BLOCKS, width // LRU_BLOCKS)
    gate_r = jax.nn.sigmoid(jnp.einsum('bsnc,ncd->bsnd', xb, wa, preferred_element_type=F32).reshape(bsz, seq, width) + ba.astype(F32))
    gate_i = jax.nn.sigmoid(jnp.einsum('bsnc,ncd->bsnd', xb, wx, preferred_element_type=F32).reshape(bsz, seq, width) + bx.astype(F32))
    log_a = -LRU_C * gate_r * jax.nn.softplus(-lam.astype(F32))
    a = jnp.exp(log_a)
    b_in = jnp.sqrt(-jnp.expm1(2.0 * log_a)) * (gate_i * xc.astype(F32))

    def combine(lhs, rhs):
        a1, b1 = lhs
        a2, b2 = rhs
        return a1 * a2, a2 * b1 + b2

    _, hseq = lax.associative_scan(combine, (a, b_in), axis=1)
    y = hseq * jax.nn.gelu(xg.astype(F32), approximate=True)
    return y.astype(xr.dtype)

def ssd_chunked(x, dt, a_neg, bm, cm):
    bsz, seq, nh, hp = x.shape
    ng, ns = bm.shape[2], bm.shape[3]
    hg = nh // ng
    nc, cl = seq // SSD_CHUNK, SSD_CHUNK

    def chunks(t):
        return jnp.moveaxis(t.reshape((bsz, nc, cl) + t.shape[2:]), 1, 0)

    xdt = (x.astype(F32) * dt[..., None]).reshape(bsz, seq, ng, hg, hp)
    da = (dt * a_neg).reshape(bsz, seq, ng, hg)
    xs = (chunks(xdt), chunks(da), chunks(bm.astype(F32)), chunks(cm.astype(F32)))
    causal = jnp.tril(jnp.ones((cl, cl), dtype=bool))

    def step(state, inp):
        xc, ac, bc, cc = inp
        cum = jnp.cumsum(ac, axis=1)
        seg = cum[:, :, None] - cum[:, None, :]
        decay = jnp.exp(jnp.where(causal[None, :, :, None, None], seg, -jnp.inf))
        cb = jnp.einsum('btgn,bsgn->btsg', cc, bc)
        y_diag = jnp.einsum('btsg,btsgh,bsghp->btghp', cb, decay, xc)
        y_off = jnp.einsum('btgn,bghpn,btgh->btghp', cc, state, jnp.exp(cum))
        tail = jnp.exp(cum[:, -1:] - cum)
        new_state = state * jnp.exp(cum[:, -1])[..., None, None] + jnp.einsum('bsgn,bsgh,bsghp->bghpn', bc, tail, xc)
        return new_state, y_diag + y_off

    state0 = jnp.zeros((bsz, ng, hg, hp, ns), F32)
    _, ys = lax.scan(step, state0, xs)
    return jnp.moveaxis(ys, 0, 1).reshape(bsz, seq, nh, hp)

def ssd_mixer(hn, w_in, conv_w, conv_b, dt_bias, a_log, d_skip, gnorm, w_out):
    bsz, seq, _ = hn.shape
    z, xbc, dt = _split(hn @ w_in, (SSD_INNER, SSD_CONV_CH, SSD_HEADS))
    xbc = jax.nn.silu(causal_dwconv(xbc, conv_w, conv_b))
    xs, bm, cm = _split(xbc, (SSD_INNER, SSD_GROUPS * SSD_STATE, SSD_GROUPS * SSD_STATE))
    dt = jax.nn.softplus(dt.astype(F32) + dt_bias.astype(F32))
    a_neg = -jnp.exp(a_log.astype(F32))
    xh = xs.reshape(bsz, seq, SSD_HEADS, SSD_HEAD_DIM)
    y = ssd_chunked(xh, dt, a_neg,
                    bm.reshape(bsz, seq, SSD_GROUPS, SSD_STATE),
                    cm.reshape(bsz, seq, SSD_GROUPS, SSD_STATE))
    y = y + d_skip.astype(F32)[:, None] * xh.astype(F32)
    y = y.reshape(bsz, seq, SSD_INNER) * jax.nn.silu(z.astype(F32))
    yg = y.reshape(bsz, seq, SSD_GROUPS, SSD_INNER // SSD_GROUPS)
    yg = yg * lax.rsqrt(jnp.mean(yg * yg, axis=-1, keepdims=True) + NORM_EPS)
    y = (yg.reshape(bsz, seq, SSD_INNER) * gnorm.astype(F32)).astype(hn.dtype)
    return y @ w_out

def moe_swiglu(hn, router, wg, wu, wd):
    logits = jnp.einsum('bsd,de->bse', hn, router, preferred_element_type=F32)
    top_val, top_idx = lax.top_k(logits, TOP_K)
    top_w = jax.nn.softmax(top_val, axis=-1)
    gates = jnp.sum(jax.nn.one_hot(top_idx, N_EXPERTS, dtype=F32) * top_w[..., None], axis=-2)
    out = jnp.zeros(hn.shape, F32)
    for e in range(N_EXPERTS):
        out = out + gates[..., e:e + 1] * swiglu(hn, wg[e], wu[e], wd[e]).astype(F32)
    return out.astype(hn.dtype)

def ple_add(h, p_i, proj, gate_norm, gate_w):
    emb = (p_i @ proj).astype(F32)
    g = jax.nn.sigmoid((rmsnorm(h, gate_norm) @ gate_w).astype(F32))
    return h + (g * emb).astype(h.dtype)

def even_layer(h, p_i, mix_norm, w_in, lru_conv_w, lru_conv_b, lru_wa, lru_ba, lru_wx, lru_bx, lru_lambda,
               w_out, ffn_norm, ffn_wg, ffn_wu, ffn_wd, ple_proj, ple_gate_norm, ple_gate):
    bsz, seq, _ = h.shape
    pos = jnp.arange(seq)
    u = rmsnorm(h, mix_norm) @ w_in
    q, k, v, qi, ki, wi, xg, xr = _split(u, (A_HEADS * HEAD_DIM, A_KV_HEADS * HEAD_DIM, A_KV_HEADS * HEAD_DIM,
                                             IDX_HEADS * IDX_DIM, IDX_DIM, IDX_HEADS, LRU_WIDTH, LRU_WIDTH))
    q = partial_rope(q.reshape(bsz, seq, A_HEADS, HEAD_DIM), pos)
    k = partial_rope(k.reshape(bsz, seq, A_KV_HEADS, HEAD_DIM), pos)
    v = v.reshape(bsz, seq, A_KV_HEADS, HEAD_DIM)
    qi = partial_rope(qi.reshape(bsz, seq, IDX_HEADS, IDX_DIM), pos)
    ki = partial_rope(ki[:, :, None, :], pos)[:, :, 0, :]
    o_a = dsa_mixer(q, k, v, qi, ki, wi)
    o_b = rglru_mixer(xg, xr, lru_conv_w, lru_conv_b, lru_wa, lru_ba, lru_wx, lru_bx, lru_lambda)
    h = h + jnp.concatenate([o_a, o_b], axis=-1) @ w_out
    h = h + swiglu(rmsnorm(h, ffn_norm), ffn_wg, ffn_wu, ffn_wd)
    return ple_add(h, p_i, ple_proj, ple_gate_norm, ple_gate)

def odd_layer(h, p_i, mix_norm, w_in, conv_w, conv_b, dt_bias, a_log, d_skip, gnorm, w_out,
              moe_norm, router, exp_wg, exp_wu, exp_wd, ple_proj, ple_gate_norm, ple_gate):
    h = h + ssd_mixer(rmsnorm(h, mix_norm), w_in, conv_w, conv_b, dt_bias, a_log, d_skip, gnorm, w_out)
    h = h + moe_swiglu(rmsnorm(h, moe_norm), router, exp_wg, exp_wu, exp_wd)
    return ple_add(h, p_i, ple_proj, ple_gate_norm, ple_gate)

def setup_inputs(seed: int = 0) -> dict:
    key = jax.random.key(seed)
    keys = iter(jax.random.split(key, 64))

    def nk():
        return next(keys)

    def dense(shape, fan_in):
        return jax.random.normal(nk(), shape, F32) * fan_in ** -0.5

    def gain(n):
        return 1.0 + 0.05 * jax.random.normal(nk(), (n,), F32)

    def bias(n):
        return 0.02 * jax.random.normal(nk(), (n,), F32)

    x = jax.random.normal(nk(), (BATCH, SEQ, D_MODEL), F32)
    p = jax.random.normal(nk(), (DEPTH, BATCH, SEQ, PLE_DIM), F32)
    blk = LRU_WIDTH // LRU_BLOCKS
    u = jax.random.uniform(nk(), (LRU_WIDTH,), F32, minval=0.9, maxval=0.999)
    s = u ** (1.0 / LRU_C)
    lru_lambda = jnp.log(s) - jnp.log1p(-s)
    dt0 = jnp.exp(jax.random.uniform(nk(), (SSD_HEADS,), F32, minval=np.log(1e-3), maxval=np.log(1e-1)))
    dt_bias = dt0 + jnp.log(-jnp.expm1(-dt0))
    a_log = jnp.log(jax.random.uniform(nk(), (SSD_HEADS,), F32, minval=1.0, maxval=16.0))
    return {
        'x': x,
        'p': p,
        'e_mix_norm': gain(D_MODEL),
        'e_w_in': dense((D_MODEL, EVEN_IN), D_MODEL),
        'e_lru_conv_w': dense((CONV_W, LRU_WIDTH), CONV_W),
        'e_lru_conv_b': bias(LRU_WIDTH),
        'e_lru_wa': dense((LRU_BLOCKS, blk, blk), blk),
        'e_lru_ba': bias(LRU_WIDTH),
        'e_lru_wx': dense((LRU_BLOCKS, blk, blk), blk),
        'e_lru_bx': bias(LRU_WIDTH),
        'e_lru_lambda': lru_lambda,
        'e_w_out': dense((EVEN_MIX, D_MODEL), EVEN_MIX),
        'e_ffn_norm': gain(D_MODEL),
        'e_ffn_wg': dense((D_MODEL, D_FF), D_MODEL),
        'e_ffn_wu': dense((D_MODEL, D_FF), D_MODEL),
        'e_ffn_wd': dense((D_FF, D_MODEL), D_FF),
        'e_ple_proj': dense((PLE_DIM, D_MODEL), PLE_DIM),
        'e_ple_gate_norm': gain(D_MODEL),
        'e_ple_gate': dense((D_MODEL, D_MODEL), D_MODEL),
        'o_mix_norm': gain(D_MODEL),
        'o_w_in': dense((D_MODEL, ODD_IN), D_MODEL),
        'o_conv_w': dense((CONV_W, SSD_CONV_CH), CONV_W),
        'o_conv_b': bias(SSD_CONV_CH),
        'o_dt_bias': dt_bias,
        'o_a_log': a_log,
        'o_d_skip': gain(SSD_HEADS),
        'o_gnorm': gain(SSD_INNER),
        'o_w_out': dense((SSD_INNER, D_MODEL), SSD_INNER),
        'o_moe_norm': gain(D_MODEL),
        'o_router': dense((D_MODEL, N_EXPERTS), D_MODEL),
        'o_exp_wg': dense((N_EXPERTS, D_MODEL, D_FF), D_MODEL),
        'o_exp_wu': dense((N_EXPERTS, D_MODEL, D_FF), D_MODEL),
        'o_exp_wd': dense((N_EXPERTS, D_FF, D_MODEL), D_FF),
        'o_ple_proj': dense((PLE_DIM, D_MODEL), PLE_DIM),
        'o_ple_gate_norm': gain(D_MODEL),
        'o_ple_gate': dense((D_MODEL, D_MODEL), D_MODEL),
        'final_norm': gain(D_MODEL),
    }

def reference(x, p, e_mix_norm, e_w_in, e_lru_conv_w, e_lru_conv_b, e_lru_wa, e_lru_ba, e_lru_wx, e_lru_bx,
              e_lru_lambda, e_w_out, e_ffn_norm, e_ffn_wg, e_ffn_wu, e_ffn_wd, e_ple_proj, e_ple_gate_norm,
              e_ple_gate, o_mix_norm, o_w_in, o_conv_w, o_conv_b, o_dt_bias, o_a_log, o_d_skip, o_gnorm, o_w_out,
              o_moe_norm, o_router, o_exp_wg, o_exp_wu, o_exp_wd, o_ple_proj, o_ple_gate_norm, o_ple_gate,
              final_norm):
    h = x
    for i in range(DEPTH):
        if i % 2 == 0:
            h = even_layer(h, p[i], e_mix_norm, e_w_in, e_lru_conv_w, e_lru_conv_b, e_lru_wa, e_lru_ba, e_lru_wx,
                           e_lru_bx, e_lru_lambda, e_w_out, e_ffn_norm, e_ffn_wg, e_ffn_wu, e_ffn_wd,
                           e_ple_proj, e_ple_gate_norm, e_ple_gate)
        else:
            h = odd_layer(h, p[i], o_mix_norm, o_w_in, o_conv_w, o_conv_b, o_dt_bias, o_a_log, o_d_skip, o_gnorm,
                          o_w_out, o_moe_norm, o_router, o_exp_wg, o_exp_wu, o_exp_wd,
                          o_ple_proj, o_ple_gate_norm, o_ple_gate)
    return rmsnorm(h, final_norm)


_drawn_inputs = setup_inputs


def setup_inputs(seed=0):
    import zlib

    import numpy as np

    out = dict(_drawn_inputs(seed))
    spreads = {}
    factors = {'e_lru_ba': 30.671,
     'e_lru_bx': 5.669,
     'e_ple_gate_norm': 3.207,
     'o_d_skip': 3.137,
     'o_ple_gate_norm': 23.942}
    for name, (base, spread) in spreads.items():
        noise = np.random.default_rng([zlib.crc32(name.encode()), seed]).standard_normal(out[name].shape)
        drawn = base * np.exp(spread * noise) if base else spread * noise
        out[name] = jnp.asarray(drawn.astype(out[name].dtype))
    for name, factor in factors.items():
        out[name] = (out[name] * factor).astype(out[name].dtype)
    return out
```

```python
from contextlib import ExitStack

import numpy as np

import concourse.bass as bass
from concourse import mybir

F32 = mybir.dt.float32
F32R = mybir.dt.float32r
I32 = mybir.dt.int32
U32 = mybir.dt.uint32
ALU = mybir.AluOpType
ACT = mybir.ActivationFunctionType
AX = mybir.AxisListType.X

P = 128
SEQ, DM, DFF = 256, 1024, 3584
NT = SEQ // P
HD, HEADS, KVH, IDXH = 64, 8, 2, 4
ROT = HD // 4 // 2
LRU = 512
LRU_K = LRU // P
PLE = 256
NSEL = 64
U_Q, U_K, U_V, U_QI, U_KI, U_WI, U_XG, U_XR, U_END = np.cumsum(
    [0, HEADS * HD, KVH * HD, KVH * HD, IDXH * HD, HD, IDXH, LRU, LRU]).tolist()
INNER, SH, GROUPS, STATE = 2048, 32, 4, 128
HPG = SH // GROUPS
Z0, X0, B0, C0, DT0, ODD_END = np.cumsum([0, INNER, INNER, GROUPS * STATE, GROUPS * STATE, SH]).tolist()
NE = 8
EPS = 1e-6
NEG = -1e30
REPLACED = -3e38

KS, WC = 4, 512
RAW, SPL = 6, 2
LAG = SPL - 1
FCH = DFF // WC
NEXP = 2 * 2 * FCH + 2 * FCH


class Chunk:

    def __init__(self, name, number, first, ksubs, width, evac, xbase=0):
        self.name, self.number, self.first, self.ksubs, self.width = name, number, first, ksubs, width
        self.evac, self.xbase = evac, xbase
        self.banks = 2 * (number % 2)
        self.panels = -(-ksubs // KS)
        self.last = first + self.panels - 1


def plan():
    panels, chunks = [], {}

    def chunk(name, weight, ksubs, col, width, evac):
        chunks[name] = Chunk(name, len(chunks), len(panels), ksubs, width, evac)
        for k in range(0, ksubs, KS):
            panels.append((weight, k, min(KS, ksubs - k), col, width))

    for name, a, b in (("kv_qi", U_K, U_KI), ("ki_wi", U_KI, U_XG), ("q", U_Q, U_K), ("xr", U_XR, U_END), ("xg", U_XG, U_XR)):
        chunk(name, "e_w_in", DM // P, a, b - a, "act")
    for h in range(2):
        chunk(f"e_out{h}", "e_w_out", DM // P, h * WC, WC, "dve")
    starts = {"ffn": len(panels)}
    panels.extend(ffn_panels("e_ffn_wg", "e_ffn_wu", "e_ffn_wd"))
    for h in range(2):
        chunk(f"e_emb{h}", "e_ple_proj", PLE // P, h * WC, WC, "act")
    for h in range(2):
        chunk(f"e_gate{h}", "e_ple_gate", DM // P, h * WC, WC, "act")
    chunk("dt", "o_w_in", DM // P, DT0, SH, "act")
    chunk("B", "o_w_in", DM // P, B0, WC, "act")
    chunk("C", "o_w_in", DM // P, C0, WC, "act")
    for j in range(INNER // WC):
        chunk(f"x{j}", "o_w_in", DM // P, X0 + j * WC, WC, "act")
    for j in range(INNER // WC):
        chunk(f"z{j}", "o_w_in", DM // P, Z0 + j * WC, WC, "act")
    for h in range(2):
        chunk(f"o_out{h}", "o_w_out", INNER // P, h * WC, WC, "dve")
    starts["experts"] = len(panels)
    panels.extend([None] * (NE * NEXP))
    for h in range(2):
        chunk(f"o_emb{h}", "o_ple_proj", PLE // P, h * WC, WC, "act")
    for h in range(2):
        chunk(f"o_gate{h}", "o_ple_gate", DM // P, h * WC, WC, "act")
    return panels, chunks, starts


def ffn_order():
    steps = []
    for j in range(FCH):
        steps += [("g", j, 0), ("g", j, 1), ("u", j, 0), ("u", j, 1)]
        if j >= 2:
            steps += [("d", j - 2, 0), ("d", j - 2, 1)]
    for j in (FCH - 2, FCH - 1):
        steps += [("d", j, 0), ("d", j, 1)]
    return steps


def ffn_panels(wg, wu, wd):
    out = []
    for kind, j, half in ffn_order():
        if kind == "d":
            out.append((wd, KS * j, KS, half * WC, WC))
        else:
            out.append((wg if kind == "g" else wu, KS * half, KS, j * WC, WC))
    return out


FFN_AT = {step: n for n, step in enumerate(ffn_order())}

GROUP = {"ple": 0, "e_mix": 2, "o_attn": 6, "e_ffn": 8, "e_ple": 12, "o_mix": 16, "ssd": 20, "o_moe": 28, "o_ple": 32}

CONST = {}
SMALL = {}


def lay(table, *items):
    at = 0
    for name, n in items:
        table[name] = (at, at + n)
        at += n
    return at


CONST_N = lay(CONST, ("ident", P), ("cmask", P), ("tri", P), ("ones", P), ("iota", P), ("cos", NT * ROT),
              ("sin", NT * ROT), ("eps", 1))
SMALL_N = lay(SMALL, ("lru_w", LRU_K * 4), ("lru_b", LRU_K), ("lru_ba", LRU_K), ("lru_bx", LRU_K), ("lam", LRU_K),
              ("lru_wa", LRU_K * HD), ("lru_wx", LRU_K * HD), ("conv_w", 24 * 4), ("conv_b", 24), ("dt_bias", SH),
              ("a_log", SH), ("d_skip", SH), ("router", DM // P * NE))



class Place:

    def __init__(self, nc, at):
        self.nc, self.at = nc, at

    def __call__(self, name, shape, dt=F32):
        t = self.nc.alloc_sbuf_tensor_at(name, shape, dt, offset=self.at)
        self.at += -(-int(np.prod(shape[1:])) * 4 // 32) * 32
        return t


class FfnSems:

    def __init__(self, sem, name, raw_in, hi_done, lo_done, panel_used):
        self.raw_in, self.hi_done, self.lo_done, self.panel_used = raw_in, hi_done, lo_done, panel_used
        self.silu = sem(name + "_silu")
        self.prod = sem(name + "_prod")
        self.aT_ps = sem(name + "_aT_ps")
        self.aT_hi = sem(name + "_aT_hi")
        self.aT_lo = sem(name + "_aT_lo")
        self.sel = sem(name + "_sel")
        self.xe_ps = sem(name + "_xe_ps")
        self.xe_hi = sem(name + "_xe_hi")
        self.xe_lo = sem(name + "_xe_lo")
        self.y_hi = sem(name + "_y_hi")
        self.y_lo = sem(name + "_y_lo")
        self.back_ps = sem(name + "_back_ps")
        self.summed = sem(name + "_summed")


def build(nc, w, x, p, const, small, out):
    panels, chunks, starts = plan()
    ordered = sorted(chunks.values(), key=lambda c: c.number)

    place = Place(nc, 16512)
    cst = place("cst", [P, CONST_N])
    sml = place("sml", [P, SMALL_N])
    raw = place("raw", [P, RAW, KS, WC])
    whi = place("whi", [P, SPL, KS, WC], F32R)
    wlo = place("wlo", [P, SPL, KS, WC], F32R)
    h = place("h", [P, NT, DM])
    hn = place("hn", [P, NT, DM])
    xT_hi = place("xT_hi", [P, DM // P, SEQ], F32R)
    xT_lo = place("xT_lo", [P, DM // P, SEQ], F32R)
    gain = place("gain", [P, DM])
    pT_hi = place("pT_hi", [P, 2, PLE // P, SEQ], F32R)
    pT_lo = place("pT_lo", [P, 2, PLE // P, SEQ], F32R)
    ident_r = place("ident_r", [P, P], F32R)
    stat = place("stat", [P, 4, NT])
    flag = place("flag", [P, 8], I32)
    phase = place.at

    place = Place(nc, phase)
    u = place("u", [P, NT, U_END])
    gr = Place(nc, place.at)("gr", [P, LRU_K, SEQ])
    kdup = place("kdup", [P, NT, KVH + 1, 2, 2, HD])
    kqT = place("kqT", [P, 8, SEQ])
    qT = place("qT", [P, 4, SEQ])
    prT_at = place.at
    relu = place("relu", [P, IDXH, SEQ])
    prT = Place(nc, prT_at)("prT", [P, 8, P])
    wi2 = place("wi2", [P, NT, IDXH])
    score = place("score", [P, NT, SEQ])
    work = place("work", [P, SEQ])
    top8 = place("top8", [P, 8])
    keep = place("keep", [P, NT, SEQ])
    early = Place(nc, place.at)
    probs = place("probs", [P, 2, 4, SEQ])
    pin = early("pin", [P, 2 * NT, PLE])
    rot = early("rot", [P, 4, NT, 10, ROT])
    assert early.at <= place.at
    nmax = place("nmax", [P, 4, 4])
    rsum = place("rsum", [P, 4, 4])
    rinv = place("rinv", [P, 4, 4])
    xrT = place("xrT", [P, LRU_K, SEQ + 3])
    xgT = place("xgT", [P, LRU_K, SEQ])
    xc = place("xc", [P, LRU_K, SEQ])
    gi = place("gi", [P, LRU_K, SEQ])
    la = place("la", [P, LRU_K, SEQ])
    bd = place("bd", [P, 2, LRU_K, P])
    c8 = place("c8", [P, 8, LRU_K])
    assert place.at <= 229344, place.at

    place = Place(nc, phase)
    aT_hi = place("aT_hi", [P, 2, KS, SEQ], F32R)
    aT_lo = place("aT_lo", [P, 2, KS, SEQ], F32R)
    sg = place("sg", [P, 2, NT, WC])
    act = place("act", [P, 2, NT, WC])
    emb = place("emb", [P, NT, DM])
    y_hi = place("y_hi", [P, DM], F32R)
    y_lo = place("y_lo", [P, DM], F32R)
    hn_hi = place("hn_hi", [P, NT, DM], F32R)
    hn_lo = place("hn_lo", [P, NT, DM], F32R)
    rt_hi = place("rt_hi", [P, DM // P, NE], F32R)
    rt_lo = place("rt_lo", [P, DM // P, NE], F32R)
    sel = place("sel", [P, NT, P], F32R)
    selT = place("selT", [P, NT * P], F32R)
    lg = place("lg", [P, NT, NE])
    lmax = place("lmax", [P, NT, 8])
    lidx = place("lidx", [P, NT, 8], U32)
    lidf = place("lidf", [P, NT, 8])
    oh = place("oh", [P, 2, NT, NE])
    gw = place("gw", [P, 4, NT])
    gates = place("gates", [P, NT, NE])
    routed = place("routed", [P, NT, NE])
    slot = place("slot", [P, 2, NT, NE])
    most = place("most", [P, 8])
    assert place.at <= 229344, place.at

    place = Place(nc, phase)
    xt = place("xt", [P, NT, INNER])
    yT = Place(nc, place.at)
    zt = place("zt", [P, NT, INNER])
    yT_hi = yT("yT_hi", [P, DM // P, SEQ], F32R)
    yT_lo = yT("yT_lo", [P, DM // P, SEQ], F32R)
    BT = place("BT", [P, GROUPS, SEQ])
    CT = place("CT", [P, GROUPS, SEQ])
    Btok = place("Btok", [P, GROUPS, STATE])
    late = Place(nc, place.at)
    pre = place("pre", [P, 2, KS, SEQ + 3])
    gn = late("gn", [P, INNER])
    late = Place(nc, place.at)
    cv = place("cv", [P, 2, KS, SEQ])
    segs = late("segs", [P, 2, HPG, P])
    cbm = place("cbm", [P, 2, P])
    xdt = place("xdt", [P, 2, WC])
    xtl = place("xtl", [P, WC])
    st = place("st", [P, WC])
    yt = place("yt", [P, WC])
    dts = place("dts", [P, 6, NT, SH])
    cum = place("cum", [P, 3, SH])
    dec = place("dec", [P, 2, SH])
    gss = place("gss", [P, 3, NT, GROUPS])
    assert place.at <= 229344, place.at

    def con(name):
        return cst[:, CONST[name][0]:CONST[name][1]]

    def par(name, **dims):
        v = sml[:, SMALL[name][0]:SMALL[name][1]]
        return v.rearrange("p (a b) -> p a b", **dims) if dims else v

    ident, cmask, tri, ones, iota, eps = (con(n) for n in ("ident", "cmask", "tri", "ones", "iota", "eps"))
    cos = con("cos").rearrange("p (t r) -> p t r", t=NT)
    sin = con("sin").rearrange("p (t r) -> p t r", t=NT)

    def tok(t):
        return slice(t * P, (t + 1) * P)

    ctx = ExitStack()
    with ctx:
        ps = ctx.enter_context(nc.psum_tensor("ps", [P, 8, 512], F32))

        def sem(name):
            return ctx.enter_context(nc.semaphore(name))

        const_in, small_in, x_in, p_in = sem("const_in"), sem("small_in"), sem("x_in"), sem("p_in")
        gain_in, gn_in, out_done = sem("gain_in"), sem("gn_in"), sem("out_done")
        raw_in = [sem(f"raw_in{i}") for i in range(RAW)]
        hi_done = sem("hi_done")
        lo_done = sem("lo_done")
        panel_used = sem("panel_used")
        chunk_act, chunk_dve = sem("chunk_act"), sem("chunk_dve")
        act_seq, dve_seq = sem("act_seq"), sem("dve_seq")
        setup = sem("setup")
        rms = sem("rms")
        hn_ready = sem("hn_ready")
        tp_ps, tp_hi, tp_lo = sem("tp_ps"), sem("tp_hi"), sem("tp_lo")
        roped = sem("roped")
        at_ps, at_sb = sem("at_ps"), sem("at_sb")
        lt_ps, lt_sb = sem("lt_ps"), sem("lt_sb")
        ix_ps, ix_relu = sem("ix_ps"), sem("ix_relu")
        conv_done = sem("conv_done")
        gate_ps, gate_sb = sem("gate_ps"), sem("gate_sb")
        lru_a, lru_b1, lru_bs, lru_gelu = sem("lru_a"), sem("lru_b1"), sem("lru_bs"), sem("lru_gelu")
        lru_y, lru_hi, lru_lo = sem("lru_y"), sem("lru_hi"), sem("lru_lo")
        lg_ps, lg_sb, pr_sb = sem("lg_ps"), sem("lg_sb"), sem("pr_sb")
        pt_ps, pt_sb = sem("pt_ps"), sem("pt_sb")
        o_ps, o_sb = sem("o_ps"), sem("o_sb")
        fw_ps, fw_sb = sem("fw_ps"), sem("fw_sb")
        cv_raw, cv_done = sem("cv_raw"), sem("cv_done")
        bk_ps, bk_sb = sem("bk_ps"), sem("bk_sb")
        dt_abs, dt_exp, dt_ln, dt_da = sem("dt_abs"), sem("dt_exp"), sem("dt_ln"), sem("dt_da")
        cum_ps, cum_sb, cum_exp = sem("cum_ps"), sem("cum_sb"), sem("cum_exp")
        sg_ps, sg_sb, sg_exp = sem("sg_ps"), sem("sg_sb"), sem("sg_exp")
        m_done, y_ps, y_sb, st_sb = sem("m_done"), sem("y_ps"), sem("y_sb"), sem("st_sb")
        gss_done, grms = sem("gss_done"), sem("grms")
        yn_ready = sem("yn_ready")
        rt_done, rt_ps, lw_max, lw_exp = sem("rt_done"), sem("rt_ps"), sem("lw_max"), sem("lw_exp")
        routed_sb, slot_ps, flag_set, hn_split = sem("routed_sb"), sem("slot_ps"), sem("flag_set"), sem("hn_split")
        gate_ple = sem("gate_ple")
        ffn_sum = sem("ffn_sum")
        fin = sem("fin")
        dense = FfnSems(sem, "ffn", raw_in, hi_done, lo_done, panel_used)
        main = FfnSems(sem, "exp", raw_in, hi_done, lo_done, panel_used)
        rest = FfnSems(sem, "rest", [sem(f"rest_in{i}") for i in range(RAW)], sem("rest_hi"), sem("rest_lo"),
                       sem("rest_used"))

        def evacuated(number):
            c = ordered[number]
            return (chunk_act if c.evac == "act" else chunk_dve,
                    sum(o.evac == c.evac for o in ordered[:number + 1]))

        def panel_dram(name, k, n, col, width, e=None):
            src = w[name]
            if e is not None:
                src = src[bass.ds(e, 1) if not isinstance(e, int) else slice(e, e + 1), k * P:(k + n) * P, col:col + width].rearrange("a k c -> (a k) c")
            else:
                src = src[k * P:(k + n) * P, col:col + width]
            return src.rearrange("(k p) c -> p k c", p=P)

        block = ctx.enter_context(nc.Block())

        @block.sync
        def _(sp):
            def load(i, panel):
                if i >= RAW:
                    sp.wait_ge(hi_done, i - RAW + 1)
                    sp.wait_ge(lo_done, i - RAW + 1)
                name, k, n, col, width = panel
                sp.dma_start(raw[:, i % RAW, 0:n, 0:width], panel_dram(*panel)).then_inc(raw_in[i % RAW], 16)

            sp.dma_start(h[:, :, :], x.rearrange("(t p) d -> p t d", p=P)).then_inc(x_in, 16)
            for i in range(starts["experts"]):
                load(i, panels[i])

            order = ffn_panels("o_exp_wg", "o_exp_wu", "o_exp_wd")
            base = starts["experts"]
            with sp.Fori(0, NE) as e:
                for n, panel in enumerate(order):
                    i = base + n
                    sp.wait_ge(hi_done, e * NEXP + (i - RAW + 1))
                    sp.wait_ge(lo_done, e * NEXP + (i - RAW + 1))
                    sp.dma_start(raw[:, i % RAW, :, :], panel_dram(*panel, e=e)).then_inc(raw_in[i % RAW], 16)
            sp.wait_ge(flag_set, 1)
            some = sp.value_load(flag[0:1, 0:1], min_val=0, max_val=1)
            with sp.If(some != 0):
                sp.wait_ge(hi_done, base + NE * NEXP)
                sp.wait_ge(lo_done, base + NE * NEXP)
                for n in range(NEXP):
                    if n >= RAW:
                        sp.wait_ge(rest.hi_done, n - RAW + 1)
                        sp.wait_ge(rest.lo_done, n - RAW + 1)
                    sp.dma_start(raw[:, n % RAW, :, :], panel_dram(*order[n], e=0)).then_inc(rest.raw_in[n % RAW], 16)
                with sp.Fori(1, NE) as e:
                    for n in range(NEXP):
                        sp.wait_ge(rest.hi_done, e * NEXP + (n - RAW + 1))
                        sp.wait_ge(rest.lo_done, e * NEXP + (n - RAW + 1))
                        sp.dma_start(raw[:, n % RAW, :, :], panel_dram(*order[n], e=e)).then_inc(
                            rest.raw_in[n % RAW], 16)
                sp.wait_ge(rest.hi_done, NE * NEXP)
                sp.wait_ge(rest.lo_done, NE * NEXP)
            for i in range(base + NE * NEXP, len(panels)):
                load(i, panels[i])
            sp.wait_ge(fin, 1)
            sp.dma_start(out.rearrange("(t p) d -> p t d", p=P), hn[:, :, :]).then_inc(out_done, 16)
            sp.wait_ge(out_done, 16)

        @block.gpsimd
        def _(pool):
            pool.dma_start(cst[:, :], const).then_inc(const_in, 16)
            pool.dma_start(pin[:, :, :], p.rearrange("l (t p) d -> p (l t) d", p=P)).then_inc(p_in, 16)
            pool.dma_start(sml[:, :], small).then_inc(small_in, 16)
            for n, name in enumerate(("e_mix_norm", "e_ffn_norm", "e_ple_gate_norm", "o_mix_norm", "o_moe_norm",
                                      "o_ple_gate_norm", "final_norm")):
                if n:
                    pool.wait_ge(hn_ready, n)
                pool.dma_start(gain[:, :], w[name].partition_broadcast(P)).then_inc(gain_in, 16)
                if name == "o_mix_norm":
                    pool.wait_ge(cv_raw, 6)
                    pool.dma_start(gn[:, :], w["o_gnorm"].partition_broadcast(P)).then_inc(gn_in, 16)

        @block.scalar
        def _(a):
            sent = [0]
            steps = [0]

            def step(ins):
                steps[0] += 1
                ins.then_inc(act_seq, 1)
                a.wait_ge(act_seq, steps[0])

            def split_hi(i, s=None, e=None, first=0):
                shift = e * NEXP if e is not None else 0
                turn = e * (NEXP // RAW) if e is not None else 0
                s = s or dense
                a.wait_ge(s.raw_in[i % RAW], (turn + (i // RAW + 1)) * 16)
                if i >= SPL or s is not rest:
                    if i >= SPL:
                        a.wait_ge(s.panel_used, shift + (i - SPL + 1))
                n, width = (panels[i][2], panels[i][4]) if e is None else (KS, WC)
                a.activation(whi[:, i % SPL, 0:n, 0:width], raw[:, i % RAW, 0:n, 0:width], ACT.Copy).then_inc(
                    s.hi_done, 1)

            def splits(upto):
                while sent[0] <= min(upto, len(panels) - 1) and panels[sent[0]] is not None:
                    split_hi(sent[0])
                    sent[0] += 1

            def taken(name):
                c = chunks[name]
                splits(c.last + LAG)
                a.wait_ge(panel_used, c.last + 1)
                return ps[:, c.banks:c.banks + 2, 0:c.width]

            def norm(n, used):
                if used:
                    a.wait_ge(tp_ps, used)
                summed = {1: (chunk_dve, 2), 2: (dense.summed, 1), 3: (gate_ple, 1), 4: (chunk_dve, 4),
                          5: (gate_ple, 2), 6: (gate_ple, 3)}
                if n:
                    a.wait_ge(*summed[n])
                for t in range(NT):
                    step(a.activation(hn[:, t, :], h[:, t, :], ACT.Square, accum_out=stat[:, 0, t:t + 1]))
                a.activation(stat[:, 1, :], stat[:, 0, :], ACT.Sqrt, scale=1.0 / DM, bias=eps).then_inc(rms, 1)

            def turn_hi(first, count=4, to=None, free=None):
                if free:
                    a.wait_ge(panel_used, free)
                for n in range(count):
                    g = first + n
                    a.wait_ge(tp_ps, g + 1)
                    dst = to(n) if to else xT_hi[:, 4 * (n % 2):4 * (n % 2) + 4, tok(n // 2)]
                    a.activation(dst, ps[:, 4 + g % 4, :].rearrange("p (k c) -> p k c", k=4), ACT.Copy).then_inc(
                        tp_hi, 1)

            splits(0)
            a.wait_ge(const_in, 16)
            for i in range(2):
                a.wait_ge(tp_ps, i + 1)
                a.activation(pT_hi[:, i].rearrange("p k (t c) -> p t k c", t=NT),
                             ps[:, 4 + i, :].rearrange("p (t k c) -> p t k c", t=NT, k=PLE // P), ACT.Copy).then_inc(tp_hi, 1)
            a.wait_ge(x_in, 16)
            norm(0, 0)
            turn_hi(GROUP["e_mix"])
            for name in ("kv_qi", "ki_wi", "q", "xr", "xg"):
                b = {"kv_qi": U_K, "ki_wi": U_KI, "q": U_Q, "xr": U_XR, "xg": U_XG}[name]
                src = taken(name)
                a.activation(u[:, :, b:b + chunks[name].width], src, ACT.Copy).then_inc(chunk_act, 1)
            splits(chunks["xg"].last + LAG)
            a.wait_ge(setup, 2)
            a.activation(c8[:, 1, :], c8[:, 0, :], ACT.Exp, scale=-1.0).then_inc(setup, 1)
            a.wait_ge(setup, 4)
            a.activation(c8[:, 3, :], c8[:, 2, :], ACT.Ln).then_inc(setup, 1)
            for n, dst in enumerate((kqT[:, 0:4, tok(0)], kqT[:, 0:4, tok(1)], kqT[:, 4:8, tok(0)], kqT[:, 4:8, tok(1)],
                                     qT[:, :, tok(0)], qT[:, :, tok(1)])):
                a.wait_ge(at_ps, n + 1)
                a.activation(dst, ps[:, (n + 4) % 8, :].rearrange("p (k c) -> p k c", k=4), ACT.Copy).then_inc(at_sb, 1)
            a.wait_ge(setup, 6)
            for n in range(4):
                a.wait_ge(lt_ps, n + 1)
                dst = xrT[:, :, 3 + n * P:3 + (n + 1) * P] if n < 2 else xgT[:, :, tok(n - 2)]
                a.activation(dst, ps[:, n + 2, :].rearrange("p (k c) -> p k c", k=4), ACT.Copy).then_inc(lt_sb, 1)
            for t in range(NT):
                if t:
                    a.wait_ge(ix_relu, t + 1)
                a.wait_ge(ix_ps, t + 1)
                keys = (t + 1) * P
                src = ps[:, 6, :].rearrange("p (h k) -> p h k", h=4) if t == 0 else \
                    ps[:, 0:2, :].rearrange("p b (h k) -> p (b h) k", h=2)
                a.activation(relu[:, :, 0:keys], src, ACT.Relu, scale=HD ** -0.5).then_inc(ix_relu, 1)
            for n, (dst, bias) in enumerate(((gr, par("lru_ba")), (gi, par("lru_bx")))):
                a.wait_ge(gate_ps, n + 1)
                for k in range(LRU_K):
                    ins = a.activation(dst[:, k, :], ps[:, 2 + 2 * n + k // 2, (k % 2) * SEQ:(k % 2 + 1) * SEQ], ACT.Sigmoid,
                                       bias=bias[:, k:k + 1])
                ins.then_inc(gate_sb, 1)
            a.wait_ge(gate_sb, 2)
            a.wait_ge(setup, 7)
            for k in range(LRU_K):
                ins = a.activation(la[:, k, :], gr[:, k, :], ACT.Exp, scale=c8[:, 6, k:k + 1])
            ins.then_inc(lru_a, 1)
            a.wait_ge(lru_a, 1)
            for k in range(LRU_K):
                ins = a.activation(gr[:, k, :], gr[:, k, :], ACT.Tanh, scale=c8[:, 7, k:k + 1])
            ins.then_inc(lru_a, 1)
            a.activation(xgT[:, :, :], xgT[:, :, :], ACT.Gelu_apprx_tanh).then_inc(lru_gelu, 1)
            a.wait_ge(lru_b1, 1)
            a.activation(gr[:, :, :], gr[:, :, :], ACT.Sqrt).then_inc(lru_bs, 1)
            a.wait_ge(lru_y, 1)
            a.wait_ge(panel_used, chunks["xg"].last + 1)
            a.activation(xT_hi[:, 4:8, :], la[:, :, :], ACT.Copy).then_inc(lru_hi, 1)

            def exps(s):
                a.wait_ge(lg_sb, s + 1)
                keys = (s // 2 + 1) * P
                for j in range(4):
                    ins = a.activation(probs[:, s % 2, j, 0:keys], probs[:, s % 2, j, 0:keys], ACT.Exp,
                                       bias=nmax[:, s, j:j + 1], accum_out=rsum[:, s, j:j + 1])
                ins.then_inc(pr_sb, 1)

            def turned_probs(s):
                a.wait_ge(pt_ps, s + 1)
                n = 4 * (s // 2 + 1)
                if s == 0:
                    src = ps[:, 2, :]
                elif s == 1:
                    src = ps[:, 3, :]
                else:
                    src = ps[:, 2:4, :].rearrange("p b c -> p (b c)")
                if s:
                    a.wait_ge(o_ps, s)
                a.activation(prT[:, 0:n, :], src.rearrange("p (k c) -> p k c", k=n), ACT.Copy).then_inc(pt_sb, 1)

            exps(0)
            exps(1)
            turned_probs(0)
            exps(2)
            turned_probs(1)
            exps(3)
            turned_probs(2)
            turned_probs(3)
            turn_hi(GROUP["o_attn"], 2, to=lambda t: xT_hi[:, 0:4, tok(t)])
            splits(chunks["e_out1"].last + LAG)

            def silu(s, nt, u_, shift, e, j):
                a.wait_ge(s.panel_used, shift + (u_ + 1))
                n = (e * FCH if e is not None else 0)
                if j >= 2 or e is not None:
                    if e is None or j >= 2:
                        a.wait_ge(s.prod, n + (j - 1))
                    else:
                        a.wait_ge(s.prod, n + j)
                src = ps[:, 0:nt, :]
                a.activation(sg[:, j % 2, 0:nt, :], src, ACT.Silu).then_inc(s.silu, 1)

            def aT_part_hi(s, nt, shift, e, j):
                n = (e * FCH if e is not None else 0)
                a.wait_ge(s.aT_ps, n + (j + 1))
                bank = 0 if nt == 2 else 4 + j % 2
                dst = aT_hi[:, j % 2, :, 0:nt * P].rearrange("p k (t c) -> p t k c", t=nt)
                a.activation(dst, ps[:, bank:bank + nt, :].rearrange("p t (k c) -> p t k c", k=4),
                             ACT.Copy).then_inc(s.aT_hi, 1)

            norm(1, GROUP["e_ffn"])
            turn_hi(GROUP["e_ffn"], free=chunks["e_out1"].last + 1)
            base = starts["ffn"]
            for j in range(FCH):
                g1 = base + FFN_AT["g", j, 1]
                splits(g1 + LAG)
                silu(dense, NT, g1, 0, None, j)
                if j:
                    splits(base + FFN_AT["u", j, 1] + LAG)
                    aT_part_hi(dense, NT, 0, None, j - 1)
            splits(base + FFN_AT["d", FCH - 2, 1] + LAG)
            aT_part_hi(dense, NT, 0, None, FCH - 1)
            splits(base + NEXP - 1 + LAG)

            def ple(layer, n, free):
                for half in range(2):
                    src = taken(f"{layer}_emb{half}")
                    a.activation(emb[:, :, half * WC:(half + 1) * WC], src, ACT.Copy).then_inc(chunk_act, 1)
                norm(n, GROUP[f"{layer}_ple"])
                turn_hi(GROUP[f"{layer}_ple"], free=free)
                for half in range(2):
                    src = taken(f"{layer}_gate{half}")
                    a.activation(sg[:, half, :, :], src, ACT.Sigmoid).then_inc(chunk_act, 1)

            ple("e", 2, base + NEXP)

            norm(3, GROUP["o_mix"])
            turn_hi(GROUP["o_mix"], free=chunks["e_gate1"].last + 1)
            src = taken("dt")
            a.activation(dts[:, 0, :, :], src, ACT.Copy).then_inc(chunk_act, 1)
            a.wait_ge(dt_abs, 1)
            a.activation(dts[:, 2, :, :], dts[:, 1, :, :], ACT.Exp, scale=-1.0).then_inc(dt_exp, 1)
            a.activation(dts[:, 5, 0, :], par("a_log"), ACT.Exp).then_inc(dt_exp, 1)
            a.wait_ge(dt_ln, 1)
            a.activation(dts[:, 3, :, :], dts[:, 1, :, :], ACT.Ln).then_inc(dt_ln, 1)

            def stage_in(q, name):
                src = taken(name)
                if q >= 2:
                    a.wait_ge(fw_ps, q - 1)
                a.activation(hn[:, :, (q % 2) * WC:(q % 2 + 1) * WC], src, ACT.Copy).then_inc(chunk_act, 1)

            def forward_out(q):
                a.wait_ge(fw_ps, q + 1)
                if q >= 2:
                    a.wait_ge(cv_raw, q - 1)
                dst = pre[:, q % 2, :, 3:3 + SEQ].rearrange("p k (t c) -> p t k c", t=NT)
                b = 4 + 2 * (q % 2)
                a.activation(dst, ps[:, b:b + 2, :].rearrange("p t (k c) -> p t k c", k=4), ACT.Copy).then_inc(fw_sb, 1)

            def conv_silu(q):
                a.wait_ge(cv_raw, q + 1)
                dst = BT if q == 0 else CT if q == 1 else cv[:, q % 2]
                dst = dst[:, :, :]
                a.activation(dst, cv[:, q % 2, :, :], ACT.Silu).then_inc(cv_done, 1)

            def backward_out(n):
                a.wait_ge(bk_ps, n + 1)
                if n == 0:
                    a.activation(Btok[:, :, :], ps[:, 4, :].rearrange("p (k c) -> p k c", k=4), ACT.Copy).then_inc(bk_sb, 1)
                else:
                    q = n + 1
                    b = 4 + 2 * (q % 2)
                    a.activation(xt[:, :, (n - 1) * WC:n * WC], ps[:, b:b + 2, :], ACT.Copy).then_inc(bk_sb, 1)

            a.wait_ge(setup, 6)
            a.wait_ge(dt_da, 1)
            a.wait_ge(tp_ps, GROUP["o_mix"] + 4)
            stage_in(0, "B")
            stage_in(1, "C")
            forward_out(0)
            stage_in(2, "x0")
            forward_out(1)
            conv_silu(0)
            backward_out(0)
            for q in range(3, 6):
                stage_in(q, f"x{q - 2}")
                forward_out(q - 1)
                conv_silu(q - 2)
                if q >= 4:
                    backward_out(q - 3)

            def z_silu(j):
                src = taken(f"z{j}")
                a.activation(zt[:, :, j * WC:(j + 1) * WC], src, ACT.Silu).then_inc(chunk_act, 1)

            z_silu(0)
            forward_out(5)
            conv_silu(4)
            backward_out(3 - 0)
            z_silu(1)
            conv_silu(5)
            backward_out(4)
            z_silu(2)
            z_silu(3)
            splits(chunks["z3"].last + LAG)
            a.wait_ge(cum_sb, 2)
            a.activation(dec[:, 0, :], dec[:, 0, :], ACT.Exp).then_inc(cum_exp, 1)
            a.activation(dec[:, 1, :], cum[:, 1, :], ACT.Exp).then_inc(cum_exp, 1)
            for i in range(2 * GROUPS):
                a.wait_ge(sg_sb, i + 1)
                a.activation(segs[:, i % 2, :, :], segs[:, i % 2, :, :], ACT.Exp).then_inc(sg_exp, 1)
                if i:
                    if i % 2:
                        a.wait_ge(y_ps, i)
                        if i > 1:
                            a.wait_ge(y_ps, i - 1)
                        a.activation(st[:, :], ps[:, 7, :], ACT.Copy).then_inc(st_sb, 1)
            for i in range(2 * GROUPS):
                g, c = i // 2, i % 2
                a.wait_ge(y_sb, i + 1)
                ins = a.activation(hn[:, 0, 0:WC], xt[:, c, g * WC:(g + 1) * WC], ACT.Square, accum_out=gss[:, 0, c, g:g + 1])
                step(ins)
            a.activation(gss[:, 1, :, :], gss[:, 0, :, :], ACT.Sqrt, scale=1.0 / WC, bias=eps).then_inc(grms, 1)
            a.wait_ge(yn_ready, 2 * GROUPS)
            turn_hi(GROUP["ssd"], 8, free=chunks["z3"].last + 1,
                    to=lambda n: (xT_hi if n // 2 < 2 else yT_hi)[:, 4 * (n // 2 % 2):4 * (n // 2 % 2) + 4, tok(n % 2)])
            splits(starts["experts"] - 1)

            norm(4, GROUP["o_moe"])
            turn_hi(GROUP["o_moe"], free=starts["experts"])
            a.activation(hn_hi[:, :, :], hn[:, :, :], ACT.Copy).then_inc(hn_split, 1)
            a.activation(rt_hi[:, :, :], par("router", a=DM // P), ACT.Copy).then_inc(rt_done, 1)
            a.wait_ge(lw_max, 1)
            a.activation(gw[:, 1, :], gw[:, 0, :], ACT.Exp).then_inc(lw_exp, 1)

            def experts_act(s, first):
                base = first
                with a.Fori(0, NE) as e:
                    shift = e * NEXP
                    done = [0]

                    def ahead(upto):
                        while done[0] <= min(upto, NEXP - 1):
                            i = base + done[0]
                            turn = e * (NEXP // RAW)
                            a.wait_ge(s.raw_in[i % RAW], (turn + (i // RAW + 1)) * 16)
                            if i - SPL + 1 > 0:
                                a.wait_ge(s.panel_used, shift + (i - SPL + 1))
                            a.activation(whi[:, i % SPL, :, :], raw[:, i % RAW, :, :], ACT.Copy).then_inc(s.hi_done, 1)
                            done[0] += 1

                    if base == 0:
                        pass
                    ahead(LAG)
                    a.wait_ge(s.xe_ps, e + 1)
                    a.activation(selT[:, :], ps[:, 6, 0:NT * P], ACT.Copy)
                    a.activation(xT_hi[:, :, 0:P], ps[:, 4:6, :].rearrange("p b (k c) -> p (b k) c", k=4),
                                 ACT.Copy).then_inc(s.xe_hi, 1)
                    for j in range(FCH):
                        u_ = FFN_AT["g", j, 1]
                        ahead(u_ + LAG)
                        a.wait_ge(s.panel_used, shift + (base + u_ + 1))
                        if j >= 2:
                            a.wait_ge(s.prod, e * FCH + (j - 1))
                        a.activation(sg[:, j % 2, 0, :], ps[:, 0, :], ACT.Silu).then_inc(s.silu, 1)
                        if j:
                            ahead(FFN_AT["u", j, 1] + LAG)
                            aT_part_hi(s, 1, shift, e, j - 1)
                    ahead(FFN_AT["d", FCH - 2, 1] + LAG)
                    aT_part_hi(s, 1, shift, e, FCH - 1)
                    ahead(NEXP - 1)
                    a.wait_ge(s.panel_used, shift + (base + NEXP))
                    a.activation(y_hi[:, :], ps[:, 2:4, :].rearrange("p b c -> p (b c)"), ACT.Copy).then_inc(s.y_hi, 1)

            experts_act(main, starts["experts"])
            a.wait_ge(flag_set, 1)
            some = a.value_load(flag[0:1, 0:1], min_val=0, max_val=1)
            with a.If(some != 0):
                experts_act(rest, 0)
            sent[0] = starts["experts"] + NE * NEXP
            splits(chunks["o_emb0"].last + LAG)
            ple("o", 5, None)
            norm(6, GROUP["o_ple"] + 4)

        @block.vector
        def _(v):
            sent = [0]
            steps = [0]

            def step(ins):
                steps[0] += 1
                ins.then_inc(dve_seq, 1)
                v.wait_ge(dve_seq, steps[0])

            def splits(upto):
                while sent[0] <= min(upto, len(panels) - 1) and panels[sent[0]] is not None:
                    i = sent[0]
                    n, width = panels[i][2], panels[i][4]
                    v.wait_ge(hi_done, i + 1)
                    v.tensor_tensor(wlo[:, i % SPL, 0:n, 0:width], raw[:, i % RAW, 0:n, 0:width],
                                    whi[:, i % SPL, 0:n, 0:width], ALU.subtract).then_inc(lo_done, 1)
                    sent[0] += 1

            def taken(name):
                c = chunks[name]
                splits(c.last + LAG)
                v.wait_ge(panel_used, c.last + 1)
                return ps[:, c.banks:c.banks + 2, 0:c.width]

            def norm(n):
                v.wait_ge(rms, n + 1)
                v.wait_ge(gain_in, 16 * (n + 1))
                step(v.reciprocal(stat[:, 2, :], stat[:, 1, :]))
                for t in range(NT):
                    ins = v.scalar_tensor_tensor(hn[:, t, :], h[:, t, :], stat[:, 2, t:t + 1], gain[:, :], ALU.mult, ALU.mult)
                ins.then_inc(hn_ready, 1)

            def turn_lo(first, count=4, to=None, hi=None):
                for n in range(count):
                    g = first + n
                    v.wait_ge(tp_hi, g + 1)
                    at = (slice(None), slice(4 * (n % 2), 4 * (n % 2) + 4), tok(n // 2))
                    dst, high = to(n) if to else (xT_lo[at], xT_hi[at])
                    v.tensor_tensor(dst, ps[:, 4 + g % 4, :].rearrange("p (k c) -> p k c", k=4), high,
                                    ALU.subtract).then_inc(tp_lo, 1)

            def softplus_ln(x_abs, e, one_e, ln, res, tmp):
                pass

            step(v.memset(xrT[:, :, 0:3], 0.0))
            step(v.memset(bd[:, :, :, :], 0.0))
            step(v.memset(kdup[:, :, :, :, :, :], 0.0))
            v.wait_ge(const_in, 16)
            v.tensor_copy(ident_r[:, :], ident).then_inc(setup, 1)
            v.wait_ge(small_in, 16)
            for n, name in enumerate(("lru_wa", "lru_wx")):
                src = par(name, a=LRU_K)
                v.tensor_copy(bd[0:HD, n, :, 0:HD], src[0:HD])
                step(v.tensor_copy(bd[HD:P, n, :, HD:P], src[HD:P]))
            step(v.tensor_scalar(c8[:, 4, :], par("lam"), -1.0, None, ALU.mult))
            v.tensor_tensor(c8[:, 0, :], c8[:, 4, :], par("lam"), ALU.max).then_inc(setup, 1)
            for i in range(2):
                v.wait_ge(tp_hi, i + 1)
                v.tensor_tensor(pT_lo[:, i].rearrange("p k (t c) -> p t k c", t=NT),
                                ps[:, 4 + i, :].rearrange("p (t k c) -> p t k c", t=NT, k=PLE // P),
                                pT_hi[:, i].rearrange("p k (t c) -> p t k c", t=NT), ALU.subtract).then_inc(tp_lo, 1)
            splits(0)
            v.wait_ge(x_in, 16)
            norm(0)
            turn_lo(GROUP["e_mix"])
            splits(chunks["q"].last + LAG)

            v.wait_ge(chunk_act, 3)
            for base, nh in ((U_Q, HEADS + KVH), (U_QI, IDXH + 1)):
                head = u[:, :, base:base + nh * HD].rearrange("p t (h d) -> p t h d", h=nh)
                for t in range(NT):
                    x1, x2 = head[:, t, :, 0:ROT], head[:, t, :, ROT:2 * ROT]
                    r = [rot[:, i, t, 0:nh, :] for i in range(4)]
                    c = cos[:, t, :].unsqueeze(1).to_broadcast([P, nh, ROT])
                    s = sin[:, t, :].unsqueeze(1).to_broadcast([P, nh, ROT])
                    v.tensor_tensor(r[0], x1, c, ALU.mult)
                    v.tensor_tensor(r[1], x2, s, ALU.mult)
                    v.tensor_tensor(r[2], x1, s, ALU.mult)
                    step(v.tensor_tensor(r[3], x2, c, ALU.mult))
                    v.tensor_tensor(x1, r[0], r[1], ALU.subtract)
                    step(v.tensor_tensor(x2, r[2], r[3], ALU.add))
            for t in range(NT):
                for r in range(2):
                    v.tensor_copy(kdup[:, t, 0:KVH, r, r, :], u[:, t, U_K:U_V].rearrange("p (g d) -> p g d", g=KVH))
                    ins = v.tensor_copy(kdup[:, t, KVH, r, r, :], u[:, t, U_KI:U_WI])
            ins.then_inc(roped, 1)
            step(v.tensor_scalar(wi2[:, :, :], u[:, :, U_WI:U_XG], IDXH ** -0.5, None, ALU.mult))
            splits(chunks["xg"].last + LAG)

            v.wait_ge(setup, 3)
            v.tensor_scalar(c8[:, 2, :], c8[:, 1, :], 1.0, None, ALU.add).then_inc(setup, 1)
            v.wait_ge(setup, 5)
            step(v.tensor_scalar(c8[:, 5, :], c8[:, 2, :], -1.0, 1e-30, ALU.add, ALU.max))
            step(v.tensor_scalar(c8[:, 6, :], c8[:, 2, :], 1.0, None, ALU.is_equal))
            step(v.reciprocal(c8[:, 5, :], c8[:, 5, :]))
            step(v.tensor_tensor(c8[:, 3, :], c8[:, 3, :], c8[:, 1, :], ALU.mult))
            step(v.tensor_tensor(c8[:, 3, :], c8[:, 3, :], c8[:, 5, :], ALU.mult))
            step(v.tensor_tensor(c8[:, 6, :], c8[:, 6, :], c8[:, 1, :], ALU.mult))
            step(v.tensor_tensor(c8[:, 3, :], c8[:, 3, :], c8[:, 6, :], ALU.add))
            step(v.tensor_scalar(c8[:, 4, :], c8[:, 4, :], 0.0, None, ALU.max))
            step(v.tensor_tensor(c8[:, 3, :], c8[:, 3, :], c8[:, 4, :], ALU.add))
            v.memset(dts[:, 4, 0, 0:1], 0.0).then_inc(setup, 1)
            step(v.tensor_scalar(c8[:, 6, :], c8[:, 3, :], -8.0, None, ALU.mult))
            v.tensor_scalar(c8[:, 7, :], c8[:, 3, :], 8.0, None, ALU.mult).then_inc(setup, 1)

            v.wait_ge(lt_sb, 2)
            cw = par("lru_w", a=LRU_K)
            for k in range(LRU_K):
                step(v.tensor_scalar(xc[:, k, :], xrT[:, k, 3:3 + SEQ], cw[:, k, 3:4], par("lru_b")[:, k:k + 1], ALU.mult,
                                     ALU.add))
                for j in range(3):
                    ins = v.scalar_tensor_tensor(xc[:, k, :], xrT[:, k, j:j + SEQ], cw[:, k, j:j + 1], xc[:, k, :],
                                                 ALU.mult, ALU.add)
                    if j < 2:
                        step(ins)
            ins.then_inc(conv_done, 1)

            for t in range(NT):
                keys = (t + 1) * P
                v.wait_ge(ix_relu, 2 * t + 1)
                step(v.tensor_scalar(score[:, t, 0:keys], relu[:, 0, 0:keys], wi2[:, t, 0:1], None, ALU.mult))
                for j in range(1, IDXH):
                    ins = v.scalar_tensor_tensor(score[:, t, 0:keys], relu[:, j, 0:keys], wi2[:, t, j:j + 1],
                                                 score[:, t, 0:keys], ALU.mult, ALU.add)
                    if j < IDXH - 1:
                        step(ins)
                if t == 0:
                    ins.then_inc(ix_relu, 1)
                    v.wait_ge(ix_relu, 2)
                else:
                    step(ins)
                step(v.tensor_tensor(score[:, t, t * P:keys], score[:, t, t * P:keys], cmask, ALU.add))
                cur = score[:, t, 0:keys]
                for n in range(NSEL // 8):
                    step(v.max(top8[:, :], cur))
                    step(v.match_replace(work[:, 0:keys], top8[:, :], cur, REPLACED))
                    cur = work[:, 0:keys]
                step(v.tensor_tensor(keep[:, t, 0:keys], cur, score[:, t, 0:keys], ALU.is_equal))
                step(v.tensor_scalar(keep[:, t, 0:keys], keep[:, t, 0:keys], NEG, None, ALU.mult))
                step(v.tensor_tensor(keep[:, t, t * P:keys], keep[:, t, t * P:keys], cmask, ALU.add))

            v.wait_ge(lru_a, 2)
            v.wait_ge(gate_ps, 2)
            aa = xrT[:, :, 0:SEQ]
            step(v.tensor_tensor(aa, la[:, :, :], la[:, :, :], ALU.mult))
            v.scalar_tensor_tensor(gr[:, :, :], aa, 1.0, gr[:, :, :], ALU.add, ALU.mult).then_inc(lru_b1, 1)
            step(v.tensor_tensor(gi[:, :, :], gi[:, :, :], xc[:, :, :], ALU.mult))
            v.wait_ge(lru_bs, 1)
            step(v.tensor_tensor(gi[:, :, :], gi[:, :, :], gr[:, :, :], ALU.mult))
            for k in range(LRU_K):
                ins = v.tensor_tensor_scan(aa[:, k, :], la[:, k, :], gi[:, k, :], 0.0, ALU.mult, ALU.add)
            step(ins)
            v.wait_ge(lru_gelu, 1)
            v.tensor_tensor(la[:, :, :], aa, xgT[:, :, :], ALU.mult).then_inc(lru_y, 1)
            v.wait_ge(lru_y, 1)
            v.wait_ge(lru_hi, 1)
            v.tensor_tensor(xT_lo[:, 4:8, :], la[:, :, :], xT_hi[:, 4:8, :], ALU.subtract).then_inc(lru_lo, 1)

            def masked(s):
                t, keys = s // 2, (s // 2 + 1) * P
                v.wait_ge(lg_ps, s + 1)
                if s >= 2:
                    v.wait_ge(pt_ps, s - 1)
                src = (ps[:, 6, :], ps[:, 7, :], ps[:, 0:2, :], ps[:, 6:8, :])[s]
                src = src.rearrange("p (h k) -> p h k", h=4) if t == 0 else src.rearrange("p b (h k) -> p (b h) k", h=2)
                dst = probs[:, s % 2, :, 0:keys]
                step(v.scalar_tensor_tensor(dst, src, HD ** -0.5, keep[:, t, 0:keys].unsqueeze(1).to_broadcast([P, 4, keys]),
                                            ALU.mult, ALU.add))
                v.tensor_reduce(nmax[:, s, :], dst, AX, ALU.max, negate=True).then_inc(lg_sb, 1)

            def attended(t):
                v.wait_ge(pr_sb, 2 * t + 2)
                v.wait_ge(o_ps, 2 * t + 2)
                step(v.reciprocal(rinv[:, 2 * t:2 * t + 2, :], rsum[:, 2 * t:2 * t + 2, :]))
                r = rinv[:, 2 * t:2 * t + 2, :].rearrange("p a b -> p (a b)").unsqueeze(2).to_broadcast([P, HEADS, HD])
                v.tensor_tensor(hn[:, t, 0:HEADS * HD].rearrange("p (h d) -> p h d", h=HEADS),
                                ps[:, 4 + t, :].rearrange("p (h d) -> p h d", h=HEADS), r, ALU.mult).then_inc(o_sb, 1)

            masked(0)
            masked(1)
            masked(2)
            masked(3)
            attended(0)
            attended(1)
            turn_lo(GROUP["o_attn"], 2, to=lambda t: (xT_lo[:, 0:4, tok(t)], xT_hi[:, 0:4, tok(t)]))

            def add_out(name, half):
                src = taken(name)
                dst = h[:, :, half * WC:(half + 1) * WC]
                v.tensor_tensor(dst, dst, src, ALU.add).then_inc(chunk_dve, 1)

            add_out("e_out0", 0)
            add_out("e_out1", 1)

            def prod(s, nt, count_used, count, j):
                v.wait_ge(s.panel_used, count_used)
                v.wait_ge(s.silu, count + 1)
                ub = 2 if nt == 2 else 1
                v.tensor_tensor(act[:, j % 2, 0:nt, :], sg[:, j % 2, 0:nt, :], ps[:, ub:ub + nt, :], ALU.mult).then_inc(
                    s.prod, 1)

            def aT_part_lo(s, nt, count, j):
                v.wait_ge(s.aT_hi, count + 1)
                bank = 0 if nt == 2 else 4 + j % 2
                view = [b[:, j % 2, :, 0:nt * P].rearrange("p k (t c) -> p t k c", t=nt) for b in (aT_lo, aT_hi)]
                v.tensor_tensor(view[0], ps[:, bank:bank + nt, :].rearrange("p t (k c) -> p t k c", k=4), view[1],
                                ALU.subtract).then_inc(s.aT_lo, 1)

            norm(1)
            turn_lo(GROUP["e_ffn"])
            base = starts["ffn"]
            for j in range(FCH):
                u1 = base + FFN_AT["u", j, 1]
                splits(u1 + LAG)
                if j >= 2:
                    v.wait_ge(dense.aT_ps, j - 1)
                prod(dense, NT, u1 + 1, j, j)
                if j:
                    aT_part_lo(dense, NT, j - 1, j - 1)
            splits(base + FFN_AT["d", FCH - 2, 1] + LAG)
            aT_part_lo(dense, NT, FCH - 1, FCH - 1)
            splits(base + NEXP - 1 + LAG)
            v.wait_ge(panel_used, base + NEXP)
            for t in range(NT):
                ins = v.tensor_tensor(h[:, t, :], h[:, t, :], ps[:, 4 + 2 * t:6 + 2 * t, :].rearrange("p b c -> p (b c)"),
                                      ALU.add)
            ins.then_inc(dense.summed, 1)

            def ple(layer, n):
                norm(n)
                turn_lo(GROUP[f"{layer}_ple"])
                for half in range(2):
                    c = chunks[f"{layer}_gate{half}"]
                    splits(c.last + LAG)
                    v.wait_ge(*evacuated(c.number))
                    cols = slice(half * WC, (half + 1) * WC)
                    step(v.tensor_tensor(emb[:, :, cols], emb[:, :, cols], sg[:, half, :, :], ALU.mult))
                    ins = v.tensor_tensor(h[:, :, cols], h[:, :, cols], emb[:, :, cols], ALU.add)
                    if half == 0:
                        step(ins)
                ins.then_inc(gate_ple, 1)

            splits(chunks["e_emb1"].last + LAG)
            ple("e", 2)

            norm(3)
            turn_lo(GROUP["o_mix"])
            c = chunks["dt"]
            splits(c.last + LAG)
            v.memset(pre[:, :, :, 0:3], 0.0)
            v.wait_ge(*evacuated(c.number))
            raw_dt, d1, d2, d3, d4, d5 = (dts[:, i, :, :] for i in range(6))
            step(v.tensor_tensor(raw_dt, raw_dt, par("dt_bias").unsqueeze(1).to_broadcast([P, NT, SH]), ALU.add))
            step(v.tensor_scalar(d3, raw_dt, -1.0, None, ALU.mult))
            v.tensor_tensor(d1, raw_dt, d3, ALU.max).then_inc(dt_abs, 1)
            v.wait_ge(dt_abs, 1)
            v.wait_ge(dt_exp, 1)
            v.tensor_scalar(d1, d2, 1.0, None, ALU.add).then_inc(dt_ln, 1)
            v.wait_ge(dt_ln, 2)
            step(v.tensor_scalar(d4, d1, -1.0, 1e-30, ALU.add, ALU.max))
            step(v.reciprocal(d4, d4))
            step(v.tensor_tensor(d3, d3, d2, ALU.mult))
            step(v.tensor_tensor(d3, d3, d4, ALU.mult))
            step(v.tensor_scalar(d4, d1, 1.0, None, ALU.is_equal))
            step(v.tensor_tensor(d4, d4, d2, ALU.mult))
            step(v.tensor_tensor(d3, d3, d4, ALU.add))
            step(v.tensor_scalar(raw_dt, raw_dt, 0.0, None, ALU.max))
            step(v.tensor_tensor(raw_dt, raw_dt, d3, ALU.add))
            v.wait_ge(dt_exp, 2)
            step(v.tensor_scalar(dts[:, 5, 0, :], dts[:, 5, 0, :], -1.0, None, ALU.mult))
            v.tensor_tensor(d1, raw_dt, dts[:, 5, 0, :].unsqueeze(1).to_broadcast([P, NT, SH]), ALU.mult).then_inc(dt_da, 1)

            def convolve(q):
                v.wait_ge(fw_sb, q + 1)
                if q >= 2:
                    if q < 4:
                        v.wait_ge(cv_done, q - 1)
                    else:
                        v.wait_ge(bk_ps, q - 2)
                k0 = {0: 16, 1: 20}.get(q, 4 * (q - 2))
                cw_ = par("conv_w", a=24)
                for k in range(4):
                    dst = cv[:, q % 2, k, :]
                    step(v.tensor_scalar(dst, pre[:, q % 2, k, 3:3 + SEQ], cw_[:, k0 + k, 3:4],
                                         par("conv_b")[:, k0 + k:k0 + k + 1], ALU.mult, ALU.add))
                    for j in range(3):
                        ins = v.scalar_tensor_tensor(dst, pre[:, q % 2, k, j:j + SEQ], cw_[:, k0 + k, j:j + 1], dst,
                                                     ALU.mult, ALU.add)
                        if j < 2:
                            step(ins)
                ins.then_inc(cv_raw, 1)

            splits(chunks["x0"].last)
            convolve(0)
            for q in range(1, 6):
                name = f"x{q}" if q < 4 else f"z{q - 4}"
                splits(chunks[name].last)
                convolve(q)
            splits(chunks["z3"].last + LAG)

            v.wait_ge(cum_ps, 1)
            v.tensor_copy(cum[:, :, :], ps[:, 6, 0:3 * SH].rearrange("p (a b) -> p a b", a=3)).then_inc(cum_sb, 1)
            v.wait_ge(cum_sb, 1)
            v.tensor_tensor(dec[:, 0, :], cum[:, 2, :], cum[:, 0, :], ALU.subtract).then_inc(cum_sb, 1)
            dt = dts[:, 0, :, :]

            def by_head(ap):
                return ap.rearrange("p (h d) -> p h d", h=HPG)

            def spread(ap, n=HD):
                return ap.unsqueeze(2).to_broadcast([P, HPG, n])

            def y_out(i):
                g, c = i // 2, i % 2
                xg_ = xt[:, c, g * WC:(g + 1) * WC]
                hs = slice(g * HPG, (g + 1) * HPG)
                v.wait_ge(y_ps, i + 1)
                step(v.tensor_tensor(by_head(xg_), by_head(xg_), spread(par("d_skip")[:, hs]), ALU.mult))
                step(v.tensor_tensor(xg_, xg_, ps[:, 6, :], ALU.add))
                if c:
                    step(v.tensor_tensor(by_head(yt[:, :]), by_head(ps[:, 7, :]), spread(dec[:, 1, hs]), ALU.mult))
                    step(v.tensor_tensor(xg_, xg_, yt[:, :], ALU.add))
                v.tensor_tensor(xg_, xg_, zt[:, c, g * WC:(g + 1) * WC], ALU.mult).then_inc(y_sb, 1)

            v.wait_ge(cum_exp, 2)
            v.wait_ge(cv_done, 6)
            v.wait_ge(bk_ps, 5)
            v.wait_ge(bk_sb, 5)
            v.wait_ge(chunk_act, evacuated(chunks["z3"].number)[1])
            for i in range(2 * GROUPS):
                g, c = i // 2, i % 2
                hs = slice(g * HPG, (g + 1) * HPG)
                v.wait_ge(sg_ps, i + 1)
                if i >= 2:
                    v.wait_ge(y_ps, i - 1)
                v.tensor_tensor(cbm[:, i % 2, :], ps[:, i % 2, 0:P], tri, ALU.mult)
                b = 2 + 2 * (i % 2)
                sgv = segs[:, i % 2, :, :]
                step(v.tensor_tensor(sgv, ps[:, b:b + 2, :].rearrange("p b (h c) -> p (b h) c", h=4),
                                     spread(cum[:, c, hs], P), ALU.subtract))
                v.tensor_scalar(sgv, sgv, 0.0, None, ALU.min).then_inc(sg_sb, 1)
                step(v.tensor_tensor(by_head(xdt[:, i % 2, :]), by_head(xt[:, c, g * WC:(g + 1) * WC]), spread(dt[:, c, hs]),
                                     ALU.mult))
                if c == 0:
                    step(v.tensor_tensor(by_head(xtl[:, :]), by_head(xdt[:, i % 2, :]), spread(dec[:, 0, hs]), ALU.mult))
                if i:
                    y_out(i - 1)
                v.wait_ge(sg_exp, i + 1)
                v.tensor_tensor(sgv, sgv, cbm[:, i % 2, :].unsqueeze(1).to_broadcast([P, HPG, P]), ALU.mult).then_inc(
                    m_done, 1)
            y_out(2 * GROUPS - 1)
            v.wait_ge(grms, 1)
            v.wait_ge(gn_in, 16)
            step(v.reciprocal(gss[:, 2, :, :], gss[:, 1, :, :]))
            for g in range(GROUPS):
                for c in range(NT):
                    y = xt[:, c, g * WC:(g + 1) * WC]
                    v.scalar_tensor_tensor(y, y, gss[:, 2, c, g:g + 1], gn[:, g * WC:(g + 1) * WC], ALU.mult,
                                           ALU.mult).then_inc(yn_ready, 1)

            def y_parts(n):
                at = (slice(None), slice(4 * (n // 2 % 2), 4 * (n // 2 % 2) + 4), tok(n % 2))
                return (xT_lo[at], xT_hi[at]) if n // 2 < 2 else (yT_lo[at], yT_hi[at])

            turn_lo(GROUP["ssd"], 8, to=y_parts)
            add_out("o_out0", 0)
            add_out("o_out1", 1)

            norm(4)
            turn_lo(GROUP["o_moe"])
            v.wait_ge(hn_split, 1)
            v.wait_ge(hn_ready, 5)
            v.tensor_tensor(hn_lo[:, :, :], hn[:, :, :], hn_hi[:, :, :], ALU.subtract).then_inc(hn_split, 1)
            v.wait_ge(rt_done, 1)
            v.tensor_tensor(rt_lo[:, :, :], par("router", a=DM // P), rt_hi[:, :, :], ALU.subtract).then_inc(rt_done, 1)
            v.wait_ge(rt_ps, 1)
            step(v.tensor_copy(lg[:, :, :], ps[:, 4, 0:NT * NE].rearrange("p (t e) -> p t e", t=NT)))
            for t in range(NT):
                step(v.max(lmax[:, t, :], lg[:, t, :]))
                step(v.max_index(lidx[:, t, :], lmax[:, t, :], lg[:, t, :]))
                step(v.tensor_copy(lidf[:, t, :], lidx[:, t, :]))
                for n in range(2):
                    step(v.tensor_scalar(oh[:, n, t, :], iota[:, 0:NE], lidf[:, t, n:n + 1], None, ALU.is_equal))
            v.tensor_tensor(gw[:, 0, :], lmax[:, :, 1], lmax[:, :, 0], ALU.subtract).then_inc(lw_max, 1)
            v.tensor_tensor(routed[:, :, :], oh[:, 0, :, :], oh[:, 1, :, :], ALU.add).then_inc(routed_sb, 1)
            v.wait_ge(lw_exp, 1)
            step(v.tensor_scalar(gw[:, 2, :], gw[:, 1, :], 1.0, None, ALU.add))
            step(v.reciprocal(gw[:, 2, :], gw[:, 2, :]))
            step(v.tensor_tensor(gw[:, 3, :], gw[:, 1, :], gw[:, 2, :], ALU.mult))
            for t in range(NT):
                step(v.tensor_scalar(gates[:, t, :], oh[:, 0, t, :], gw[:, 2, t:t + 1], None, ALU.mult))
                step(v.scalar_tensor_tensor(gates[:, t, :], oh[:, 1, t, :], gw[:, 3, t:t + 1], gates[:, t, :], ALU.mult,
                                            ALU.add))
            v.wait_ge(slot_ps, 1)
            v.wait_ge(routed_sb, 1)
            pos = ps[:, 5, 0:NT * NE].rearrange("p (t e) -> p t e", t=NT)
            step(v.tensor_tensor(slot[:, 0, :, :], pos, routed[:, :, :], ALU.mult))
            step(v.tensor_scalar(slot[:, 0, :, :], slot[:, 0, :, :], -1.0, None, ALU.add))
            step(v.tensor_scalar(slot[:, 1, :, :], slot[:, 0, :, :], -float(P), None, ALU.add))
            step(v.tensor_reduce(most[:, 0:1], ps[:, 5, NT * NE:(NT + 1) * NE], AX, ALU.max))
            step(v.tensor_scalar(most[:, 1:2], most[:, 0:1], P + 0.5, None, ALU.is_gt))
            v.tensor_copy(flag[:, 0:1], most[:, 1:2]).then_inc(flag_set, 1)

            def experts_dve(s, first, turn):
                base = first
                with v.Fori(0, NE) as e:
                    shift = e * NEXP
                    done = [0]

                    def ahead(upto):
                        while done[0] <= min(upto, NEXP - 1):
                            i = base + done[0]
                            v.wait_ge(s.hi_done, shift + (i + 1))
                            v.tensor_tensor(wlo[:, i % SPL, :, :], raw[:, i % RAW, :, :], whi[:, i % SPL, :, :],
                                            ALU.subtract).then_inc(s.lo_done, 1)
                            done[0] += 1

                    for t in range(NT):
                        ins = v.tensor_scalar(sel[:, t, :], iota, slot[:, turn, t, bass.ds(e, 1)], None, ALU.is_equal)
                    ins.then_inc(s.sel, 1)
                    ahead(LAG)
                    v.wait_ge(s.xe_hi, e + 1)
                    v.tensor_tensor(xT_lo[:, :, 0:P], ps[:, 4:6, :].rearrange("p b (k c) -> p (b k) c", k=4),
                                    xT_hi[:, :, 0:P], ALU.subtract).then_inc(s.xe_lo, 1)
                    for j in range(FCH):
                        u1 = FFN_AT["u", j, 1]
                        ahead(u1 + LAG)
                        if j >= 2:
                            v.wait_ge(s.aT_ps, e * FCH + (j - 1))
                        v.wait_ge(s.panel_used, shift + (base + u1 + 1))
                        v.wait_ge(s.silu, e * FCH + (j + 1))
                        v.tensor_tensor(act[:, j % 2, 0, :], sg[:, j % 2, 0, :], ps[:, 1, :], ALU.mult).then_inc(s.prod, 1)
                        if j:
                            aT_part_lo(s, 1, e * FCH + (j - 1), j - 1)
                    ahead(FFN_AT["d", FCH - 2, 1] + LAG)
                    aT_part_lo(s, 1, e * FCH + (FCH - 1), FCH - 1)
                    ahead(NEXP - 1)
                    v.wait_ge(s.y_hi, e + 1)
                    v.tensor_tensor(y_lo[:, :], ps[:, 2:4, :].rearrange("p b c -> p (b c)"), y_hi[:, :],
                                    ALU.subtract).then_inc(s.y_lo, 1)
                    v.wait_ge(s.back_ps, e + 1)
                    for t in range(NT):
                        ins = v.scalar_tensor_tensor(h[:, t, :], ps[:, 4 + 2 * t:6 + 2 * t, :].rearrange("p b c -> p (b c)"),
                                                     gates[:, t, bass.ds(e, 1)], h[:, t, :], ALU.mult, ALU.add)
                    ins.then_inc(s.summed, 1)
                    v.wait_ge(s.summed, e + 1)

            experts_dve(main, starts["experts"], 0)
            v.wait_ge(flag_set, 1)
            some = v.value_load(flag[0:1, 0:1], min_val=0, max_val=1)
            with v.If(some != 0):
                experts_dve(rest, 0, 1)
            v.sem_inc(gate_ple, 1)
            sent[0] = starts["experts"] + NE * NEXP
            splits(chunks["o_emb1"].last + LAG)
            ple("o", 5)
            v.wait_ge(rms, 7)
            v.wait_ge(gain_in, 16 * 7)
            step(v.reciprocal(stat[:, 2, :], stat[:, 1, :]))
            for t in range(NT):
                ins = v.scalar_tensor_tensor(hn[:, t, :], h[:, t, :], stat[:, 2, t:t + 1], gain[:, :], ALU.mult, ALU.mult)
            ins.then_inc(fin, 1)

        @block.tensor
        def _(pe):
            def turn(g, srcs):
                if g >= 4:
                    pe.wait_ge(tp_hi, g - 3)
                    pe.wait_ge(tp_lo, g - 3)
                for n, src in enumerate(srcs):
                    ins = pe.transpose(ps[:, 4 + g % 4, n * P:(n + 1) * P], src, ident)
                ins.then_inc(tp_ps, 1)

            def turn_hn(first, n):
                pe.wait_ge(hn_ready, n)
                for i in range(4):
                    turn(first + i, [hn[:, i // 2, (4 * (i % 2) + k) * P:(4 * (i % 2) + k + 1) * P] for k in range(4)])
                pe.wait_ge(tp_hi, first + 4)
                pe.wait_ge(tp_lo, first + 4)

            def three(out_ap, left, right, first, last):
                (lh, ll), (rh, rl) = left, right
                pe.matmul(out_ap, lh, rh, start=first, stop=False)
                pe.matmul(out_ap, lh, rl, start=False, stop=False)
                return pe.matmul(out_ap, ll, rh, start=False, stop=last)

            def left_xT(k, t):
                return xT_hi[:, k, tok(t)], xT_lo[:, k, tok(t)]

            def left_y(k, t):
                return left_xT(k, t) if k < 8 else (yT_hi[:, k - 8, tok(t)], yT_lo[:, k - 8, tok(t)])

            def panel_mm(i, outs, left, k0, n, width, first, last):
                for k in range(n):
                    for t, o in enumerate(outs):
                        ins = three(o, left(k0 + k, t), (whi[:, i % SPL, k, 0:width], wlo[:, i % SPL, k, 0:width]),
                                    first and k == 0, last and k == n - 1)
                return ins

            def chunk(name, left=left_xT):
                c = chunks[name]
                if c.number >= 2:
                    pe.wait_ge(*evacuated(c.number - 2))
                for n in range(c.panels):
                    i = c.first + n
                    k = min(KS, c.ksubs - n * KS)
                    pe.wait_ge(lo_done, i + 1)
                    outs = [ps[:, c.banks + t, 0:c.width] for t in range(NT)]
                    panel_mm(i, outs, left, n * KS, k, c.width, n == 0, n == c.panels - 1).then_inc(panel_used, 1)

            def blocks(ap, n):
                return [ap[:, k * P:(k + 1) * P] for k in range(n)]

            pe.wait_ge(const_in, 16)
            pe.wait_ge(p_in, 16)
            for i in range(2):
                turn(i, [pin[:, i * NT + t, k * P:(k + 1) * P] for t in range(NT) for k in range(PLE // P)])
            turn_hn(GROUP["e_mix"], 1)
            for name in ("kv_qi", "ki_wi", "q", "xr", "xg"):
                chunk(name)

            pe.wait_ge(roped, 1)
            pe.wait_ge(*evacuated(chunks["xg"].number))
            for n in range(6):
                t = n % 2
                if n < 2:
                    srcs = [kdup[:, t, g, r].rearrange("p a d -> p (a d)") for g in range(KVH) for r in range(2)]
                elif n < 4:
                    srcs = [kdup[:, t, KVH, r].rearrange("p a d -> p (a d)") for r in range(2)] + blocks(u[:, t, U_QI:U_KI], 2)
                else:
                    srcs = blocks(u[:, t, U_Q:U_K], 4)
                for k, src in enumerate(srcs):
                    ins = pe.transpose(ps[:, (n + 4) % 8, k * P:(k + 1) * P], src, ident)
                ins.then_inc(at_ps, 1)
            for n in range(4):
                if n >= 2:
                    pe.wait_ge(at_sb, n - 1)
                b = U_XR if n < 2 else U_XG
                for k, src in enumerate(blocks(u[:, n % 2, b:b + LRU], 4)):
                    ins = pe.transpose(ps[:, n + 2, k * P:(k + 1) * P], src, ident)
                ins.then_inc(lt_ps, 1)
            for t in range(NT):
                pe.wait_ge(at_sb, 4 if t == 0 else 6)
                keys = (t + 1) * P
                for j in range(IDXH):
                    o = ps[:, 6, j * P:(j + 1) * P] if t == 0 else ps[:, j // 2, (j % 2) * SEQ:(j % 2 + 1) * SEQ]
                    ins = pe.matmul(o, kqT[:, 6 + j // 2, tok(t)], kqT[:, 4 + j % 2, 0:keys], start=True, stop=True)
                ins.then_inc(ix_ps, 1)
            pe.wait_ge(lt_sb, 4)
            pe.wait_ge(conv_done, 1)
            for n in range(2):
                for k in range(LRU_K):
                    ins = pe.matmul(ps[:, 2 + 2 * n + k // 2, (k % 2) * SEQ:(k % 2 + 1) * SEQ], bd[:, n, k, :], xc[:, k, :],
                                    start=True, stop=True)
                ins.then_inc(gate_ps, 1)

            def logits(s):
                t, g, keys = s // 2, s % 2, (s // 2 + 1) * P
                if s == 0:
                    pe.wait_ge(ix_relu, 1)
                elif s == 2:
                    pe.wait_ge(ix_relu, 3)
                elif s == 3:
                    pe.wait_ge(lg_sb, 2)
                for j in range(4):
                    hd = 4 * g + j
                    o = ps[:, 6 + s, j * P:(j + 1) * P] if t == 0 else \
                        ps[:, (0 if s == 2 else 6) + j // 2, (j % 2) * SEQ:(j % 2 + 1) * SEQ]
                    ins = pe.matmul(o, qT[:, hd // 2, tok(t)], kqT[:, 2 * g + hd % 2, 0:keys], start=True, stop=True)
                ins.then_inc(lg_ps, 1)

            def turn_probs(s):
                t = s // 2
                pe.wait_ge(pr_sb, s + 1)
                if s >= 2:
                    pe.wait_ge(pt_sb, s)
                for j in range(4):
                    for kb in range(t + 1):
                        n = j * (t + 1) + kb
                        bank = 2 + s if t == 0 else 2 + n // 4
                        ins = pe.transpose(ps[:, bank, (n % 4) * P:(n % 4 + 1) * P], probs[:, s % 2, j, tok(kb)], ident)
                ins.then_inc(pt_ps, 1)

            def attend(s):
                t, g = s // 2, s % 2
                pe.wait_ge(pt_sb, s + 1)
                for j in range(4):
                    hd = 4 * g + j
                    for kb in range(t + 1):
                        ins = pe.matmul(ps[:, 4 + t, hd * HD:(hd + 1) * HD], prT[:, j * (t + 1) + kb, :],
                                        u[:, kb, U_V + g * HD:U_V + (g + 1) * HD], start=(kb == 0), stop=(kb == t))
                ins.then_inc(o_ps, 1)

            logits(0)
            logits(1)
            logits(2)
            pe.wait_ge(gate_sb, 2)
            turn_probs(0)
            logits(3)
            turn_probs(1)
            attend(0)
            attend(1)
            turn_probs(2)
            attend(2)
            turn_probs(3)
            attend(3)
            for t in range(NT):
                pe.wait_ge(o_sb, t + 1)
                if t == 0:
                    pe.wait_ge(lg_sb, 4)
                turn(GROUP["o_attn"] + t, blocks(hn[:, t, 0:HEADS * HD], 4))
            pe.wait_ge(tp_lo, GROUP["o_attn"] + 2)
            pe.wait_ge(lru_lo, 1)
            chunk("e_out0")
            chunk("e_out1")

            def ffn(s, nt, base, e, left):
                shift = e * NEXP if e is not None else 0
                count = e * FCH if e is not None else 0
                ub = nt
                db = 4 if nt == 2 else 2

                def panel(step_, outs, left_, k0, first, last):
                    i = base + FFN_AT[step_]
                    pe.wait_ge(s.lo_done, shift + (i + 1))
                    panel_mm(i, outs, left_, k0, KS, WC, first, last).then_inc(s.panel_used, 1)

                def turn_act(j):
                    pe.wait_ge(s.prod, count + (j + 1))
                    if nt == 2:
                        pe.wait_ge(s.silu, min(j + 2, FCH))
                    elif j >= 2:
                        pe.wait_ge(s.aT_lo, count + (j - 1))
                    for t in range(nt):
                        bank = t if nt == 2 else 4 + j % 2
                        for k in range(4):
                            ins = pe.transpose(ps[:, bank, k * P:(k + 1) * P], act[:, j % 2, t, k * P:(k + 1) * P], ident)
                    ins.then_inc(s.aT_ps, 1)

                def down(j):
                    pe.wait_ge(s.aT_lo, count + (j + 1))
                    for half in range(2):
                        outs = [ps[:, db + 2 * t + half, :] for t in range(nt)]
                        panel(("d", j, half), outs, lambda k, t: (aT_hi[:, j % 2, k, tok(t)], aT_lo[:, j % 2, k, tok(t)]),
                              0, j == 0, j == FCH - 1)

                for j in range(FCH):
                    if j:
                        pe.wait_ge(s.silu, count + j)
                        if nt == 2 and j >= 2:
                            pe.wait_ge(s.aT_lo, j - 1)
                    for half in range(2):
                        panel(("g", j, half), [ps[:, t, :] for t in range(nt)], left, KS * half, half == 0, half == 1)
                    if j:
                        pe.wait_ge(s.prod, count + j)
                    for half in range(2):
                        panel(("u", j, half), [ps[:, ub + t, :] for t in range(nt)], left, KS * half, half == 0, half == 1)
                    if j:
                        turn_act(j - 1)
                    if j >= 2:
                        down(j - 2)
                down(FCH - 2)
                turn_act(FCH - 1)
                down(FCH - 1)

            turn_hn(GROUP["e_ffn"], 2)
            ffn(dense, NT, starts["ffn"], None, left_xT)

            def ple(layer, index, first, n):
                def left_p(k, t):
                    return pT_hi[:, index, k, tok(t)], pT_lo[:, index, k, tok(t)]
                for half in range(2):
                    chunk(f"{layer}_emb{half}", left_p)
                turn_hn(first, n)
                for half in range(2):
                    chunk(f"{layer}_gate{half}")

            ple("e", 0, GROUP["e_ple"], 3)

            turn_hn(GROUP["o_mix"], 4)
            stage = ["B", "C", "x0", "x1", "x2", "x3"]

            def forward(q):
                pe.wait_ge(*evacuated(chunks[stage[q]].number))
                if q >= 2:
                    pe.wait_ge(fw_sb, q - 1)
                    if q != 3:
                        pe.wait_ge(bk_sb, 1 if q == 2 else q - 2)
                for t in range(NT):
                    for k, src in enumerate(blocks(hn[:, t, (q % 2) * WC:(q % 2 + 1) * WC], 4)):
                        ins = pe.transpose(ps[:, 4 + 2 * (q % 2) + t, k * P:(k + 1) * P], src, ident)
                ins.then_inc(fw_ps, 1)

            def backward(q):
                pe.wait_ge(cv_done, q + 1)
                if q == 1:
                    return
                src = BT if q == 0 else cv[:, q % 2]
                for t in range(1 if q == 0 else NT):
                    for k in range(4):
                        ins = pe.transpose(ps[:, 4 + 2 * (q % 2) + t, k * P:(k + 1) * P], src[:, k, tok(t)], ident)
                ins.then_inc(bk_ps, 1)

            chunk("dt")
            chunk("B")
            chunk("C")
            forward(0)
            chunk("x0")
            forward(1)
            backward(0)
            for q in range(2, 6):
                chunk(f"x{q - 1}" if q < 5 else "z0")
                forward(q)
                backward(q - 1)
            chunk("z1")
            backward(5)
            chunk("z2")
            chunk("z3")

            pe.wait_ge(dt_da, 1)
            pe.wait_ge(bk_sb, 5)
            pe.wait_ge(chunk_act, evacuated(chunks["z3"].number)[1])
            da = dts[:, 1, :, :]
            for c in range(NT):
                pe.matmul(ps[:, 6, c * SH:(c + 1) * SH], tri, da[:, c, :], start=True, stop=True)
            pe.matmul(ps[:, 6, 2 * SH:3 * SH], ones, da[:, 0, :], start=True, stop=True).then_inc(cum_ps, 1)

            def decays(i):
                g, c = i // 2, i % 2
                if i >= 2:
                    pe.wait_ge(sg_sb, i - 1)
                pe.matmul(ps[:, i % 2, 0:P], BT[:, g, tok(c)], CT[:, g, tok(c)], start=True, stop=True)
                for j in range(HPG):
                    ins = pe.matmul(ps[:, 2 + 2 * (i % 2) + j // 4, (j % 4) * P:(j % 4 + 1) * P],
                                    da[:, c, g * HPG + j:g * HPG + j + 1].to_broadcast([P, P]), tri, start=True, stop=True)
                ins.then_inc(sg_ps, 1)

            def ssd(i):
                g, c = i // 2, i % 2
                pe.wait_ge(m_done, i + 1)
                if i:
                    pe.wait_ge(y_sb, i)
                else:
                    pe.wait_ge(cum_sb, 1)
                for j in range(HPG):
                    ins = pe.matmul(ps[:, 6, j * HD:(j + 1) * HD], segs[:, i % 2, j, :],
                                    xdt[:, i % 2, j * HD:(j + 1) * HD], start=True, stop=True)
                if c == 0:
                    ins = pe.matmul(ps[:, 7, :], Btok[:, g, :], xtl[:, :], start=True, stop=True)
                else:
                    pe.wait_ge(st_sb, g + 1)
                    ins = pe.matmul(ps[:, 7, :], CT[:, g, tok(1)], st[:, :], start=True, stop=True)
                ins.then_inc(y_ps, 1)

            decays(0)
            for i in range(2 * GROUPS):
                if i + 1 < 2 * GROUPS:
                    decays(i + 1)
                ssd(i)
            for n in range(8):
                g, t = n // 2, n % 2
                pe.wait_ge(yn_ready, n + 1)
                turn(GROUP["ssd"] + n, blocks(xt[:, t, g * WC:(g + 1) * WC], 4))
            pe.wait_ge(tp_lo, GROUP["ssd"] + 8)
            chunk("o_out0", left_y)
            chunk("o_out1", left_y)

            turn_hn(GROUP["o_moe"], 5)
            pe.wait_ge(rt_done, 2)
            for t in range(NT):
                for k in range(DM // P):
                    ins = three(ps[:, 4, t * NE:(t + 1) * NE], left_xT(k, t), (rt_hi[:, k, :], rt_lo[:, k, :]), k == 0,
                                k == DM // P - 1)
            ins.then_inc(rt_ps, 1)
            pe.wait_ge(routed_sb, 1)
            pe.matmul(ps[:, 5, 0:NE], tri, routed[:, 0, :], start=True, stop=True)
            pe.matmul(ps[:, 5, NE:2 * NE], tri, routed[:, 1, :], start=True, stop=False)
            pe.matmul(ps[:, 5, NE:2 * NE], ones, routed[:, 0, :], start=False, stop=True)
            pe.matmul(ps[:, 5, 2 * NE:3 * NE], ones, routed[:, 0, :], start=True, stop=False)
            pe.matmul(ps[:, 5, 2 * NE:3 * NE], ones, routed[:, 1, :], start=False, stop=True).then_inc(slot_ps, 1)
            pe.wait_ge(flag_set, 1)
            pe.wait_ge(hn_split, 2)
            pe.wait_ge(setup, 1)

            def experts_pe(s, base):
                with pe.Fori(0, NE) as e:
                    pe.wait_ge(s.sel, e + 1)
                    for k in range(DM // P):
                        o = ps[:, 4 + k // 4, (k % 4) * P:(k % 4 + 1) * P]
                        for n, (t, part) in enumerate(((0, hn_hi), (0, hn_lo), (1, hn_hi), (1, hn_lo))):
                            pe.matmul(o, part[:, t, k * P:(k + 1) * P], sel[:, t, :], start=(n == 0), stop=(n == 3))
                    for t in range(NT):
                        ins = pe.matmul(ps[:, 6, tok(t)], sel[:, t, :], ident_r[:, :], start=True, stop=True)
                    ins.then_inc(s.xe_ps, 1)
                    pe.wait_ge(s.xe_lo, e + 1)
                    ffn(s, 1, base, e, left_xT)
                    pe.wait_ge(s.y_lo, e + 1)
                    for t in range(NT):
                        for half in range(2):
                            cols = slice(half * WC, (half + 1) * WC)
                            pe.matmul(ps[:, 4 + 2 * t + half, :], selT[:, tok(t)], y_hi[:, cols], start=True, stop=False)
                            ins = pe.matmul(ps[:, 4 + 2 * t + half, :], selT[:, tok(t)], y_lo[:, cols], start=False,
                                            stop=True)
                    ins.then_inc(s.back_ps, 1)

            experts_pe(main, starts["experts"])
            some = pe.value_load(flag[0:1, 0:1], min_val=0, max_val=1)
            with pe.If(some != 0):
                experts_pe(rest, 0)
            ple("o", 1, GROUP["o_ple"], 6)


_WEIGHTS = ["e_mix_norm", "e_w_in", "e_w_out", "e_ffn_norm", "e_ffn_wg", "e_ffn_wu", "e_ffn_wd", "e_ple_proj",
            "e_ple_gate_norm", "e_ple_gate", "o_mix_norm", "o_w_in", "o_gnorm", "o_w_out", "o_moe_norm", "o_exp_wg",
            "o_exp_wu", "o_exp_wd", "o_ple_proj", "o_ple_gate_norm", "o_ple_gate", "final_norm"]


def kernel(**inputs):
    import concourse.bacc as _bacc
    from concourse.bass_utils import run_bass_kernel_spmd as _run

    nc = _bacc.Bacc("TRN2", target_bir_lowering=False, num_devices=1)
    arrays = {}

    def dram(name, a):
        a = np.ascontiguousarray(a)
        arrays[f"in_{name}_dram"] = a
        return nc.dram_tensor(f"in_{name}_dram", a.shape, mybir.dt.from_np(a.dtype), kind="ExternalInput").ap()

    r = np.arange(P)
    inv = np.float32(500000.0) ** (-np.arange(ROT, dtype=np.float32) / np.float32(ROT))
    ang = np.arange(SEQ, dtype=np.float32)[:, None] * inv[None, :].astype(np.float32)
    by_tile = lambda a: a.reshape(NT, P, ROT).transpose(1, 0, 2).reshape(P, NT * ROT)
    const = np.concatenate([
        np.eye(P), np.where(r[None, :] <= r[:, None], 0.0, NEG), r[:, None] <= r[None, :], np.ones((P, P)),
        np.broadcast_to(r[None, :], (P, P)), by_tile(np.cos(ang)), by_tile(np.sin(ang)), np.full((P, 1), EPS)],
        axis=1).astype(np.float32)

    f = {k: np.asarray(v) for k, v in inputs.items()}
    chan = lambda a: a.reshape(-1, P).T
    taps = lambda a: a.T.reshape(-1, P, 4).transpose(1, 0, 2).reshape(P, -1)
    blocks = lambda a: a.reshape(LRU_K, 2, HD, HD).transpose(1, 2, 0, 3).reshape(P, -1)
    row = lambda a: np.broadcast_to(a[None, :], (P, a.shape[0]))
    small = np.concatenate([
        taps(f["e_lru_conv_w"]), chan(f["e_lru_conv_b"]), chan(f["e_lru_ba"]), chan(f["e_lru_bx"]),
        chan(f["e_lru_lambda"]), blocks(f["e_lru_wa"]), blocks(f["e_lru_wx"]), taps(f["o_conv_w"]),
        chan(f["o_conv_b"]), row(f["o_dt_bias"]), row(f["o_a_log"]), row(f["o_d_skip"]),
        f["o_router"].reshape(DM // P, P, NE).transpose(1, 0, 2).reshape(P, -1)], axis=1)

    w = {name: dram(name, f[name]) for name in _WEIGHTS}
    x = dram("x", f["x"].reshape(SEQ, DM))
    p = dram("p", f["p"].reshape(2, SEQ, PLE))
    cst, sml = dram("const", const), dram("small", small)
    out = nc.dram_tensor("out_0_dram", (SEQ, DM), F32, kind="ExternalOutput").ap()
    build(nc, w, x, p, cst, sml, out)
    r = _run(nc, [arrays], core_ids=[0])
    return r.results[0]["out_0_dram"].reshape(1, SEQ, DM)
```

```python
from contextlib import ExitStack

import numpy as np

import concourse.bass as bass
from concourse import mybir

F32 = mybir.dt.float32
F32R = mybir.dt.float32r
I32 = mybir.dt.int32
U32 = mybir.dt.uint32
ALU = mybir.AluOpType
ACT = mybir.ActivationFunctionType
AX = mybir.AxisListType.X

P = 128
SEQ, DM, DFF = 256, 1024, 3584
NT = SEQ // P
HD, HEADS, KVH, IDXH = 64, 8, 2, 4
ROT = HD // 4 // 2
LRU = 512
LRU_K = LRU // P
PLE = 256
NSEL = 64
U_Q, U_K, U_V, U_QI, U_KI, U_WI, U_XG, U_XR, U_END = np.cumsum(
    [0, HEADS * HD, KVH * HD, KVH * HD, IDXH * HD, HD, IDXH, LRU, LRU]).tolist()
INNER, SH, GROUPS, STATE = 2048, 32, 4, 128
HPG = SH // GROUPS
Z0, X0, B0, C0, DT0, ODD_END = np.cumsum([0, INNER, INNER, GROUPS * STATE, GROUPS * STATE, SH]).tolist()
NE = 8
EPS = 1e-6
NEG = -1e30
REPLACED = -3e38

KS, WC = 4, 512
HK = 2
RAW, SPL = 6, 4
LAG = SPL - 1
FCH = DFF // WC
NEXP = 2 * 2 * FCH + 2 * FCH
NHALF = NEXP * KS // HK


class Chunk:

    def __init__(self, name, number, first, ksubs, width, evac, xbase=0):
        self.name, self.number, self.first, self.ksubs, self.width = name, number, first, ksubs, width
        self.evac, self.xbase = evac, xbase
        self.banks = 2 * (number % 2)
        self.panels = -(-ksubs // KS)
        self.last = first + self.panels - 1


def plan():
    panels, chunks = [], {}

    def chunk(name, weight, ksubs, col, width, evac):
        chunks[name] = Chunk(name, len(chunks), len(panels), ksubs, width, evac)
        for k in range(0, ksubs, KS):
            panels.append((weight, k, min(KS, ksubs - k), col, width))

    for name, a, b in (("kv_qi", U_K, U_KI), ("ki_wi", U_KI, U_XG), ("q", U_Q, U_K), ("xr", U_XR, U_END), ("xg", U_XG, U_XR)):
        chunk(name, "e_w_in", DM // P, a, b - a, "act")
    for h in range(2):
        chunk(f"e_out{h}", "e_w_out", DM // P, h * WC, WC, "dve")
    starts = {"ffn": len(panels)}
    panels.extend(ffn_panels("e_ffn_wg", "e_ffn_wu", "e_ffn_wd"))
    for h in range(2):
        chunk(f"e_emb{h}", "e_ple_proj", PLE // P, h * WC, WC, "act")
    for h in range(2):
        chunk(f"e_gate{h}", "e_ple_gate", DM // P, h * WC, WC, "act")
    chunk("dt", "o_w_in", DM // P, DT0, SH, "act")
    chunk("B", "o_w_in", DM // P, B0, WC, "act")
    chunk("C", "o_w_in", DM // P, C0, WC, "act")
    for j in range(INNER // WC):
        chunk(f"x{j}", "o_w_in", DM // P, X0 + j * WC, WC, "act")
    for j in range(INNER // WC):
        chunk(f"z{j}", "o_w_in", DM // P, Z0 + j * WC, WC, "act")
    for h in range(2):
        chunk(f"o_out{h}", "o_w_out", INNER // P, h * WC, WC, "dve")
    for h in range(2):
        chunk(f"o_emb{h}", "o_ple_proj", PLE // P, h * WC, WC, "act")
    starts["experts"] = len(panels)
    panels.extend([None] * (NE * NEXP))
    for h in range(2):
        chunk(f"o_gate{h}", "o_ple_gate", DM // P, h * WC, WC, "act")
    return panels, chunks, starts


def half_ends(panels):
    n, out = 0, []
    for panel in panels:
        n += -(-(panel[2] if panel else KS) // HK)
        out.append(n)
    return out


def ffn_order():
    steps = []
    for j in range(FCH):
        steps += [("g", j, 0), ("g", j, 1), ("u", j, 0), ("u", j, 1)]
        if j >= 2:
            steps += [("d", j - 2, 0), ("d", j - 2, 1)]
    for j in (FCH - 2, FCH - 1):
        steps += [("d", j, 0), ("d", j, 1)]
    return steps


def ffn_panels(wg, wu, wd):
    out = []
    for kind, j, half in ffn_order():
        if kind == "d":
            out.append((wd, KS * j, KS, half * WC, WC))
        else:
            out.append((wg if kind == "g" else wu, KS * half, KS, j * WC, WC))
    return out


FFN_AT = {step: n for n, step in enumerate(ffn_order())}

GROUP = {"e_mix": 0, "ple": 4, "o_attn": 6, "e_ffn": 8, "e_ple": 12, "o_mix": 16, "ssd": 20, "o_moe": 28, "o_ple": 32}

CONST = {}
SMALL = {}


def lay(table, *items):
    at = 0
    for name, n in items:
        table[name] = (at, at + n)
        at += n
    return at


CONST_N = lay(CONST, ("ident", P), ("cmask", P), ("tri", P), ("ones", P), ("iota", P), ("cos", NT * ROT),
              ("sin", NT * ROT), ("eps", 1))
SMALL_N = lay(SMALL, ("lru_w", LRU_K * 4), ("lru_b", LRU_K), ("lru_ba", LRU_K), ("lru_bx", LRU_K), ("lam", LRU_K),
              ("lru_wa", LRU_K * HD), ("lru_wx", LRU_K * HD), ("conv_w", 24 * 4), ("conv_b", 24), ("dt_bias", SH),
              ("a_log", SH), ("d_skip", SH), ("router", DM // P * NE))



class Place:

    def __init__(self, nc, at):
        self.nc, self.at = nc, at

    def __call__(self, name, shape, dt=F32):
        t = self.nc.alloc_sbuf_tensor_at(name, shape, dt, offset=self.at)
        self.at += -(-int(np.prod(shape[1:])) * 4 // 32) * 32
        return t


class FfnSems:

    def __init__(self, sem, name, raw_in, hi_done, lo_done, half_used):
        self.raw_in, self.hi_done, self.lo_done, self.half_used = raw_in, hi_done, lo_done, half_used
        self.silu = sem(name + "_silu")
        self.prod = sem(name + "_prod")
        self.aT_ps = sem(name + "_aT_ps")
        self.aT_hi = sem(name + "_aT_hi")
        self.aT_lo = sem(name + "_aT_lo")
        self.sel = sem(name + "_sel")
        self.xe_ps = sem(name + "_xe_ps")
        self.xe_hi = sem(name + "_xe_hi")
        self.xe_lo = sem(name + "_xe_lo")
        self.selT_ps = sem(name + "_selT_ps")
        self.selT_sb = sem(name + "_selT_sb")
        self.y_hi = sem(name + "_y_hi")
        self.y_lo = sem(name + "_y_lo")
        self.back_ps = sem(name + "_back_ps")
        self.summed = sem(name + "_summed")


def build(nc, w, x, p, const, small, out):
    panels, chunks, starts = plan()
    ends = half_ends(panels)
    halves = [(i, k) for i, panel in enumerate(panels) for k in range(0, panel[2] if panel else KS, HK)]
    ordered = sorted(chunks.values(), key=lambda c: c.number)

    place = Place(nc, 16512)
    cst = place("cst", [P, CONST_N])
    sml = place("sml", [P, SMALL_N])
    raw = place("raw", [P, RAW, KS, WC])
    whi = place("whi", [P, SPL, HK, WC], F32R)
    wlo = place("wlo", [P, SPL, HK, WC], F32R)
    h = place("h", [P, NT, DM])
    hn = place("hn", [P, NT, DM])
    xT_hi = place("xT_hi", [P, DM // P, SEQ], F32R)
    xT_lo = place("xT_lo", [P, DM // P, SEQ], F32R)
    gain = place("gain", [P, DM])
    pT_hi = place("pT_hi", [P, 2, PLE // P, SEQ], F32R)
    pT_lo = place("pT_lo", [P, 2, PLE // P, SEQ], F32R)
    ident_r = place("ident_r", [P, P], F32R)
    stat = place("stat", [P, 4, NT])
    warm = place("warm", [P, 8])
    flag = place("flag", [P, 8], I32)
    rt_hi = place("rt_hi", [P, DM // P, NE], F32R)
    rt_lo = place("rt_lo", [P, DM // P, NE], F32R)
    phase = place.at

    place = Place(nc, phase)
    u = place("u", [P, NT, U_END])
    gr = Place(nc, place.at)("gr", [P, LRU_K, SEQ])
    kdup = place("kdup", [P, NT, KVH + 1, 2, 2, HD])
    kqT = place("kqT", [P, 8, SEQ])
    qT = place("qT", [P, 4, SEQ])
    prT_at = place.at
    relu = place("relu", [P, IDXH, SEQ])
    prT = Place(nc, prT_at)("prT", [P, 8, P])
    wi2 = place("wi2", [P, NT, IDXH])
    score = place("score", [P, NT, SEQ])
    work = place("work", [P, SEQ])
    top8 = place("top8", [P, 8])
    keep = place("keep", [P, NT, SEQ])
    early = Place(nc, place.at)
    probs = place("probs", [P, 2, 4, SEQ])
    pin = early("pin", [P, 2 * NT, PLE])
    rot = early("rot", [P, 4, NT, 10, ROT])
    assert early.at <= place.at
    nmax = place("nmax", [P, 4, 4])
    rsum = place("rsum", [P, 4, 4])
    rinv = place("rinv", [P, 4, 4])
    xrT = place("xrT", [P, LRU_K, SEQ + 3])
    xgT = place("xgT", [P, LRU_K, SEQ])
    xc = place("xc", [P, LRU_K, SEQ])
    gi = place("gi", [P, LRU_K, SEQ])
    la = place("la", [P, LRU_K, SEQ])
    bd = place("bd", [P, 2, LRU_K, P])
    c8 = place("c8", [P, 8, LRU_K])
    assert place.at <= 229344, place.at

    place = Place(nc, phase)
    aT_hi = place("aT_hi", [P, 2, KS, SEQ], F32R)
    aT_lo = place("aT_lo", [P, 2, KS, SEQ], F32R)
    sg = place("sg", [P, 2, NT, WC])
    act = place("act", [P, 2, NT, WC])
    emb = place("emb", [P, NT, DM])
    y_hi = place("y_hi", [P, DM], F32R)
    y_lo = place("y_lo", [P, DM], F32R)
    hn_hi = place("hn_hi", [P, NT, DM], F32R)
    hn_lo = place("hn_lo", [P, NT, DM], F32R)
    sel = place("sel", [P, NT, P], F32R)
    selT = place("selT", [P, NT * P], F32R)
    lg = place("lg", [P, NT, NE])
    lmax = place("lmax", [P, NT, 8])
    lidx = place("lidx", [P, NT, 8], U32)
    lidf = place("lidf", [P, NT, 8])
    oh = place("oh", [P, 2, NT, NE])
    gw = place("gw", [P, 4, NT])
    gates = place("gates", [P, NT, NE])
    routed = place("routed", [P, NT, NE])
    slot = place("slot", [P, 2, NT, NE + 1])
    most = place("most", [P, 8])
    assert place.at <= 229344, place.at

    place = Place(nc, phase)
    xt = place("xt", [P, NT, INNER])
    yT = Place(nc, place.at)
    zt = place("zt", [P, NT, INNER])
    yT_hi = yT("yT_hi", [P, DM // P, SEQ], F32R)
    yT_lo = yT("yT_lo", [P, DM // P, SEQ], F32R)
    BT = place("BT", [P, GROUPS, SEQ])
    CT = place("CT", [P, GROUPS, SEQ])
    Btok = place("Btok", [P, GROUPS, STATE])
    late = Place(nc, place.at)
    pre = place("pre", [P, 2, KS, SEQ + 3])
    gn = late("gn", [P, INNER])
    late = Place(nc, place.at)
    cv = place("cv", [P, 2, KS, SEQ])
    segs = late("segs", [P, 2, HPG, P])
    cbm = place("cbm", [P, 2, P])
    xdt = place("xdt", [P, 2, WC])
    xtl = place("xtl", [P, WC])
    st = place("st", [P, WC])
    yt = place("yt", [P, WC])
    dts = place("dts", [P, 6, NT, SH])
    cum = place("cum", [P, 3, SH])
    dec = place("dec", [P, 2, SH])
    gss = place("gss", [P, 3, NT, GROUPS])
    assert place.at <= 229344, place.at

    def con(name):
        return cst[:, CONST[name][0]:CONST[name][1]]

    def par(name, **dims):
        v = sml[:, SMALL[name][0]:SMALL[name][1]]
        return v.rearrange("p (a b) -> p a b", **dims) if dims else v

    ident, cmask, tri, ones, iota, eps = (con(n) for n in ("ident", "cmask", "tri", "ones", "iota", "eps"))
    cos = con("cos").rearrange("p (t r) -> p t r", t=NT)
    sin = con("sin").rearrange("p (t r) -> p t r", t=NT)

    def tok(t):
        return slice(t * P, (t + 1) * P)

    ctx = ExitStack()
    with ctx:
        ps = ctx.enter_context(nc.psum_tensor("ps", [P, 8, 512], F32))

        def sem(name):
            return ctx.enter_context(nc.semaphore(name))

        const_in, small_in, x_in, p_in = sem("const_in"), sem("small_in"), sem("x_in"), sem("p_in")
        gain0_in, gain_in = sem("gain0_in"), sem("gain_in")
        gn_in, out_done = sem("gn_in"), sem("out_done")
        raw_in = [sem(f"raw_in{i}") for i in range(RAW)]
        hi_done = sem("hi_done")
        lo_done = sem("lo_done")
        half_used = sem("half_used")
        chunk_act, chunk_dve = sem("chunk_act"), sem("chunk_dve")
        act_seq, dve_seq = sem("act_seq"), sem("dve_seq")
        setup = sem("setup")
        rms = sem("rms")
        hg_ready = sem("hg_ready")
        rstd_ready = sem("rstd_ready")
        tp_ps, tp_hi, tp_lo = sem("tp_ps"), sem("tp_hi"), sem("tp_lo")
        roped = sem("roped")
        at_ps, at_sb = sem("at_ps"), sem("at_sb")
        lt_ps, lt_sb = sem("lt_ps"), sem("lt_sb")
        ix_ps, ix_relu = sem("ix_ps"), sem("ix_relu")
        conv_done = sem("conv_done")
        gate_ps, gate_sb = sem("gate_ps"), sem("gate_sb")
        lru_a, lru_b1, lru_bs, lru_gelu = sem("lru_a"), sem("lru_b1"), sem("lru_bs"), sem("lru_gelu")
        lru_y, lru_hi, lru_lo = sem("lru_y"), sem("lru_hi"), sem("lru_lo")
        lg_ps, lg_sb, pr_sb = sem("lg_ps"), sem("lg_sb"), sem("pr_sb")
        pt_ps, pt_sb = sem("pt_ps"), sem("pt_sb")
        o_ps, o_sb = sem("o_ps"), sem("o_sb")
        fw_ps, fw_sb = sem("fw_ps"), sem("fw_sb")
        cv_raw, cv_done = sem("cv_raw"), sem("cv_done")
        bk_ps, bk_sb = sem("bk_ps"), sem("bk_sb")
        dt_abs, dt_exp, dt_ln, dt_da = sem("dt_abs"), sem("dt_exp"), sem("dt_ln"), sem("dt_da")
        cum_ps, cum_sb, cum_exp = sem("cum_ps"), sem("cum_sb"), sem("cum_exp")
        sg_ps, sg_sb, sg_exp = sem("sg_ps"), sem("sg_sb"), sem("sg_exp")
        m_done, y_ps, y_sb, st_sb = sem("m_done"), sem("y_ps"), sem("y_sb"), sem("st_sb")
        gss_done, grms = sem("gss_done"), sem("grms")
        yn_ready = sem("yn_ready")
        rt_done, rt_ps, lw_max, lw_exp = sem("rt_done"), sem("rt_ps"), sem("lw_max"), sem("lw_exp")
        routed_sb, slot_ps, flag_set, hn_split = sem("routed_sb"), sem("slot_ps"), sem("flag_set"), sem("hn_split")
        gate_ple = sem("gate_ple")
        ffn_sum = sem("ffn_sum")
        fin = sem("fin")
        dense = FfnSems(sem, "ffn", raw_in, hi_done, lo_done, half_used)
        main = FfnSems(sem, "exp", raw_in, hi_done, lo_done, half_used)
        rest = FfnSems(sem, "rest", [sem(f"rest_in{i}") for i in range(RAW)], sem("rest_hi"), sem("rest_lo"),
                       sem("rest_used"))

        def evacuated(number):
            c = ordered[number]
            return (chunk_act if c.evac == "act" else chunk_dve,
                    sum(o.evac == c.evac for o in ordered[:number + 1]))

        def panel_dram(name, k, n, col, width, e=None):
            src = w[name]
            if e is not None:
                src = src[bass.ds(e, 1) if not isinstance(e, int) else slice(e, e + 1), k * P:(k + n) * P, col:col + width].rearrange("a k c -> (a k) c")
            else:
                src = src[k * P:(k + n) * P, col:col + width]
            return src.rearrange("(k p) c -> p k c", p=P)

        block = ctx.enter_context(nc.Block())

        @block.sync
        def _(sp):
            def load(i, panel):
                if i >= RAW:
                    sp.wait_ge(hi_done, ends[i - RAW])
                    sp.wait_ge(lo_done, ends[i - RAW])
                name, k, n, col, width = panel
                sp.dma_start(raw[:, i % RAW, 0:n, 0:width], panel_dram(*panel)).then_inc(raw_in[i % RAW], 16)

            sp.dma_start(h[:, :, :], x.rearrange("(t p) d -> p t d", p=P)).then_inc(x_in, 16)
            for i in range(starts["experts"]):
                load(i, panels[i])

            order = ffn_panels("o_exp_wg", "o_exp_wu", "o_exp_wd")
            base = starts["experts"]
            with sp.Fori(0, NE) as e:
                for n, panel in enumerate(order):
                    i = base + n
                    sp.wait_ge(hi_done, e * NHALF + ends[i - RAW])
                    sp.wait_ge(lo_done, e * NHALF + ends[i - RAW])
                    sp.dma_start(raw[:, i % RAW, :, :], panel_dram(*panel, e=e)).then_inc(raw_in[i % RAW], 16)
            sp.wait_ge(flag_set, 1)
            some = sp.value_load(flag[0:1, 0:1], min_val=0, max_val=1)
            with sp.If(some != 0):
                sp.wait_ge(hi_done, ends[base + NE * NEXP - 1])
                sp.wait_ge(lo_done, ends[base + NE * NEXP - 1])
                for n in range(NEXP):
                    if n >= RAW:
                        sp.wait_ge(rest.hi_done, 2 * (n - RAW + 1))
                        sp.wait_ge(rest.lo_done, 2 * (n - RAW + 1))
                    sp.dma_start(raw[:, n % RAW, :, :], panel_dram(*order[n], e=0)).then_inc(rest.raw_in[n % RAW], 16)
                with sp.Fori(1, NE) as e:
                    for n in range(NEXP):
                        sp.wait_ge(rest.hi_done, e * NHALF + 2 * (n - RAW + 1))
                        sp.wait_ge(rest.lo_done, e * NHALF + 2 * (n - RAW + 1))
                        sp.dma_start(raw[:, n % RAW, :, :], panel_dram(*order[n], e=e)).then_inc(
                            rest.raw_in[n % RAW], 16)
                sp.wait_ge(rest.hi_done, NE * NHALF)
                sp.wait_ge(rest.lo_done, NE * NHALF)
            for i in range(base + NE * NEXP, len(panels)):
                load(i, panels[i])
            sp.wait_ge(fin, 1)
            sp.dma_start(out.rearrange("(t p) d -> p t d", p=P), hn[:, :, :]).then_inc(out_done, 16)
            sp.wait_ge(out_done, 16)

        @block.gpsimd
        def _(pool):
            for n, name in enumerate(("e_ffn_norm", "e_ple_gate_norm", "o_mix_norm", "o_moe_norm", "o_ple_gate_norm",
                                      "final_norm")):
                pool.wait_ge(hg_ready, NT * (n + 1))
                pool.dma_start(gain[:, :], w[name].partition_broadcast(P)).then_inc(gain_in, 16)
                if name == "o_mix_norm":
                    pool.wait_ge(cv_raw, 6)
                    pool.dma_start(gn[:, :], w["o_gnorm"].partition_broadcast(P)).then_inc(gn_in, 16)

        @block.scalar
        def _(a):
            sent = [0]
            steps = [0]

            def step(ins):
                steps[0] += 1
                ins.then_inc(act_seq, 1)
                a.wait_ge(act_seq, steps[0])

            def splits(upto):
                while sent[0] < min(upto, len(halves)) and panels[halves[sent[0]][0]] is not None:
                    q = sent[0]
                    i, k = halves[q]
                    n, width = min(HK, panels[i][2] - k), panels[i][4]
                    a.wait_ge(raw_in[i % RAW], 16 * (i // RAW + 1))
                    if q >= SPL:
                        a.wait_ge(half_used, q - SPL + 1)
                    a.activation(whi[:, q % SPL, 0:n, 0:width], raw[:, i % RAW, k:k + n, 0:width], ACT.Copy).then_inc(
                        hi_done, 1)
                    sent[0] += 1

            def taken(name):
                c = chunks[name]
                splits(ends[c.last] + LAG)
                a.wait_ge(half_used, ends[c.last])
                return ps[:, c.banks:c.banks + 2, 0:c.width]

            def norm(n, scratch, then=None):
                a.activation(warm[:, 0:1], eps, ACT.Sqrt)
                summed = {0: (x_in, 16), 1: (chunk_dve, 2), 2: (dense.summed, 1), 3: (gate_ple, 1), 4: (chunk_dve, 4),
                          5: (gate_ple, 2), 6: (gate_ple, 3)}
                a.wait_ge(*summed[n])
                for t in range(NT):
                    step(a.activation(scratch, h[:, t, :], ACT.Square, accum_out=stat[:, 0, t:t + 1]))
                a.activation(stat[:, 1, :], stat[:, 0, :], ACT.Sqrt, scale=1.0 / DM, bias=eps).then_inc(rms, 1)
                if then:
                    a.activation(warm[:, 1:2], eps, then)

            def normed(dst, src, func, n):
                a.wait_ge(rstd_ready, n + 1)
                for t in range(NT):
                    ins = a.activation(dst[:, t], src[:, t], func, scale=stat[:, 2, t:t + 1])
                return ins

            def turn_hi(first, count=4, to=None, free=None):
                if free:
                    a.wait_ge(half_used, free)
                for n in range(count):
                    g = first + n
                    a.wait_ge(tp_ps, g + 1)
                    dst = to(n) if to else xT_hi[:, 4 * (n % 2):4 * (n % 2) + 4, tok(n // 2)]
                    a.activation(dst, ps[:, 4 + g % 4, :].rearrange("p (k c) -> p k c", k=4), ACT.Copy).then_inc(
                        tp_hi, 1)

            a.dma_start(cst[:, :], const).then_inc(const_in, 16)
            a.dma_start(gain[:, :], w["e_mix_norm"].partition_broadcast(P)).then_inc(gain0_in, 16)
            a.dma_start(pin[:, :, :], p.rearrange("l (t p) d -> p (l t) d", p=P)).then_inc(p_in, 16)
            a.dma_start(sml[:, :], small).then_inc(small_in, 16)
            splits(1)
            a.wait_ge(const_in, 16)
            norm(0, scratch=u[:, 0, 0:DM])
            turn_hi(GROUP["e_mix"])
            splits(SPL)
            for i in range(2):
                a.wait_ge(tp_ps, GROUP["ple"] + i + 1)
                a.activation(pT_hi[:, i].rearrange("p k (t c) -> p t k c", t=NT),
                             ps[:, 4 + i, :].rearrange("p (t k c) -> p t k c", t=NT, k=PLE // P), ACT.Copy).then_inc(tp_hi, 1)
            a.wait_ge(small_in, 16)
            a.activation(rt_hi[:, :, :], par("router", a=DM // P), ACT.Copy).then_inc(rt_done, 1)
            for name in ("kv_qi", "ki_wi", "q", "xr", "xg"):
                b = {"kv_qi": U_K, "ki_wi": U_KI, "q": U_Q, "xr": U_XR, "xg": U_XG}[name]
                normed(u[:, :, b:b + chunks[name].width], taken(name), ACT.Copy, 0).then_inc(chunk_act, 1)
            splits(ends[chunks["xg"].last] + LAG)
            a.wait_ge(setup, 2)
            a.activation(c8[:, 1, :], c8[:, 0, :], ACT.Exp, scale=-1.0).then_inc(setup, 1)
            a.wait_ge(setup, 4)
            a.activation(c8[:, 3, :], c8[:, 2, :], ACT.Ln).then_inc(setup, 1)
            for n, dst in enumerate((kqT[:, 0:4, tok(0)], kqT[:, 0:4, tok(1)], kqT[:, 4:8, tok(0)], kqT[:, 4:8, tok(1)],
                                     qT[:, :, tok(0)], qT[:, :, tok(1)])):
                a.wait_ge(at_ps, n + 1)
                a.activation(dst, ps[:, (n + 4) % 8, :].rearrange("p (k c) -> p k c", k=4), ACT.Copy).then_inc(at_sb, 1)
            a.wait_ge(setup, 6)
            for n in range(4):
                a.wait_ge(lt_ps, n + 1)
                dst = xrT[:, :, 3 + n * P:3 + (n + 1) * P] if n < 2 else xgT[:, :, tok(n - 2)]
                a.activation(dst, ps[:, n + 2, :].rearrange("p (k c) -> p k c", k=4), ACT.Copy).then_inc(lt_sb, 1)
            for t in range(NT):
                if t:
                    a.wait_ge(ix_relu, t + 1)
                a.wait_ge(ix_ps, t + 1)
                keys = (t + 1) * P
                src = ps[:, 6, :].rearrange("p (h k) -> p h k", h=4) if t == 0 else \
                    ps[:, 0:2, :].rearrange("p b (h k) -> p (b h) k", h=2)
                a.activation(relu[:, :, 0:keys], src, ACT.Relu, scale=HD ** -0.5).then_inc(ix_relu, 1)
            for n, (dst, bias) in enumerate(((gr, par("lru_ba")), (gi, par("lru_bx")))):
                a.wait_ge(gate_ps, n + 1)
                for k in range(LRU_K):
                    ins = a.activation(dst[:, k, :], ps[:, 2 + 2 * n + k // 2, (k % 2) * SEQ:(k % 2 + 1) * SEQ], ACT.Sigmoid,
                                       bias=bias[:, k:k + 1])
                ins.then_inc(gate_sb, 1)
            a.wait_ge(gate_sb, 2)
            a.wait_ge(setup, 7)
            for k in range(LRU_K):
                ins = a.activation(la[:, k, :], gr[:, k, :], ACT.Exp, scale=c8[:, 6, k:k + 1])
            ins.then_inc(lru_a, 1)
            a.wait_ge(lru_a, 1)
            for k in range(LRU_K):
                ins = a.activation(gr[:, k, :], gr[:, k, :], ACT.Tanh, scale=c8[:, 7, k:k + 1])
            ins.then_inc(lru_a, 1)
            a.activation(xgT[:, :, :], xgT[:, :, :], ACT.Gelu_apprx_tanh).then_inc(lru_gelu, 1)
            a.wait_ge(lru_b1, 1)
            a.activation(gr[:, :, :], gr[:, :, :], ACT.Sqrt).then_inc(lru_bs, 1)
            a.wait_ge(lru_y, 1)
            a.wait_ge(half_used, ends[chunks["xg"].last])
            a.activation(xT_hi[:, 4:8, :], la[:, :, :], ACT.Copy).then_inc(lru_hi, 1)

            def exps(s):
                a.wait_ge(lg_sb, s + 1)
                keys = (s // 2 + 1) * P
                for j in range(4):
                    ins = a.activation(probs[:, s % 2, j, 0:keys], probs[:, s % 2, j, 0:keys], ACT.Exp,
                                       bias=nmax[:, s, j:j + 1], accum_out=rsum[:, s, j:j + 1])
                ins.then_inc(pr_sb, 1)

            def turned_probs(s):
                a.wait_ge(pt_ps, s + 1)
                n = 4 * (s // 2 + 1)
                if s == 0:
                    src = ps[:, 2, :]
                elif s == 1:
                    src = ps[:, 3, :]
                else:
                    src = ps[:, 2:4, :].rearrange("p b c -> p (b c)")
                if s:
                    a.wait_ge(o_ps, s)
                a.activation(prT[:, 0:n, :], src.rearrange("p (k c) -> p k c", k=n), ACT.Copy).then_inc(pt_sb, 1)

            exps(0)
            exps(1)
            turned_probs(0)
            exps(2)
            turned_probs(1)
            exps(3)
            turned_probs(2)
            turned_probs(3)
            turn_hi(GROUP["o_attn"], 2, to=lambda t: xT_hi[:, 0:4, tok(t)])
            splits(ends[chunks["e_out1"].last] + LAG)

            def silu(s, nt, used, count, j):
                a.wait_ge(s.half_used, used)
                if j >= 2:
                    a.wait_ge(s.prod, count + (j - 1))
                if nt == NT:
                    normed(sg[:, j % 2], ps[:, 0:nt, :], ACT.Silu, 1).then_inc(s.silu, 1)
                else:
                    a.activation(sg[:, j % 2, 0:nt, :], ps[:, 0:nt, :], ACT.Silu).then_inc(s.silu, 1)

            def aT_part_hi(s, nt, count, j):
                a.wait_ge(s.aT_ps, count + (j + 1))
                bank = 0 if nt == 2 else 4 + j % 2
                dst = aT_hi[:, j % 2, :, 0:nt * P].rearrange("p k (t c) -> p t k c", t=nt)
                a.activation(dst, ps[:, bank:bank + nt, :].rearrange("p t (k c) -> p t k c", k=4),
                             ACT.Copy).then_inc(s.aT_hi, 1)

            norm(1, u[:, 0, 0:DM], ACT.Silu)
            turn_hi(GROUP["e_ffn"], free=ends[chunks["e_out1"].last])
            base = starts["ffn"]
            for j in range(FCH):
                g1 = base + FFN_AT["g", j, 1]
                splits(ends[g1] + LAG)
                silu(dense, NT, ends[g1], 0, j)
                if j:
                    splits(ends[base + FFN_AT["u", j, 1]] + LAG)
                    aT_part_hi(dense, NT, 0, j - 1)
            splits(ends[base + FFN_AT["d", FCH - 2, 1]] + LAG)
            aT_part_hi(dense, NT, 0, FCH - 1)
            splits(ends[base + NEXP - 1] + LAG)

            def embed(layer):
                for half in range(2):
                    src = taken(f"{layer}_emb{half}")
                    a.activation(emb[:, :, half * WC:(half + 1) * WC], src, ACT.Copy).then_inc(chunk_act, 1)

            def embed_gate(layer, n, free):
                norm(n, act[:, :, :, :].rearrange("p a t n -> p (a t n)")[:, 0:DM], ACT.Sigmoid)
                turn_hi(GROUP[f"{layer}_ple"], free=free)
                for half in range(2):
                    normed(sg[:, half], taken(f"{layer}_gate{half}"), ACT.Sigmoid, n).then_inc(chunk_act, 1)

            embed("e")
            embed_gate("e", 2, ends[base + NEXP - 1])

            norm(3, xt[:, 0, 0:DM], ACT.Exp)
            turn_hi(GROUP["o_mix"], free=ends[chunks["e_gate1"].last])
            normed(dts[:, 0], taken("dt"), ACT.Copy, 3).then_inc(chunk_act, 1)
            a.wait_ge(dt_abs, 1)
            a.activation(dts[:, 2, :, :], dts[:, 1, :, :], ACT.Exp, scale=-1.0).then_inc(dt_exp, 1)
            a.activation(dts[:, 5, 0, :], par("a_log"), ACT.Exp).then_inc(dt_exp, 1)
            a.wait_ge(dt_ln, 1)
            a.activation(dts[:, 3, :, :], dts[:, 1, :, :], ACT.Ln).then_inc(dt_ln, 1)

            def stage_in(q, name):
                src = taken(name)
                if q >= 2:
                    a.wait_ge(fw_ps, q - 1)
                normed(hn[:, :, (q % 2) * WC:(q % 2 + 1) * WC], src, ACT.Copy, 3).then_inc(chunk_act, 1)

            def forward_out(q):
                a.wait_ge(fw_ps, q + 1)
                if q >= 2:
                    a.wait_ge(cv_raw, q - 1)
                dst = pre[:, q % 2, :, 3:3 + SEQ].rearrange("p k (t c) -> p t k c", t=NT)
                b = 4 + 2 * (q % 2)
                a.activation(dst, ps[:, b:b + 2, :].rearrange("p t (k c) -> p t k c", k=4), ACT.Copy).then_inc(fw_sb, 1)

            def conv_silu(q):
                a.wait_ge(cv_raw, q + 1)
                dst = BT if q == 0 else CT if q == 1 else cv[:, q % 2]
                dst = dst[:, :, :]
                a.activation(dst, cv[:, q % 2, :, :], ACT.Silu).then_inc(cv_done, 1)

            def backward_out(n):
                a.wait_ge(bk_ps, n + 1)
                if n == 0:
                    a.activation(Btok[:, :, :], ps[:, 4, :].rearrange("p (k c) -> p k c", k=4), ACT.Copy).then_inc(bk_sb, 1)
                else:
                    q = n + 1
                    b = 4 + 2 * (q % 2)
                    a.activation(xt[:, :, (n - 1) * WC:n * WC], ps[:, b:b + 2, :], ACT.Copy).then_inc(bk_sb, 1)

            a.wait_ge(setup, 6)
            a.wait_ge(dt_da, 1)
            a.wait_ge(tp_ps, GROUP["o_mix"] + 4)
            stage_in(0, "B")
            stage_in(1, "C")
            forward_out(0)
            stage_in(2, "x0")
            forward_out(1)
            conv_silu(0)
            backward_out(0)
            for q in range(3, 6):
                stage_in(q, f"x{q - 2}")
                forward_out(q - 1)
                conv_silu(q - 2)
                if q >= 4:
                    backward_out(q - 3)

            def z_silu(j):
                src = taken(f"z{j}")
                normed(zt[:, :, j * WC:(j + 1) * WC], src, ACT.Silu, 3).then_inc(chunk_act, 1)

            z_silu(0)
            forward_out(5)
            conv_silu(4)
            backward_out(3 - 0)
            z_silu(1)
            conv_silu(5)
            backward_out(4)
            z_silu(2)
            z_silu(3)
            splits(ends[chunks["z3"].last] + LAG)
            a.wait_ge(cum_sb, 2)
            a.activation(dec[:, 0, :], dec[:, 0, :], ACT.Exp).then_inc(cum_exp, 1)
            a.activation(dec[:, 1, :], cum[:, 1, :], ACT.Exp).then_inc(cum_exp, 1)
            for i in range(2 * GROUPS):
                a.wait_ge(sg_sb, i + 1)
                a.activation(segs[:, i % 2, :, :], segs[:, i % 2, :, :], ACT.Exp).then_inc(sg_exp, 1)
                if i:
                    if i % 2:
                        a.wait_ge(y_ps, i)
                        if i > 1:
                            a.wait_ge(y_ps, i - 1)
                        a.activation(st[:, :], ps[:, 7, :], ACT.Copy).then_inc(st_sb, 1)
            for i in range(2 * GROUPS):
                g, c = i // 2, i % 2
                a.wait_ge(y_sb, i + 1)
                ins = a.activation(hn[:, 0, 0:WC], xt[:, c, g * WC:(g + 1) * WC], ACT.Square, accum_out=gss[:, 0, c, g:g + 1])
                step(ins)
            a.activation(gss[:, 1, :, :], gss[:, 0, :, :], ACT.Sqrt, scale=1.0 / WC, bias=eps).then_inc(grms, 1)
            a.wait_ge(yn_ready, 2 * GROUPS)
            turn_hi(GROUP["ssd"], 8, free=ends[chunks["z3"].last],
                    to=lambda n: (xT_hi if n // 2 < 2 else yT_hi)[:, 4 * (n // 2 % 2):4 * (n // 2 % 2) + 4, tok(n % 2)])
            embed("o")

            norm(4, act[:, :, :, :].rearrange("p a t n -> p (a t n)")[:, 0:DM], ACT.Exp)
            turn_hi(GROUP["o_moe"], free=ends[starts["experts"] - 1])
            normed(hn_hi, hn, ACT.Copy, 4).then_inc(hn_split, 1)
            a.wait_ge(lw_max, 1)
            a.activation(gw[:, 1, :], gw[:, 0, :], ACT.Exp).then_inc(lw_exp, 1)

            def expert_splits(s, base, e):
                first = ends[base - 1] if base else 0
                done = [0]

                def ahead(upto):
                    while done[0] < min(upto, NHALF):
                        q = first + done[0]
                        i = base + done[0] // 2
                        k = HK * (done[0] % 2)
                        a.wait_ge(s.raw_in[i % RAW], (e * (NEXP // RAW) + (i // RAW + 1)) * 16)
                        if q >= SPL or not isinstance(e, int):
                            a.wait_ge(s.half_used, e * NHALF + (q - SPL + 1))
                        a.activation(whi[:, q % SPL, :, :], raw[:, i % RAW, k:k + HK, :], ACT.Copy).then_inc(s.hi_done, 1)
                        done[0] += 1
                return first, ahead

            def end(step_):
                return 2 * (FFN_AT[step_] + 1)

            def take_tokens_hi(s, count):
                a.wait_ge(s.xe_ps, count)
                a.activation(xT_hi[:, :, 0:P], ps[:, 6:8, :].rearrange("p b (k c) -> p (b k) c", k=4),
                             ACT.Copy).then_inc(s.xe_hi, 1)

            def result_hi(s, used, count):
                a.wait_ge(s.half_used, used)
                a.activation(y_hi[:, :], ps[:, 2:4, :].rearrange("p b c -> p (b c)"), ACT.Copy).then_inc(s.y_hi, 1)

            def expert(s, base, e, peeled):
                first, ahead = expert_splits(s, base, e)
                shift, count = e * NHALF + first, e * FCH
                ahead(SPL)
                if not peeled:
                    result_hi(s, shift, e)
                ahead(end(("g", 0, 1)) + LAG)
                silu(s, 1, shift + end(("g", 0, 1)), count, 0)
                ahead(end(("u", 0, 1)) + LAG)
                a.wait_ge(s.selT_ps, e + 1)
                a.activation(selT[:, :], ps[:, 5, 0:NT * P], ACT.Copy).then_inc(s.selT_sb, 1)
                for j in range(1, FCH):
                    ahead(end(("g", j, 1)) + LAG)
                    silu(s, 1, shift + end(("g", j, 1)), count, j)
                    ahead(end(("u", j, 1)) + LAG)
                    aT_part_hi(s, 1, count, j - 1)
                ahead(end(("d", FCH - 3, 1)) + LAG)
                take_tokens_hi(s, e + 2)
                ahead(end(("d", FCH - 2, 1)) + LAG)
                aT_part_hi(s, 1, count, FCH - 1)
                ahead(NHALF)

            def experts_act(s, base):
                first = ends[base - 1] if base else 0
                take_tokens_hi(s, 1)
                expert(s, base, 0, True)
                with a.Fori(1, NE) as e:
                    expert(s, base, e, False)
                result_hi(s, NE * NHALF + first, NE)

            experts_act(main, starts["experts"])
            a.wait_ge(flag_set, 1)
            some = a.value_load(flag[0:1, 0:1], min_val=0, max_val=1)
            with a.If(some != 0):
                experts_act(rest, 0)
            sent[0] = ends[starts["experts"] + NE * NEXP - 1]
            splits(ends[chunks["o_gate0"].first])
            embed_gate("o", 5, None)
            norm(6, act[:, :, :, :].rearrange("p a t n -> p (a t n)")[:, 0:DM])

        @block.vector
        def _(v):
            sent = [0]
            steps = [0]

            def step(ins):
                steps[0] += 1
                ins.then_inc(dve_seq, 1)
                v.wait_ge(dve_seq, steps[0])

            def splits(upto):
                while sent[0] < min(upto, len(halves)) and panels[halves[sent[0]][0]] is not None:
                    q = sent[0]
                    i, k = halves[q]
                    n, width = min(HK, panels[i][2] - k), panels[i][4]
                    v.wait_ge(hi_done, q + 1)
                    v.tensor_tensor(wlo[:, q % SPL, 0:n, 0:width], raw[:, i % RAW, k:k + n, 0:width],
                                    whi[:, q % SPL, 0:n, 0:width], ALU.subtract).then_inc(lo_done, 1)
                    sent[0] += 1

            def taken(name):
                c = chunks[name]
                splits(ends[c.last] + LAG)
                v.wait_ge(half_used, ends[c.last])
                return ps[:, c.banks:c.banks + 2, 0:c.width]

            def norm(n, used):
                v.wait_ge(*((gain_in, 16 * n) if n else (gain0_in, 16)))
                if used:
                    v.wait_ge(tp_ps, used)
                for t in range(NT):
                    v.tensor_tensor(hn[:, t, :], h[:, t, :], gain[:, :], ALU.mult).then_inc(hg_ready, 1)
                factor(n)

            def factor(n):
                v.wait_ge(rms, n + 1)
                v.reciprocal(stat[:, 2, :], stat[:, 1, :]).then_inc(rstd_ready, 1)

            def turn_lo(first, count=4, to=None, hi=None):
                for n in range(count):
                    g = first + n
                    v.wait_ge(tp_hi, g + 1)
                    at = (slice(None), slice(4 * (n % 2), 4 * (n % 2) + 4), tok(n // 2))
                    dst, high = to(n) if to else (xT_lo[at], xT_hi[at])
                    v.tensor_tensor(dst, ps[:, 4 + g % 4, :].rearrange("p (k c) -> p k c", k=4), high,
                                    ALU.subtract).then_inc(tp_lo, 1)

            v.wait_ge(x_in, 16)
            norm(0, 0)
            turn_lo(GROUP["e_mix"])
            splits(SPL)
            step(v.memset(xrT[:, :, 0:3], 0.0))
            step(v.memset(bd[:, :, :, :], 0.0))
            step(v.memset(kdup[:, :, :, :, :, :], 0.0))
            v.tensor_copy(ident_r[:, :], ident).then_inc(setup, 1)
            v.wait_ge(small_in, 16)
            for n, name in enumerate(("lru_wa", "lru_wx")):
                src = par(name, a=LRU_K)
                v.tensor_copy(bd[0:HD, n, :, 0:HD], src[0:HD])
                step(v.tensor_copy(bd[HD:P, n, :, HD:P], src[HD:P]))
            step(v.tensor_scalar(c8[:, 4, :], par("lam"), -1.0, None, ALU.mult))
            v.tensor_tensor(c8[:, 0, :], c8[:, 4, :], par("lam"), ALU.max).then_inc(setup, 1)
            for i in range(2):
                v.wait_ge(tp_hi, GROUP["ple"] + i + 1)
                v.tensor_tensor(pT_lo[:, i].rearrange("p k (t c) -> p t k c", t=NT),
                                ps[:, 4 + i, :].rearrange("p (t k c) -> p t k c", t=NT, k=PLE // P),
                                pT_hi[:, i].rearrange("p k (t c) -> p t k c", t=NT), ALU.subtract).then_inc(tp_lo, 1)
            v.wait_ge(rt_done, 1)
            v.tensor_tensor(rt_lo[:, :, :], par("router", a=DM // P), rt_hi[:, :, :], ALU.subtract).then_inc(rt_done, 1)
            splits(ends[chunks["q"].last] + LAG)

            v.wait_ge(chunk_act, 3)
            for base, nh in ((U_Q, HEADS + KVH), (U_QI, IDXH + 1)):
                head = u[:, :, base:base + nh * HD].rearrange("p t (h d) -> p t h d", h=nh)
                for t in range(NT):
                    x1, x2 = head[:, t, :, 0:ROT], head[:, t, :, ROT:2 * ROT]
                    r = [rot[:, i, t, 0:nh, :] for i in range(4)]
                    c = cos[:, t, :].unsqueeze(1).to_broadcast([P, nh, ROT])
                    s = sin[:, t, :].unsqueeze(1).to_broadcast([P, nh, ROT])
                    v.tensor_tensor(r[0], x1, c, ALU.mult)
                    v.tensor_tensor(r[1], x2, s, ALU.mult)
                    v.tensor_tensor(r[2], x1, s, ALU.mult)
                    step(v.tensor_tensor(r[3], x2, c, ALU.mult))
                    v.tensor_tensor(x1, r[0], r[1], ALU.subtract)
                    step(v.tensor_tensor(x2, r[2], r[3], ALU.add))
            for t in range(NT):
                for r in range(2):
                    v.tensor_copy(kdup[:, t, 0:KVH, r, r, :], u[:, t, U_K:U_V].rearrange("p (g d) -> p g d", g=KVH))
                    ins = v.tensor_copy(kdup[:, t, KVH, r, r, :], u[:, t, U_KI:U_WI])
            ins.then_inc(roped, 1)
            step(v.tensor_scalar(wi2[:, :, :], u[:, :, U_WI:U_XG], IDXH ** -0.5, None, ALU.mult))
            splits(ends[chunks["xg"].last] + LAG)

            v.wait_ge(setup, 3)
            v.tensor_scalar(c8[:, 2, :], c8[:, 1, :], 1.0, None, ALU.add).then_inc(setup, 1)
            v.wait_ge(setup, 5)
            step(v.tensor_scalar(c8[:, 5, :], c8[:, 2, :], -1.0, 1e-30, ALU.add, ALU.max))
            step(v.tensor_scalar(c8[:, 6, :], c8[:, 2, :], 1.0, None, ALU.is_equal))
            step(v.reciprocal(c8[:, 5, :], c8[:, 5, :]))
            step(v.tensor_tensor(c8[:, 3, :], c8[:, 3, :], c8[:, 1, :], ALU.mult))
            step(v.tensor_tensor(c8[:, 3, :], c8[:, 3, :], c8[:, 5, :], ALU.mult))
            step(v.tensor_tensor(c8[:, 6, :], c8[:, 6, :], c8[:, 1, :], ALU.mult))
            step(v.tensor_tensor(c8[:, 3, :], c8[:, 3, :], c8[:, 6, :], ALU.add))
            step(v.tensor_scalar(c8[:, 4, :], c8[:, 4, :], 0.0, None, ALU.max))
            step(v.tensor_tensor(c8[:, 3, :], c8[:, 3, :], c8[:, 4, :], ALU.add))
            v.memset(dts[:, 4, 0, 0:1], 0.0).then_inc(setup, 1)
            step(v.tensor_scalar(c8[:, 6, :], c8[:, 3, :], -8.0, None, ALU.mult))
            v.tensor_scalar(c8[:, 7, :], c8[:, 3, :], 8.0, None, ALU.mult).then_inc(setup, 1)

            v.wait_ge(lt_sb, 2)
            cw = par("lru_w", a=LRU_K)
            for k in range(LRU_K):
                step(v.tensor_scalar(xc[:, k, :], xrT[:, k, 3:3 + SEQ], cw[:, k, 3:4], par("lru_b")[:, k:k + 1], ALU.mult,
                                     ALU.add))
                for j in range(3):
                    ins = v.scalar_tensor_tensor(xc[:, k, :], xrT[:, k, j:j + SEQ], cw[:, k, j:j + 1], xc[:, k, :],
                                                 ALU.mult, ALU.add)
                    if j < 2:
                        step(ins)
            ins.then_inc(conv_done, 1)

            for t in range(NT):
                keys = (t + 1) * P
                v.wait_ge(ix_relu, 2 * t + 1)
                step(v.tensor_scalar(score[:, t, 0:keys], relu[:, 0, 0:keys], wi2[:, t, 0:1], None, ALU.mult))
                for j in range(1, IDXH):
                    ins = v.scalar_tensor_tensor(score[:, t, 0:keys], relu[:, j, 0:keys], wi2[:, t, j:j + 1],
                                                 score[:, t, 0:keys], ALU.mult, ALU.add)
                    if j < IDXH - 1:
                        step(ins)
                if t == 0:
                    ins.then_inc(ix_relu, 1)
                    v.wait_ge(ix_relu, 2)
                else:
                    step(ins)
                step(v.tensor_tensor(score[:, t, t * P:keys], score[:, t, t * P:keys], cmask, ALU.add))
                cur = score[:, t, 0:keys]
                for n in range(NSEL // 8):
                    step(v.max(top8[:, :], cur))
                    step(v.match_replace(work[:, 0:keys], top8[:, :], cur, REPLACED))
                    cur = work[:, 0:keys]
                step(v.tensor_tensor(keep[:, t, 0:keys], cur, score[:, t, 0:keys], ALU.is_equal))
                step(v.tensor_scalar(keep[:, t, 0:keys], keep[:, t, 0:keys], NEG, None, ALU.mult))
                step(v.tensor_tensor(keep[:, t, t * P:keys], keep[:, t, t * P:keys], cmask, ALU.add))

            v.wait_ge(lru_a, 2)
            v.wait_ge(gate_ps, 2)
            aa = xrT[:, :, 0:SEQ]
            step(v.tensor_tensor(aa, la[:, :, :], la[:, :, :], ALU.mult))
            v.scalar_tensor_tensor(gr[:, :, :], aa, 1.0, gr[:, :, :], ALU.add, ALU.mult).then_inc(lru_b1, 1)
            step(v.tensor_tensor(gi[:, :, :], gi[:, :, :], xc[:, :, :], ALU.mult))
            v.wait_ge(lru_bs, 1)
            step(v.tensor_tensor(gi[:, :, :], gi[:, :, :], gr[:, :, :], ALU.mult))
            for k in range(LRU_K):
                ins = v.tensor_tensor_scan(aa[:, k, :], la[:, k, :], gi[:, k, :], 0.0, ALU.mult, ALU.add)
            step(ins)
            v.wait_ge(lru_gelu, 1)
            v.tensor_tensor(la[:, :, :], aa, xgT[:, :, :], ALU.mult).then_inc(lru_y, 1)
            v.wait_ge(lru_y, 1)
            v.wait_ge(lru_hi, 1)
            v.tensor_tensor(xT_lo[:, 4:8, :], la[:, :, :], xT_hi[:, 4:8, :], ALU.subtract).then_inc(lru_lo, 1)

            def masked(s):
                t, keys = s // 2, (s // 2 + 1) * P
                v.wait_ge(lg_ps, s + 1)
                if s >= 2:
                    v.wait_ge(pt_ps, s - 1)
                src = (ps[:, 6, :], ps[:, 7, :], ps[:, 0:2, :], ps[:, 6:8, :])[s]
                src = src.rearrange("p (h k) -> p h k", h=4) if t == 0 else src.rearrange("p b (h k) -> p (b h) k", h=2)
                dst = probs[:, s % 2, :, 0:keys]
                step(v.scalar_tensor_tensor(dst, src, HD ** -0.5, keep[:, t, 0:keys].unsqueeze(1).to_broadcast([P, 4, keys]),
                                            ALU.mult, ALU.add))
                v.tensor_reduce(nmax[:, s, :], dst, AX, ALU.max, negate=True).then_inc(lg_sb, 1)

            def attended(t):
                v.wait_ge(pr_sb, 2 * t + 2)
                v.wait_ge(o_ps, 2 * t + 2)
                step(v.reciprocal(rinv[:, 2 * t:2 * t + 2, :], rsum[:, 2 * t:2 * t + 2, :]))
                r = rinv[:, 2 * t:2 * t + 2, :].rearrange("p a b -> p (a b)").unsqueeze(2).to_broadcast([P, HEADS, HD])
                v.tensor_tensor(hn[:, t, 0:HEADS * HD].rearrange("p (h d) -> p h d", h=HEADS),
                                ps[:, 4 + t, :].rearrange("p (h d) -> p h d", h=HEADS), r, ALU.mult).then_inc(o_sb, 1)

            masked(0)
            masked(1)
            masked(2)
            masked(3)
            attended(0)
            attended(1)
            turn_lo(GROUP["o_attn"], 2, to=lambda t: (xT_lo[:, 0:4, tok(t)], xT_hi[:, 0:4, tok(t)]))

            def add_out(name, half):
                src = taken(name)
                dst = h[:, :, half * WC:(half + 1) * WC]
                v.tensor_tensor(dst, dst, src, ALU.add).then_inc(chunk_dve, 1)

            add_out("e_out0", 0)
            add_out("e_out1", 1)

            def prod(s, nt, count_used, count, j):
                v.wait_ge(s.half_used, count_used)
                v.wait_ge(s.silu, count + 1)
                ub = 2 if nt == 2 else 1
                if nt == NT:
                    for t in range(NT):
                        ins = v.scalar_tensor_tensor(act[:, j % 2, t, :], ps[:, ub + t, :], stat[:, 2, t:t + 1],
                                                     sg[:, j % 2, t, :], ALU.mult, ALU.mult)
                    ins.then_inc(s.prod, 1)
                else:
                    v.tensor_tensor(act[:, j % 2, 0:nt, :], sg[:, j % 2, 0:nt, :], ps[:, ub:ub + nt, :],
                                    ALU.mult).then_inc(s.prod, 1)

            def aT_part_lo(s, nt, count, j):
                v.wait_ge(s.aT_hi, count + 1)
                bank = 0 if nt == 2 else 4 + j % 2
                view = [b[:, j % 2, :, 0:nt * P].rearrange("p k (t c) -> p t k c", t=nt) for b in (aT_lo, aT_hi)]
                v.tensor_tensor(view[0], ps[:, bank:bank + nt, :].rearrange("p t (k c) -> p t k c", k=4), view[1],
                                ALU.subtract).then_inc(s.aT_lo, 1)

            v.wait_ge(chunk_dve, 2)
            norm(1, GROUP["o_attn"] + 2)
            turn_lo(GROUP["e_ffn"])
            base = starts["ffn"]
            for j in range(FCH):
                u1 = base + FFN_AT["u", j, 1]
                splits(ends[u1] + LAG)
                if j >= 2:
                    v.wait_ge(dense.aT_ps, j - 1)
                prod(dense, NT, ends[u1], j, j)
                if j:
                    aT_part_lo(dense, NT, j - 1, j - 1)
            splits(ends[base + FFN_AT["d", FCH - 2, 1]] + LAG)
            aT_part_lo(dense, NT, FCH - 1, FCH - 1)
            splits(ends[base + NEXP - 1] + LAG)
            v.wait_ge(half_used, ends[base + NEXP - 1])
            for t in range(NT):
                ins = v.tensor_tensor(h[:, t, :], h[:, t, :], ps[:, 4 + 2 * t:6 + 2 * t, :].rearrange("p b c -> p (b c)"),
                                      ALU.add)
            ins.then_inc(dense.summed, 1)

            def ple(layer, n, used):
                norm(n, used)
                turn_lo(GROUP[f"{layer}_ple"])
                for half in range(2):
                    c = chunks[f"{layer}_gate{half}"]
                    splits(ends[c.last] + LAG)
                    v.wait_ge(*evacuated(c.number))
                    cols = slice(half * WC, (half + 1) * WC)
                    step(v.tensor_tensor(emb[:, :, cols], emb[:, :, cols], sg[:, half, :, :], ALU.mult))
                    ins = v.tensor_tensor(h[:, :, cols], h[:, :, cols], emb[:, :, cols], ALU.add)
                    if half == 0:
                        step(ins)
                ins.then_inc(gate_ple, 1)

            splits(ends[chunks["e_emb1"].last] + LAG)
            v.wait_ge(dense.summed, 1)
            ple("e", 2, GROUP["e_ffn"] + 4)

            v.wait_ge(gate_ple, 1)
            norm(3, GROUP["e_ple"] + 4)
            turn_lo(GROUP["o_mix"])
            c = chunks["dt"]
            splits(ends[c.last] + LAG)
            v.memset(pre[:, :, :, 0:3], 0.0)
            v.wait_ge(*evacuated(c.number))
            raw_dt, d1, d2, d3, d4, d5 = (dts[:, i, :, :] for i in range(6))
            step(v.tensor_tensor(raw_dt, raw_dt, par("dt_bias").unsqueeze(1).to_broadcast([P, NT, SH]), ALU.add))
            step(v.tensor_scalar(d3, raw_dt, -1.0, None, ALU.mult))
            v.tensor_tensor(d1, raw_dt, d3, ALU.max).then_inc(dt_abs, 1)
            v.wait_ge(dt_abs, 1)
            v.wait_ge(dt_exp, 1)
            v.tensor_scalar(d1, d2, 1.0, None, ALU.add).then_inc(dt_ln, 1)
            v.wait_ge(dt_ln, 2)
            step(v.tensor_scalar(d4, d1, -1.0, 1e-30, ALU.add, ALU.max))
            step(v.reciprocal(d4, d4))
            step(v.tensor_tensor(d3, d3, d2, ALU.mult))
            step(v.tensor_tensor(d3, d3, d4, ALU.mult))
            step(v.tensor_scalar(d4, d1, 1.0, None, ALU.is_equal))
            step(v.tensor_tensor(d4, d4, d2, ALU.mult))
            step(v.tensor_tensor(d3, d3, d4, ALU.add))
            step(v.tensor_scalar(raw_dt, raw_dt, 0.0, None, ALU.max))
            step(v.tensor_tensor(raw_dt, raw_dt, d3, ALU.add))
            v.wait_ge(dt_exp, 2)
            step(v.tensor_scalar(dts[:, 5, 0, :], dts[:, 5, 0, :], -1.0, None, ALU.mult))
            v.tensor_tensor(d1, raw_dt, dts[:, 5, 0, :].unsqueeze(1).to_broadcast([P, NT, SH]), ALU.mult).then_inc(dt_da, 1)

            def convolve(q):
                v.wait_ge(fw_sb, q + 1)
                if q >= 2:
                    if q < 4:
                        v.wait_ge(cv_done, q - 1)
                    else:
                        v.wait_ge(bk_ps, q - 2)
                k0 = {0: 16, 1: 20}.get(q, 4 * (q - 2))
                cw_ = par("conv_w", a=24)
                for k in range(4):
                    dst = cv[:, q % 2, k, :]
                    step(v.tensor_scalar(dst, pre[:, q % 2, k, 3:3 + SEQ], cw_[:, k0 + k, 3:4],
                                         par("conv_b")[:, k0 + k:k0 + k + 1], ALU.mult, ALU.add))
                    for j in range(3):
                        ins = v.scalar_tensor_tensor(dst, pre[:, q % 2, k, j:j + SEQ], cw_[:, k0 + k, j:j + 1], dst,
                                                     ALU.mult, ALU.add)
                        if j < 2:
                            step(ins)
                ins.then_inc(cv_raw, 1)

            splits(ends[chunks["x0"].last])
            convolve(0)
            for q in range(1, 6):
                name = f"x{q}" if q < 4 else f"z{q - 4}"
                splits(ends[chunks[name].last])
                convolve(q)
            splits(ends[chunks["z3"].last] + LAG)

            v.wait_ge(cum_ps, 1)
            v.tensor_copy(cum[:, :, :], ps[:, 6, 0:3 * SH].rearrange("p (a b) -> p a b", a=3)).then_inc(cum_sb, 1)
            v.wait_ge(cum_sb, 1)
            v.tensor_tensor(dec[:, 0, :], cum[:, 2, :], cum[:, 0, :], ALU.subtract).then_inc(cum_sb, 1)
            dt = dts[:, 0, :, :]

            def by_head(ap):
                return ap.rearrange("p (h d) -> p h d", h=HPG)

            def spread(ap, n=HD):
                return ap.unsqueeze(2).to_broadcast([P, HPG, n])

            def y_out(i):
                g, c = i // 2, i % 2
                xg_ = xt[:, c, g * WC:(g + 1) * WC]
                hs = slice(g * HPG, (g + 1) * HPG)
                v.wait_ge(y_ps, i + 1)
                step(v.tensor_tensor(by_head(xg_), by_head(xg_), spread(par("d_skip")[:, hs]), ALU.mult))
                step(v.tensor_tensor(xg_, xg_, ps[:, 6, :], ALU.add))
                if c:
                    step(v.tensor_tensor(by_head(yt[:, :]), by_head(ps[:, 7, :]), spread(dec[:, 1, hs]), ALU.mult))
                    step(v.tensor_tensor(xg_, xg_, yt[:, :], ALU.add))
                v.tensor_tensor(xg_, xg_, zt[:, c, g * WC:(g + 1) * WC], ALU.mult).then_inc(y_sb, 1)

            v.wait_ge(cum_exp, 2)
            v.wait_ge(cv_done, 6)
            v.wait_ge(bk_ps, 5)
            v.wait_ge(bk_sb, 5)
            v.wait_ge(chunk_act, evacuated(chunks["z3"].number)[1])
            for i in range(2 * GROUPS):
                g, c = i // 2, i % 2
                hs = slice(g * HPG, (g + 1) * HPG)
                v.wait_ge(sg_ps, i + 1)
                if i >= 2:
                    v.wait_ge(y_ps, i - 1)
                v.tensor_tensor(cbm[:, i % 2, :], ps[:, i % 2, 0:P], tri, ALU.mult)
                b = 2 + 2 * (i % 2)
                sgv = segs[:, i % 2, :, :]
                step(v.tensor_tensor(sgv, ps[:, b:b + 2, :].rearrange("p b (h c) -> p (b h) c", h=4),
                                     spread(cum[:, c, hs], P), ALU.subtract))
                v.tensor_scalar(sgv, sgv, 0.0, None, ALU.min).then_inc(sg_sb, 1)
                step(v.tensor_tensor(by_head(xdt[:, i % 2, :]), by_head(xt[:, c, g * WC:(g + 1) * WC]), spread(dt[:, c, hs]),
                                     ALU.mult))
                if c == 0:
                    step(v.tensor_tensor(by_head(xtl[:, :]), by_head(xdt[:, i % 2, :]), spread(dec[:, 0, hs]), ALU.mult))
                if i:
                    y_out(i - 1)
                v.wait_ge(sg_exp, i + 1)
                v.tensor_tensor(sgv, sgv, cbm[:, i % 2, :].unsqueeze(1).to_broadcast([P, HPG, P]), ALU.mult).then_inc(
                    m_done, 1)
            y_out(2 * GROUPS - 1)
            v.wait_ge(grms, 1)
            v.wait_ge(gn_in, 16)
            step(v.reciprocal(gss[:, 2, :, :], gss[:, 1, :, :]))
            for g in range(GROUPS):
                for c in range(NT):
                    y = xt[:, c, g * WC:(g + 1) * WC]
                    v.scalar_tensor_tensor(y, y, gss[:, 2, c, g:g + 1], gn[:, g * WC:(g + 1) * WC], ALU.mult,
                                           ALU.mult).then_inc(yn_ready, 1)

            def y_parts(n):
                at = (slice(None), slice(4 * (n // 2 % 2), 4 * (n // 2 % 2) + 4), tok(n % 2))
                return (xT_lo[at], xT_hi[at]) if n // 2 < 2 else (yT_lo[at], yT_hi[at])

            turn_lo(GROUP["ssd"], 8, to=y_parts)
            add_out("o_out0", 0)
            add_out("o_out1", 1)

            v.wait_ge(chunk_dve, 4)
            norm(4, GROUP["ssd"] + 8)
            splits(ends[starts["experts"] - 1])
            turn_lo(GROUP["o_moe"])
            v.wait_ge(rt_ps, 1)
            v.wait_ge(rstd_ready, 5)
            for t in range(NT):
                step(v.tensor_scalar(lg[:, t, :], ps[:, 4, t * NE:(t + 1) * NE], stat[:, 2, t:t + 1], None, ALU.mult))
            for t in range(NT):
                step(v.max(lmax[:, t, :], lg[:, t, :]))
                step(v.max_index(lidx[:, t, :], lmax[:, t, :], lg[:, t, :]))
                step(v.tensor_copy(lidf[:, t, :], lidx[:, t, :]))
                for n in range(2):
                    step(v.tensor_scalar(oh[:, n, t, :], iota[:, 0:NE], lidf[:, t, n:n + 1], None, ALU.is_equal))
            v.tensor_tensor(gw[:, 0, :], lmax[:, :, 1], lmax[:, :, 0], ALU.subtract).then_inc(lw_max, 1)
            v.tensor_tensor(routed[:, :, :], oh[:, 0, :, :], oh[:, 1, :, :], ALU.add).then_inc(routed_sb, 1)
            v.wait_ge(lw_exp, 1)
            step(v.tensor_scalar(gw[:, 2, :], gw[:, 1, :], 1.0, None, ALU.add))
            step(v.reciprocal(gw[:, 2, :], gw[:, 2, :]))
            step(v.tensor_tensor(gw[:, 3, :], gw[:, 1, :], gw[:, 2, :], ALU.mult))
            for t in range(NT):
                step(v.tensor_scalar(gates[:, t, :], oh[:, 0, t, :], gw[:, 2, t:t + 1], None, ALU.mult))
                step(v.scalar_tensor_tensor(gates[:, t, :], oh[:, 1, t, :], gw[:, 3, t:t + 1], gates[:, t, :], ALU.mult,
                                            ALU.add))
            v.wait_ge(slot_ps, 1)
            v.wait_ge(routed_sb, 1)
            pos = ps[:, 5, 0:NT * NE].rearrange("p (t e) -> p t e", t=NT)
            step(v.memset(slot[:, :, :, NE:NE + 1], -1.0))
            step(v.tensor_tensor(slot[:, 0, :, 0:NE], pos, routed[:, :, :], ALU.mult))
            step(v.tensor_scalar(slot[:, 0, :, 0:NE], slot[:, 0, :, 0:NE], -1.0, None, ALU.add))
            step(v.tensor_scalar(slot[:, 1, :, :], slot[:, 0, :, :], -float(P), None, ALU.add))
            step(v.tensor_reduce(most[:, 0:1], ps[:, 5, NT * NE:(NT + 1) * NE], AX, ALU.max))
            step(v.tensor_scalar(most[:, 1:2], most[:, 0:1], P + 0.5, None, ALU.is_gt))
            v.tensor_copy(flag[:, 0:1], most[:, 1:2]).then_inc(flag_set, 1)
            v.wait_ge(hn_split, 1)
            for t in range(NT):
                ins = v.scalar_tensor_tensor(hn_lo[:, t, :], hn[:, t, :], stat[:, 2, t:t + 1], hn_hi[:, t, :], ALU.mult,
                                             ALU.subtract)
            ins.then_inc(hn_split, 1)

            def end(step_):
                return 2 * (FFN_AT[step_] + 1)

            def select(s, turn, e):
                for t in range(NT):
                    at = slice(e, e + 1) if isinstance(e, int) else bass.ds(e, 1)
                    ins = v.tensor_scalar(sel[:, t, :], iota, slot[:, turn, t, at], None, ALU.is_equal)
                ins.then_inc(s.sel, 1)

            def take_tokens_lo(s, count):
                v.wait_ge(s.xe_hi, count)
                v.tensor_tensor(xT_lo[:, :, 0:P], ps[:, 6:8, :].rearrange("p b (k c) -> p (b k) c", k=4),
                                xT_hi[:, :, 0:P], ALU.subtract).then_inc(s.xe_lo, 1)

            def result_lo(s, count):
                v.wait_ge(s.y_hi, count)
                v.tensor_tensor(y_lo[:, :], ps[:, 2:4, :].rearrange("p b c -> p (b c)"), y_hi[:, :],
                                ALU.subtract).then_inc(s.y_lo, 1)

            def add_result(s, count, e):
                v.wait_ge(s.back_ps, count)
                at = slice(e, e + 1) if isinstance(e, int) else bass.ds(e, 1)
                for t in range(NT):
                    ins = v.scalar_tensor_tensor(h[:, t, :], ps[:, 4 + 2 * t:6 + 2 * t, :].rearrange("p b c -> p (b c)"),
                                                 gates[:, t, at], h[:, t, :], ALU.mult, ALU.add)
                ins.then_inc(s.summed, 1)

            def expert(s, base, turn, e, peeled):
                first = ends[base - 1] if base else 0
                shift, count = e * NHALF + first, e * FCH
                done = [0]

                def ahead(upto):
                    while done[0] < min(upto, NHALF):
                        q = first + done[0]
                        i = base + done[0] // 2
                        k = HK * (done[0] % 2)
                        v.wait_ge(s.hi_done, e * NHALF + (q + 1))
                        v.tensor_tensor(wlo[:, q % SPL, :, :], raw[:, i % RAW, k:k + HK, :], whi[:, q % SPL, :, :],
                                        ALU.subtract).then_inc(s.lo_done, 1)
                        done[0] += 1

                ahead(SPL)
                if not peeled:
                    result_lo(s, e)
                    ahead(end(("g", 0, 1)) + LAG)
                    add_result(s, e, e - 1)
                ahead(end(("u", 0, 1)) + LAG)
                prod(s, 1, shift + end(("u", 0, 1)), count, 0)
                v.wait_ge(s.selT_ps, e + 1)
                select(s, turn, e + 1)
                for j in range(1, FCH):
                    ahead(end(("u", j, 1)) + LAG)
                    if j >= 2:
                        v.wait_ge(s.aT_ps, count + (j - 1))
                    prod(s, 1, shift + end(("u", j, 1)), count + j, j)
                    aT_part_lo(s, 1, count + (j - 1), j - 1)
                ahead(end(("d", FCH - 3, 1)) + LAG)
                take_tokens_lo(s, e + 2)
                ahead(end(("d", FCH - 2, 1)) + LAG)
                aT_part_lo(s, 1, count + (FCH - 1), FCH - 1)
                ahead(NHALF)
                if not peeled:
                    v.wait_ge(s.summed, e)

            def experts_dve(s, base, turn):
                select(s, turn, 0)
                take_tokens_lo(s, 1)
                expert(s, base, turn, 0, True)
                with v.Fori(1, NE) as e:
                    expert(s, base, turn, e, False)
                result_lo(s, NE)
                add_result(s, NE, NE - 1)
                v.wait_ge(s.summed, NE)

            experts_dve(main, starts["experts"], 0)
            v.wait_ge(flag_set, 1)
            some = v.value_load(flag[0:1, 0:1], min_val=0, max_val=1)
            with v.If(some != 0):
                experts_dve(rest, 0, 1)
            v.sem_inc(gate_ple, 1)
            sent[0] = ends[starts["experts"] + NE * NEXP - 1]
            splits(ends[chunks["o_gate0"].first])
            ple("o", 5, GROUP["o_moe"] + 4)
            v.wait_ge(rms, 7)
            v.wait_ge(gain_in, 16 * 6)
            step(v.reciprocal(stat[:, 2, :], stat[:, 1, :]))
            for t in range(NT):
                ins = v.scalar_tensor_tensor(hn[:, t, :], h[:, t, :], stat[:, 2, t:t + 1], gain[:, :], ALU.mult, ALU.mult)
            ins.then_inc(fin, 1)

        @block.tensor
        def _(pe):
            def turn(g, srcs):
                if g >= 4:
                    pe.wait_ge(tp_hi, g - 3)
                    pe.wait_ge(tp_lo, g - 3)
                for n, src in enumerate(srcs):
                    ins = pe.transpose(ps[:, 4 + g % 4, n * P:(n + 1) * P], src, ident)
                ins.then_inc(tp_ps, 1)

            def turn_hn(first, n):
                for i in range(4):
                    pe.wait_ge(hg_ready, NT * (n - 1) + i // 2 + 1)
                    turn(first + i, [hn[:, i // 2, (4 * (i % 2) + k) * P:(4 * (i % 2) + k + 1) * P] for k in range(4)])
                pe.wait_ge(tp_hi, first + 4)
                pe.wait_ge(tp_lo, first + 4)

            def three(out_ap, left, right, first, last):
                (lh, ll), (rh, rl) = left, right
                pe.matmul(out_ap, lh, rh, start=first, stop=False)
                pe.matmul(out_ap, lh, rl, start=False, stop=False)
                return pe.matmul(out_ap, ll, rh, start=False, stop=last)

            def left_xT(k, t):
                return xT_hi[:, k, tok(t)], xT_lo[:, k, tok(t)]

            def left_y(k, t):
                return left_xT(k, t) if k < 8 else (yT_hi[:, k - 8, tok(t)], yT_lo[:, k - 8, tok(t)])

            def panel_mm(s, shift, half0, outs, left, k0, n, width, first, last):
                for k in range(n):
                    q = half0 + k // HK
                    if k % HK == 0:
                        pe.wait_ge(s.lo_done, shift + (q + 1) if shift is not None else q + 1)
                    for t, o in enumerate(outs):
                        ins = three(o, left(k0 + k, t),
                                    (whi[:, q % SPL, k % HK, 0:width], wlo[:, q % SPL, k % HK, 0:width]),
                                    first and k == 0, last and k == n - 1)
                    if k % HK == HK - 1 or k == n - 1:
                        ins.then_inc(s.half_used, 1)

            def chunk(name, left=left_xT):
                c = chunks[name]
                if c.number >= 2:
                    pe.wait_ge(*evacuated(c.number - 2))
                for n in range(c.panels):
                    i = c.first + n
                    k = min(KS, c.ksubs - n * KS)
                    outs = [ps[:, c.banks + t, 0:c.width] for t in range(NT)]
                    panel_mm(dense, None, ends[i] - -(-k // HK), outs, left, n * KS, k, c.width, n == 0,
                             n == c.panels - 1)

            def blocks(ap, n):
                return [ap[:, k * P:(k + 1) * P] for k in range(n)]

            pe.wait_ge(const_in, 16)
            turn_hn(GROUP["e_mix"], 1)
            pe.wait_ge(p_in, 16)
            for i in range(2):
                turn(GROUP["ple"] + i, [pin[:, i * NT + t, k * P:(k + 1) * P] for t in range(NT) for k in range(PLE // P)])
            for name in ("kv_qi", "ki_wi", "q", "xr", "xg"):
                chunk(name)

            pe.wait_ge(roped, 1)
            pe.wait_ge(*evacuated(chunks["xg"].number))
            for n in range(6):
                t = n % 2
                if n < 2:
                    srcs = [kdup[:, t, g, r].rearrange("p a d -> p (a d)") for g in range(KVH) for r in range(2)]
                elif n < 4:
                    srcs = [kdup[:, t, KVH, r].rearrange("p a d -> p (a d)") for r in range(2)] + blocks(u[:, t, U_QI:U_KI], 2)
                else:
                    srcs = blocks(u[:, t, U_Q:U_K], 4)
                for k, src in enumerate(srcs):
                    ins = pe.transpose(ps[:, (n + 4) % 8, k * P:(k + 1) * P], src, ident)
                ins.then_inc(at_ps, 1)
            for n in range(4):
                if n >= 2:
                    pe.wait_ge(at_sb, n - 1)
                b = U_XR if n < 2 else U_XG
                for k, src in enumerate(blocks(u[:, n % 2, b:b + LRU], 4)):
                    ins = pe.transpose(ps[:, n + 2, k * P:(k + 1) * P], src, ident)
                ins.then_inc(lt_ps, 1)
            for t in range(NT):
                pe.wait_ge(at_sb, 4 if t == 0 else 6)
                keys = (t + 1) * P
                for j in range(IDXH):
                    o = ps[:, 6, j * P:(j + 1) * P] if t == 0 else ps[:, j // 2, (j % 2) * SEQ:(j % 2 + 1) * SEQ]
                    ins = pe.matmul(o, kqT[:, 6 + j // 2, tok(t)], kqT[:, 4 + j % 2, 0:keys], start=True, stop=True)
                ins.then_inc(ix_ps, 1)
            pe.wait_ge(lt_sb, 4)
            pe.wait_ge(conv_done, 1)
            for n in range(2):
                for k in range(LRU_K):
                    ins = pe.matmul(ps[:, 2 + 2 * n + k // 2, (k % 2) * SEQ:(k % 2 + 1) * SEQ], bd[:, n, k, :], xc[:, k, :],
                                    start=True, stop=True)
                ins.then_inc(gate_ps, 1)

            def logits(s):
                t, g, keys = s // 2, s % 2, (s // 2 + 1) * P
                if s == 0:
                    pe.wait_ge(ix_relu, 1)
                elif s == 2:
                    pe.wait_ge(ix_relu, 3)
                elif s == 3:
                    pe.wait_ge(lg_sb, 2)
                for j in range(4):
                    hd = 4 * g + j
                    o = ps[:, 6 + s, j * P:(j + 1) * P] if t == 0 else \
                        ps[:, (0 if s == 2 else 6) + j // 2, (j % 2) * SEQ:(j % 2 + 1) * SEQ]
                    ins = pe.matmul(o, qT[:, hd // 2, tok(t)], kqT[:, 2 * g + hd % 2, 0:keys], start=True, stop=True)
                ins.then_inc(lg_ps, 1)

            def turn_probs(s):
                t = s // 2
                pe.wait_ge(pr_sb, s + 1)
                if s >= 2:
                    pe.wait_ge(pt_sb, s)
                for j in range(4):
                    for kb in range(t + 1):
                        n = j * (t + 1) + kb
                        bank = 2 + s if t == 0 else 2 + n // 4
                        ins = pe.transpose(ps[:, bank, (n % 4) * P:(n % 4 + 1) * P], probs[:, s % 2, j, tok(kb)], ident)
                ins.then_inc(pt_ps, 1)

            def attend(s):
                t, g = s // 2, s % 2
                pe.wait_ge(pt_sb, s + 1)
                for j in range(4):
                    hd = 4 * g + j
                    for kb in range(t + 1):
                        ins = pe.matmul(ps[:, 4 + t, hd * HD:(hd + 1) * HD], prT[:, j * (t + 1) + kb, :],
                                        u[:, kb, U_V + g * HD:U_V + (g + 1) * HD], start=(kb == 0), stop=(kb == t))
                ins.then_inc(o_ps, 1)

            logits(0)
            logits(1)
            logits(2)
            pe.wait_ge(gate_sb, 2)
            turn_probs(0)
            logits(3)
            turn_probs(1)
            attend(0)
            attend(1)
            turn_probs(2)
            attend(2)
            turn_probs(3)
            attend(3)
            for t in range(NT):
                pe.wait_ge(o_sb, t + 1)
                if t == 0:
                    pe.wait_ge(lg_sb, 4)
                turn(GROUP["o_attn"] + t, blocks(hn[:, t, 0:HEADS * HD], 4))
            pe.wait_ge(tp_lo, GROUP["o_attn"] + 2)
            pe.wait_ge(lru_lo, 1)
            chunk("e_out0")
            chunk("e_out1")

            def ffn(s, nt, base, e, after_g0=None, after_u0=None, before_end=None):
                shift = e * NHALF if e is not None else None
                count = e * FCH if e is not None else 0
                first = ends[base - 1] if base else 0
                ub = nt
                db = 4 if nt == 2 else 2

                def panel(step_, outs, left_, k0, start, stop):
                    panel_mm(s, shift, first + 2 * FFN_AT[step_], outs, left_, k0, KS, WC, start, stop)

                def turn_act(j):
                    pe.wait_ge(s.prod, count + (j + 1))
                    if nt == 2:
                        pe.wait_ge(s.silu, min(j + 2, FCH))
                    elif j >= 2:
                        pe.wait_ge(s.aT_lo, count + (j - 1))
                    else:
                        pe.wait_ge(s.selT_sb, e + 1)
                    for t in range(nt):
                        bank = t if nt == 2 else 4 + j % 2
                        for k in range(4):
                            ins = pe.transpose(ps[:, bank, k * P:(k + 1) * P], act[:, j % 2, t, k * P:(k + 1) * P], ident)
                    ins.then_inc(s.aT_ps, 1)

                def down(j):
                    pe.wait_ge(s.aT_lo, count + (j + 1))
                    for half in range(2):
                        outs = [ps[:, db + 2 * t + half, :] for t in range(nt)]
                        panel(("d", j, half), outs, lambda k, t: (aT_hi[:, j % 2, k, tok(t)], aT_lo[:, j % 2, k, tok(t)]),
                              0, j == 0, j == FCH - 1)

                for j in range(FCH):
                    if j:
                        pe.wait_ge(s.silu, count + j)
                        if nt == 2 and j >= 2:
                            pe.wait_ge(s.aT_lo, j - 1)
                    for half in range(2):
                        panel(("g", j, half), [ps[:, t, :] for t in range(nt)], left_xT, KS * half, half == 0, half == 1)
                    if j == 0 and after_g0:
                        after_g0()
                    if j:
                        pe.wait_ge(s.prod, count + j)
                    for half in range(2):
                        panel(("u", j, half), [ps[:, ub + t, :] for t in range(nt)], left_xT, KS * half, half == 0,
                              half == 1)
                    if j == 0 and after_u0:
                        after_u0()
                    if j:
                        turn_act(j - 1)
                    if j >= 2:
                        down(j - 2)
                if before_end:
                    before_end()
                down(FCH - 2)
                turn_act(FCH - 1)
                down(FCH - 1)

            turn_hn(GROUP["e_ffn"], 2)
            ffn(dense, NT, starts["ffn"], None)

            def embed(layer, index):
                for half in range(2):
                    chunk(f"{layer}_emb{half}", lambda k, t: (pT_hi[:, index, k, tok(t)], pT_lo[:, index, k, tok(t)]))

            embed("e", 0)
            turn_hn(GROUP["e_ple"], 3)
            chunk("e_gate0")
            chunk("e_gate1")

            turn_hn(GROUP["o_mix"], 4)
            stage = ["B", "C", "x0", "x1", "x2", "x3"]

            def forward(q):
                pe.wait_ge(*evacuated(chunks[stage[q]].number))
                if q >= 2:
                    pe.wait_ge(fw_sb, q - 1)
                    if q != 3:
                        pe.wait_ge(bk_sb, 1 if q == 2 else q - 2)
                for t in range(NT):
                    for k, src in enumerate(blocks(hn[:, t, (q % 2) * WC:(q % 2 + 1) * WC], 4)):
                        ins = pe.transpose(ps[:, 4 + 2 * (q % 2) + t, k * P:(k + 1) * P], src, ident)
                ins.then_inc(fw_ps, 1)

            def backward(q):
                pe.wait_ge(cv_done, q + 1)
                if q == 1:
                    return
                src = BT if q == 0 else cv[:, q % 2]
                for t in range(1 if q == 0 else NT):
                    for k in range(4):
                        ins = pe.transpose(ps[:, 4 + 2 * (q % 2) + t, k * P:(k + 1) * P], src[:, k, tok(t)], ident)
                ins.then_inc(bk_ps, 1)

            chunk("dt")
            chunk("B")
            chunk("C")
            forward(0)
            chunk("x0")
            forward(1)
            backward(0)
            for q in range(2, 6):
                chunk(f"x{q - 1}" if q < 5 else "z0")
                forward(q)
                backward(q - 1)
            chunk("z1")
            backward(5)
            chunk("z2")
            chunk("z3")

            pe.wait_ge(dt_da, 1)
            pe.wait_ge(bk_sb, 5)
            pe.wait_ge(chunk_act, evacuated(chunks["z3"].number)[1])
            da = dts[:, 1, :, :]
            for c in range(NT):
                pe.matmul(ps[:, 6, c * SH:(c + 1) * SH], tri, da[:, c, :], start=True, stop=True)
            pe.matmul(ps[:, 6, 2 * SH:3 * SH], ones, da[:, 0, :], start=True, stop=True).then_inc(cum_ps, 1)

            def decays(i):
                g, c = i // 2, i % 2
                if i >= 2:
                    pe.wait_ge(sg_sb, i - 1)
                pe.matmul(ps[:, i % 2, 0:P], BT[:, g, tok(c)], CT[:, g, tok(c)], start=True, stop=True)
                for j in range(HPG):
                    ins = pe.matmul(ps[:, 2 + 2 * (i % 2) + j // 4, (j % 4) * P:(j % 4 + 1) * P],
                                    da[:, c, g * HPG + j:g * HPG + j + 1].to_broadcast([P, P]), tri, start=True, stop=True)
                ins.then_inc(sg_ps, 1)

            def ssd(i):
                g, c = i // 2, i % 2
                pe.wait_ge(m_done, i + 1)
                if i:
                    pe.wait_ge(y_sb, i)
                else:
                    pe.wait_ge(cum_sb, 1)
                for j in range(HPG):
                    ins = pe.matmul(ps[:, 6, j * HD:(j + 1) * HD], segs[:, i % 2, j, :],
                                    xdt[:, i % 2, j * HD:(j + 1) * HD], start=True, stop=True)
                if c == 0:
                    ins = pe.matmul(ps[:, 7, :], Btok[:, g, :], xtl[:, :], start=True, stop=True)
                else:
                    pe.wait_ge(st_sb, g + 1)
                    ins = pe.matmul(ps[:, 7, :], CT[:, g, tok(1)], st[:, :], start=True, stop=True)
                ins.then_inc(y_ps, 1)

            decays(0)
            for i in range(2 * GROUPS):
                if i + 1 < 2 * GROUPS:
                    decays(i + 1)
                ssd(i)
            for n in range(8):
                g, t = n // 2, n % 2
                pe.wait_ge(yn_ready, n + 1)
                turn(GROUP["ssd"] + n, blocks(xt[:, t, g * WC:(g + 1) * WC], 4))
            pe.wait_ge(tp_lo, GROUP["ssd"] + 8)
            chunk("o_out0", left_y)
            chunk("o_out1", left_y)

            embed("o", 1)

            turn_hn(GROUP["o_moe"], 5)
            pe.wait_ge(rt_done, 2)
            for t in range(NT):
                for k in range(DM // P):
                    ins = three(ps[:, 4, t * NE:(t + 1) * NE], left_xT(k, t), (rt_hi[:, k, :], rt_lo[:, k, :]), k == 0,
                                k == DM // P - 1)
            ins.then_inc(rt_ps, 1)
            pe.wait_ge(routed_sb, 1)
            pe.matmul(ps[:, 5, 0:NE], tri, routed[:, 0, :], start=True, stop=True)
            pe.matmul(ps[:, 5, NE:2 * NE], tri, routed[:, 1, :], start=True, stop=False)
            pe.matmul(ps[:, 5, NE:2 * NE], ones, routed[:, 0, :], start=False, stop=True)
            pe.matmul(ps[:, 5, 2 * NE:3 * NE], ones, routed[:, 0, :], start=True, stop=False)
            pe.matmul(ps[:, 5, 2 * NE:3 * NE], ones, routed[:, 1, :], start=False, stop=True).then_inc(slot_ps, 1)
            pe.wait_ge(flag_set, 1)
            pe.wait_ge(hn_split, 2)
            pe.wait_ge(setup, 1)

            def gather(s, count):
                pe.wait_ge(s.sel, count)
                for k in range(DM // P):
                    o = ps[:, 6 + k // 4, (k % 4) * P:(k % 4 + 1) * P]
                    for n, (t, part) in enumerate(((0, hn_hi), (0, hn_lo), (1, hn_hi), (1, hn_lo))):
                        ins = pe.matmul(o, part[:, t, k * P:(k + 1) * P], sel[:, t, :], start=(n == 0), stop=(n == 3))
                ins.then_inc(s.xe_ps, 1)

            def scatter(s, count):
                pe.wait_ge(s.y_lo, count)
                pe.wait_ge(s.xe_lo, count + 1)
                for t in range(NT):
                    for half in range(2):
                        cols = slice(half * WC, (half + 1) * WC)
                        o = ps[:, 4 + 2 * t + half, :]
                        pe.matmul(o, selT[:, tok(t)], y_hi[:, cols], start=True, stop=False)
                        ins = pe.matmul(o, selT[:, tok(t)], y_lo[:, cols], start=False, stop=True)
                ins.then_inc(s.back_ps, 1)

            def turn_selection(s, e, peeled):
                if not peeled:
                    pe.wait_ge(s.summed, e)
                for t in range(NT):
                    ins = pe.matmul(ps[:, 5, tok(t)], sel[:, t, :], ident_r[:, :], start=True, stop=True)
                ins.then_inc(s.selT_ps, 1)

            def experts_pe(s, base):
                def expert(e, peeled):
                    pe.wait_ge(s.xe_lo, e + 1)
                    ffn(s, 1, base, e, after_g0=None if peeled else lambda: scatter(s, e),
                        after_u0=lambda: turn_selection(s, e, peeled), before_end=lambda: gather(s, e + 2))

                gather(s, 1)
                expert(0, True)
                with pe.Fori(1, NE) as e:
                    expert(e, False)
                scatter(s, NE)

            experts_pe(main, starts["experts"])
            some = pe.value_load(flag[0:1, 0:1], min_val=0, max_val=1)
            with pe.If(some != 0):
                experts_pe(rest, 0)
            turn_hn(GROUP["o_ple"], 6)
            chunk("o_gate0")
            chunk("o_gate1")


_WEIGHTS = ["e_mix_norm", "e_w_in", "e_w_out", "e_ffn_norm", "e_ffn_wg", "e_ffn_wu", "e_ffn_wd", "e_ple_proj",
            "e_ple_gate_norm", "e_ple_gate", "o_mix_norm", "o_w_in", "o_gnorm", "o_w_out", "o_moe_norm", "o_exp_wg",
            "o_exp_wu", "o_exp_wd", "o_ple_proj", "o_ple_gate_norm", "o_ple_gate", "final_norm"]


def kernel(**inputs):
    import concourse.bacc as _bacc
    from concourse.bass_utils import run_bass_kernel_spmd as _run

    nc = _bacc.Bacc("TRN2", target_bir_lowering=False, num_devices=1)
    arrays = {}

    def dram(name, a):
        a = np.ascontiguousarray(a)
        arrays[f"in_{name}_dram"] = a
        return nc.dram_tensor(f"in_{name}_dram", a.shape, mybir.dt.from_np(a.dtype), kind="ExternalInput").ap()

    r = np.arange(P)
    inv = np.float32(500000.0) ** (-np.arange(ROT, dtype=np.float32) / np.float32(ROT))
    ang = np.arange(SEQ, dtype=np.float32)[:, None] * inv[None, :].astype(np.float32)
    by_tile = lambda a: a.reshape(NT, P, ROT).transpose(1, 0, 2).reshape(P, NT * ROT)
    const = np.concatenate([
        np.eye(P), np.where(r[None, :] <= r[:, None], 0.0, NEG), r[:, None] <= r[None, :], np.ones((P, P)),
        np.broadcast_to(r[None, :], (P, P)), by_tile(np.cos(ang)), by_tile(np.sin(ang)), np.full((P, 1), EPS)],
        axis=1).astype(np.float32)

    f = {k: np.asarray(v) for k, v in inputs.items()}
    chan = lambda a: a.reshape(-1, P).T
    taps = lambda a: a.T.reshape(-1, P, 4).transpose(1, 0, 2).reshape(P, -1)
    blocks = lambda a: a.reshape(LRU_K, 2, HD, HD).transpose(1, 2, 0, 3).reshape(P, -1)
    row = lambda a: np.broadcast_to(a[None, :], (P, a.shape[0]))
    small = np.concatenate([
        taps(f["e_lru_conv_w"]), chan(f["e_lru_conv_b"]), chan(f["e_lru_ba"]), chan(f["e_lru_bx"]),
        chan(f["e_lru_lambda"]), blocks(f["e_lru_wa"]), blocks(f["e_lru_wx"]), taps(f["o_conv_w"]),
        chan(f["o_conv_b"]), row(f["o_dt_bias"]), row(f["o_a_log"]), row(f["o_d_skip"]),
        f["o_router"].reshape(DM // P, P, NE).transpose(1, 0, 2).reshape(P, -1)], axis=1)

    w = {name: dram(name, f[name]) for name in _WEIGHTS}
    x = dram("x", f["x"].reshape(SEQ, DM))
    p = dram("p", f["p"].reshape(2, SEQ, PLE))
    cst, sml = dram("const", const), dram("small", small)
    out = nc.dram_tensor("out_0_dram", (SEQ, DM), F32, kind="ExternalOutput").ap()
    build(nc, w, x, p, cst, sml, out)
    r = _run(nc, [arrays], core_ids=[0])
    return r.results[0]["out_0_dram"].reshape(1, SEQ, DM)
```

```python
from contextlib import ExitStack

import numpy as np

import concourse.bass as bass
from concourse import mybir

F32 = mybir.dt.float32
F32R = mybir.dt.float32r
I32 = mybir.dt.int32
U32 = mybir.dt.uint32
ALU = mybir.AluOpType
ACT = mybir.ActivationFunctionType
AX = mybir.AxisListType.X

P = 128
SEQ, DM, DFF = 256, 1024, 3584
NT = SEQ // P
HD, HEADS, KVH, IDXH = 64, 8, 2, 4
CONV_DVE = 2
ROT = HD // 4 // 2
LRU = 512
LRU_K = LRU // P
PLE = 256
NSEL = 64
U_Q, U_K, U_V, U_QI, U_KI, U_WI, U_XG, U_XR, U_END = np.cumsum(
    [0, HEADS * HD, KVH * HD, KVH * HD, IDXH * HD, HD, IDXH, LRU, LRU]).tolist()
INNER, SH, GROUPS, STATE = 2048, 32, 4, 128
HPG = SH // GROUPS
UNITS = 8
HPU, UW = SH // UNITS, INNER // UNITS
Z0, X0, B0, C0, DT0, ODD_END = np.cumsum([0, INNER, INNER, GROUPS * STATE, GROUPS * STATE, SH]).tolist()
NE = 8
EPS = 1e-6
NEG = -1e30
REPLACED = -3e38

KS, WC = 4, 512
HK = 2
RAW, SPL = 6, 4
LAG = SPL - 1
FCH = DFF // WC
NEXP = 2 * 2 * FCH + 2 * FCH
NHALF = NEXP * KS // HK
AHEAD = range(RAW, RAW + 3)


def ring(starts, i):
    return i if i < starts["experts"] + AHEAD[0] else i - len(AHEAD)


class Chunk:

    def __init__(self, name, number, first, ksubs, width, evac):
        self.name, self.number, self.first, self.ksubs, self.width = name, number, first, ksubs, width
        self.evac = evac
        self.banks = 2 * (number % 2)
        self.before = number - 2
        self.panels = -(-ksubs // KS)
        self.last = first + self.panels - 1


def plan():
    panels, chunks = [], {}

    def chunk(name, weight, ksubs, col, width, evac):
        chunks[name] = Chunk(name, len(chunks), len(panels), ksubs, width, evac)
        for k in range(0, ksubs, KS):
            panels.append((weight, k, min(KS, ksubs - k), col, width))

    for name, a, b in (("ki_wi", U_KI, U_XG), ("kv_qi", U_K, U_KI), ("xr", U_XR, U_END), ("q", U_Q, U_K), ("xg", U_XG, U_XR)):
        chunk(name, "e_w_in", DM // P, a, b - a, "act")
    at = len(panels)
    for h in range(2):
        chunk(f"e_out{h}", "e_w_out", DM // P, h * WC, WC, "dve")
        chunks[f"e_out{h}"].banks = 2 * h
        chunks[f"e_out{h}"].first, chunks[f"e_out{h}"].last = at + h, at + 2 + h
    panels[at:] = [("e_w_out", k, KS, h * WC, WC) for k in (KS, 0) for h in range(2)]
    starts = {"ffn": len(panels)}
    panels.extend(ffn_panels("e_ffn_wg", "e_ffn_wu", "e_ffn_wd"))
    for h in range(2):
        chunk(f"e_emb{h}", "e_ple_proj", PLE // P, h * WC, WC, "act")
    for h in range(2):
        chunk(f"e_gate{h}", "e_ple_gate", DM // P, h * WC, WC, "act")
    chunk("B", "o_w_in", DM // P, B0, WC, "act")
    chunk("dt", "o_w_in", DM // P, DT0, SH, "act")
    chunk("C", "o_w_in", DM // P, C0, WC, "act")
    for j in range(INNER // WC):
        chunk(f"x{j}", "o_w_in", DM // P, X0 + j * WC, WC, "act")
    for j in range(INNER // WC):
        chunk(f"z{j}", "o_w_in", DM // P, Z0 + j * WC, WC, "act")
    chunks["z3"].banks, chunks["z3"].before = chunks["z2"].banks, chunks["z2"].number
    for h in range(2):
        chunk(f"o_out{h}", "o_w_out", INNER // P, h * WC, WC, "dve")
    chunks["o_out0"].before = chunks["z3"].number
    for h in range(2):
        chunk(f"o_emb{h}", "o_ple_proj", PLE // P, h * WC, WC, "act")
    starts["experts"] = len(panels)
    panels.extend([None] * (NE * NEXP))
    for h in range(2):
        chunk(f"o_gate{h}", "o_ple_gate", DM // P, h * WC, WC, "act")
    return panels, chunks, starts


def half_ends(panels):
    n, out = 0, []
    for panel in panels:
        n += -(-(panel[2] if panel else KS) // HK)
        out.append(n)
    return out


def ffn_order():
    steps = []
    for j in range(FCH):
        steps += [("g", j, 0), ("g", j, 1), ("u", j, 0), ("u", j, 1)]
        if j >= 2:
            steps += [("d", j - 2, 0), ("d", j - 2, 1)]
    for j in (FCH - 2, FCH - 1):
        steps += [("d", j, 0), ("d", j, 1)]
    return steps


def ffn_panels(wg, wu, wd):
    out = []
    for kind, j, half in ffn_order():
        if kind == "d":
            out.append((wd, KS * j, KS, half * WC, WC))
        else:
            out.append((wg if kind == "g" else wu, KS * half, KS, j * WC, WC))
    return out


FFN_AT = {step: n for n, step in enumerate(ffn_order())}

GROUP = {"e_mix": 0, "ple": 4, "o_attn": 6, "e_ffn": 8, "e_ple": 12, "o_mix": 16, "ssd": 20, "o_moe": 28, "o_ple": 32}
NORMS = ["e_mix", "e_ffn", "e_ple", "o_mix", "o_moe", "o_ple"]


def bank(g):
    return 4 + (0, 2, 1, 3)[g % 4]


CONST = {}
SMALL = {}


def lay(table, *items):
    at = 0
    for name, n in items:
        table[name] = (at, at + n)
        at += n
    return at


CONST_N = lay(CONST, ("ident", P), ("cmask", P), ("tri", P), ("ones", P), ("iota", P), ("cos", NT * ROT),
              ("sin", NT * ROT), ("eps", 1))
SMALL_N = lay(SMALL, ("lru_w", LRU_K * 4), ("lru_b", LRU_K), ("lru_ba", LRU_K), ("lru_bx", LRU_K), ("lam", LRU_K),
              ("lru_wa", LRU_K * HD), ("lru_wx", LRU_K * HD), ("conv_w", 24 * 4), ("conv_b", 24), ("dt_bias", SH),
              ("a_log", SH), ("d_skip", SH), ("router", DM // P * NE))



class Place:

    def __init__(self, nc, at):
        self.nc, self.at = nc, at

    def __call__(self, name, shape, dt=F32):
        t = self.nc.alloc_sbuf_tensor_at(name, shape, dt, offset=self.at)
        self.at += -(-int(np.prod(shape[1:])) * 4 // 32) * 32
        return t


class FfnSems:

    def __init__(self, sem, name, raw_in, hi_done, lo_done, half_used, experts=True):
        self.raw_in, self.hi_done, self.lo_done, self.half_used = raw_in, hi_done, lo_done, half_used
        self.silu = sem(name + "_silu")
        self.prod = sem(name + "_prod")
        self.aT_ps = sem(name + "_aT_ps")
        self.aT_hi = sem(name + "_aT_hi")
        self.aT_lo = sem(name + "_aT_lo")
        self.summed = sem(name + "_summed")
        if not experts:
            return
        self.sel = sem(name + "_sel")
        self.xe_raw = sem(name + "_xe_raw")
        self.xe_tok = sem(name + "_xe_tok")
        self.xe_ps = sem(name + "_xe_ps")
        self.xe_hi = sem(name + "_xe_hi")
        self.xe_lo = sem(name + "_xe_lo")
        self.selT_ps = sem(name + "_selT_ps")
        self.selT_sb = sem(name + "_selT_sb")
        self.y_hi = sem(name + "_y_hi")
        self.y_lo = sem(name + "_y_lo")
        self.back_ps = sem(name + "_back_ps")


def build(nc, w, x, p, const, small, out):
    panels, chunks, starts = plan()
    ends = half_ends(panels)
    halves = [(i, k) for i, panel in enumerate(panels) for k in range(0, panel[2] if panel else KS, HK)]
    ordered = sorted(chunks.values(), key=lambda c: c.number)

    place = Place(nc, 16512)
    cst = place("cst", [P, CONST_N])
    sml = place("sml", [P, SMALL_N])
    raw = place("raw", [P, RAW, KS, WC])
    whi = place("whi", [P, SPL, HK, WC], F32R)
    wlo = place("wlo", [P, SPL, HK, WC], F32R)
    h = place("h", [P, NT, DM])
    hn = place("hn", [P, NT, DM])
    xT_hi = place("xT_hi", [P, DM // P, SEQ], F32R)
    xT_lo = place("xT_lo", [P, DM // P, SEQ], F32R)
    gain = place("gain", [P, DM])
    pT_hi = place("pT_hi", [P, 2, PLE // P, SEQ], F32R)
    pT_lo = place("pT_lo", [P, 2, PLE // P, SEQ], F32R)
    in_pT = Place(nc, place.at - KS * WC * 4)("in_pT", [P, KS, WC])
    ident_r = place("ident_r", [P, P], F32R)
    stat = place("stat", [P, 4, NT])
    warm = place("warm", [P, 16])
    flag = place("flag", [P, 8], I32)
    rt = place("rt", [P, DM // P, 2 * NE], F32R)
    phase = place.at

    place = Place(nc, phase)
    u = place("u", [P, NT, U_END])
    gr = Place(nc, place.at)("gr", [P, LRU_K, SEQ])
    kdup = place("kdup", [P, NT, KVH + 1, 2, 2, HD])
    kqT = place("kqT", [P, 8, SEQ])
    qT = place("qT", [P, 4, SEQ])
    prT_at = place.at
    relu = place("relu", [P, IDXH, SEQ])
    prT = Place(nc, prT_at)("prT", [P, 8, P])
    wi2 = place("wi2", [P, NT, IDXH])
    score = place("score", [P, NT, SEQ])
    work = place("work", [P, SEQ])
    top8 = place("top8", [P, 8])
    keep = place("keep", [P, NT, SEQ])
    early = Place(nc, place.at)
    probs = place("probs", [P, 2, 4, SEQ])
    pin = early("pin", [P, 2 * NT, PLE])
    rot = early("rot", [P, 4, NT, 10, ROT])
    assert early.at <= place.at
    nmax = place("nmax", [P, 4, 4])
    rsum = place("rsum", [P, 4, 4])
    rinv = place("rinv", [P, 4, 4])
    xrT = place("xrT", [P, LRU_K, SEQ + 3])
    xgT = place("xgT", [P, LRU_K, SEQ])
    xc = place("xc", [P, LRU_K, SEQ])
    gi = place("gi", [P, LRU_K, SEQ])
    la = place("la", [P, LRU_K, SEQ])
    bd = place("bd", [P, 2, LRU_K, P])
    c8 = place("c8", [P, 8, LRU_K])
    assert place.at <= 229344, place.at

    place = Place(nc, phase)
    aT_hi = place("aT_hi", [P, 2, KS, SEQ], F32R)
    aT_lo = place("aT_lo", [P, 2, KS, SEQ], F32R)
    sg = place("sg", [P, 2, NT, WC])
    act = place("act", [P, 2, NT, WC])
    emb = place("emb", [P, NT, DM])
    in_y = Place(nc, place.at)("in_y", [P, KS, WC])
    y_hi = place("y_hi", [P, DM], F32R)
    y_lo = place("y_lo", [P, DM], F32R)
    hn_hi = place("hn_hi", [P, NT, DM], F32R)
    hn_lo = place("hn_lo", [P, NT, DM], F32R)
    sel = place("sel", [P, NT, P], F32R)
    selT = place("selT", [P, NT * P], F32R)
    lg = place("lg", [P, NT, NE])
    lmax = place("lmax", [P, NT, 8])
    lidx = place("lidx", [P, NT, 8], U32)
    lidf = place("lidf", [P, NT, 8])
    oh = place("oh", [P, 2, NT, NE])
    gw = place("gw", [P, 4, NT])
    gates = place("gates", [P, NT, NE])
    routed = place("routed", [P, NT, NE])
    slot = place("slot", [P, 2, NT, NE + 1])
    most = place("most", [P, 8])
    xe_tok = place("xe_tok", [P, DM])
    ahead_of = dict(zip(AHEAD, (in_y, hn.rearrange("p t (k c) -> p (t k) c", c=WC), in_pT)))
    assert place.at <= 229344, place.at

    place = Place(nc, phase)
    xt = place("xt", [P, NT, INNER])
    yT = Place(nc, place.at)
    zt = place("zt", [P, NT, INNER])
    yT_hi = yT("yT_hi", [P, DM // P, SEQ], F32R)
    yT_lo = yT("yT_lo", [P, DM // P, SEQ], F32R)
    dx = Place(nc, place.at)("dx", [P, 2, NT, UW])
    BT = place("BT", [P, GROUPS, SEQ])
    CT = place("CT", [P, GROUPS, SEQ])
    Btok = place("Btok", [P, GROUPS, STATE])
    late = Place(nc, place.at)
    pre = place("pre", [P, 2, KS, SEQ + 3])
    gn = late("gn", [P, INNER])
    late = Place(nc, place.at)
    cv = place("cv", [P, 2, KS, SEQ])
    segs = late("segs", [P, 2, HPU, NT, P])
    cbm = place("cbm", [P, GROUPS * NT, P])
    xdt = place("xdt", [P, 2, NT, UW])
    xtl = place("xtl", [P, 2, UW])
    st = place("st", [P, 2, UW])
    yt = place("yt", [P, UW])
    dts = place("dts", [P, 6, NT, SH])
    da3 = place("da3", [P, NT, 3, SH])
    cumT = place("cumT", [P, SEQ], F32R)
    cumT_rest = place("cumT_rest", [P, SEQ])
    pick = place("pick", [P, SH], F32R)
    cum = place("cum", [P, 3, SH])
    dec = place("dec", [P, 2, SH])
    gss = place("gss", [P, 3, NT, GROUPS])
    assert place.at <= 229344, place.at

    in_xT = xT_hi, xT_lo
    in_hn = tuple(b.rearrange("p t (k s) -> p (t k) s", s=SEQ) for b in (hn_hi, hn_lo))
    in_aT = tuple(b.rearrange("p a k s -> p (a k) s") for b in (aT_hi, aT_lo))
    left_of = [in_xT, in_hn, in_hn, in_xT, in_aT, in_xT]

    def con(name):
        return cst[:, CONST[name][0]:CONST[name][1]]

    def par(name, **dims):
        v = sml[:, SMALL[name][0]:SMALL[name][1]]
        return v.rearrange("p (a b) -> p a b", **dims) if dims else v

    ident, cmask, tri, ones, iota, eps = (con(n) for n in ("ident", "cmask", "tri", "ones", "iota", "eps"))
    cos = con("cos").rearrange("p (t r) -> p t r", t=NT)
    sin = con("sin").rearrange("p (t r) -> p t r", t=NT)

    def tok(t):
        return slice(t * P, (t + 1) * P)

    ctx = ExitStack()
    with ctx:
        ps = ctx.enter_context(nc.psum_tensor("ps", [P, 8, 512], F32))

        def sem(name):
            return ctx.enter_context(nc.semaphore(name))

        const_in, small_in, x_in, p_in = sem("const_in"), sem("small_in"), sem("x_in"), sem("p_in")
        gain0_in, gain_in = sem("gain0_in"), sem("gain_in")
        gn_in, out_done = sem("gn_in"), sem("out_done")
        raw_in = [sem(f"raw_in{i}") for i in range(RAW)]
        ahead_in = {n: sem(f"ahead_in{n}") for n in AHEAD}
        hi_done = sem("hi_done")
        lo_done = sem("lo_done")
        half_used = sem("half_used")
        chunk_act, chunk_dve = sem("chunk_act"), sem("chunk_dve")
        act_seq, dve_seq, pool_seq = sem("act_seq"), sem("dve_seq"), sem("pool_seq")
        setup = sem("setup")
        rms = sem("rms")
        hg_ready = sem("hg_ready")
        rstd_ready = sem("rstd_ready")
        tp_ps, tp_hi, tp_lo = sem("tp_ps"), sem("tp_hi"), sem("tp_lo")
        roped = sem("roped")
        at_ps, at_sb = sem("at_ps"), sem("at_sb")
        lt_ps, lt_sb = sem("lt_ps"), sem("lt_sb")
        ix_ps, ix_relu = sem("ix_ps"), sem("ix_relu")
        conv_done, conv_pool = sem("conv_done"), sem("conv_pool")
        gate_ps, gate_sb = sem("gate_ps"), sem("gate_sb")
        lru_a, lru_b1, lru_bs, lru_gelu = sem("lru_a"), sem("lru_b1"), sem("lru_bs"), sem("lru_gelu")
        lru_y, lru_hi, lru_lo = sem("lru_y"), sem("lru_hi"), sem("lru_lo")
        lg_ps, lg_sb, pr_sb = sem("lg_ps"), sem("lg_sb"), sem("pr_sb")
        pt_ps, pt_sb = sem("pt_ps"), sem("pt_sb")
        o_ps, o_sb = sem("o_ps"), sem("o_sb")
        fw_ps, fw_sb = sem("fw_ps"), sem("fw_sb")
        cv_raw, cv_done = sem("cv_raw"), sem("cv_done")
        bk_ps, bk_sb = sem("bk_ps"), sem("bk_sb")
        dt_abs, dt_exp, dt_ln, dt_da = sem("dt_abs"), sem("dt_exp"), sem("dt_ln"), sem("dt_da")
        cum_ps, cum_sb, cum_exp = sem("cum_ps"), sem("cum_sb"), sem("cum_exp")
        cumT_part = sem("cumT_part")
        picked = sem("picked")
        cb_ps, cb_sb = sem("cb_ps"), sem("cb_sb")
        seg_ps, seg_relu, seg_exp = sem("seg_ps"), sem("seg_relu"), sem("seg_exp")
        m_done = sem("m_done")
        xdt_done, dx_done = sem("xdt_done"), sem("dx_done")
        st_ps, st_sb = sem("st_ps"), sem("st_sb")
        y_ps, y_sb, y_done = sem("y_ps"), sem("y_sb"), sem("y_done")
        gss_done, grms = sem("gss_done"), sem("grms")
        yn_ready = sem("yn_ready")
        rt_done, rt_ps, lw_max, lw_exp = sem("rt_done"), sem("rt_ps"), sem("lw_max"), sem("lw_exp")
        routed_sb, slot_ps, flag_set, hn_split = sem("routed_sb"), sem("slot_ps"), sem("flag_set"), sem("hn_split")
        gate_ple = sem("gate_ple")
        ffn_sum = sem("ffn_sum")
        fin = sem("fin")
        dense = FfnSems(sem, "ffn", raw_in, hi_done, lo_done, half_used, experts=False)
        main = FfnSems(sem, "exp", raw_in, hi_done, lo_done, half_used)
        rest = FfnSems(sem, "rest", [sem(f"rest_in{i}") for i in range(RAW)], sem("rest_hi"), sem("rest_lo"),
                       sem("rest_used"))

        def evacuated(number):
            c = ordered[number]
            return (chunk_act if c.evac == "act" else chunk_dve,
                    sum(o.evac == c.evac for o in ordered[:number + 1]))

        def place_of(s, first_expert, i, n):
            return i - len(AHEAD) if s is main and (not first_expert or n > AHEAD[-1]) else i

        def landing(s, first_expert, i, n):
            if s is main and first_expert and n in AHEAD:
                return ahead_of[n]
            return raw[:, place_of(s, first_expert, i, n) % RAW]

        def panel_dram(name, k, n, col, width, e=None):
            src = w[name]
            if e is not None:
                at = slice(e, e + 1) if isinstance(e, int) else bass.ds(e, 1)
                src = src[at, k * P:(k + n) * P, col:col + width].rearrange("a k c -> (a k) c")
            else:
                src = src[k * P:(k + n) * P, col:col + width]
            return src.rearrange("(k p) c -> p k c", p=P)

        block = ctx.enter_context(nc.Block())

        @block.sync
        def _(sp):
            def load(i, panel):
                if i >= RAW:
                    sp.wait_ge(hi_done, ends[i - RAW])
                    sp.wait_ge(lo_done, ends[i - RAW])
                name, k, n, col, width = panel
                r = ring(starts, i)
                sp.dma_start(raw[:, r % RAW, 0:n, 0:width], panel_dram(*panel)).then_inc(raw_in[r % RAW], 16)

            sp.dma_start(h[:, :, :], x.rearrange("(t p) d -> p t d", p=P)).then_inc(x_in, 16)
            for i in range(starts["experts"]):
                load(i, panels[i])

            order = ffn_panels("o_exp_wg", "o_exp_wu", "o_exp_wd")
            base = starts["experts"]
            for n, panel in enumerate(order):
                i = base + n
                if n in AHEAD:
                    if n == AHEAD[0]:
                        sp.wait_ge(yn_ready, 2 * GROUPS)
                    elif n == AHEAD[1]:
                        sp.wait_ge(tp_ps, GROUP["o_moe"] + 4)
                        sp.wait_ge(hn_split, 2)
                    else:
                        sp.wait_ge(half_used, ends[base - 1])
                    sp.dma_start(ahead_of[n][:, :, :], panel_dram(*panel, e=0)).then_inc(ahead_in[n], 16)
                else:
                    r = ring(starts, i)
                    before = i - RAW if n < RAW or n - RAW > AHEAD[-1] else i - RAW - len(AHEAD)
                    sp.wait_ge(hi_done, ends[before])
                    sp.wait_ge(lo_done, ends[before])
                    sp.dma_start(raw[:, r % RAW, :, :], panel_dram(*panel, e=0)).then_inc(raw_in[r % RAW], 16)
            with sp.Fori(1, NE) as e:
                for n, panel in enumerate(order):
                    i = base + n
                    r = i - len(AHEAD)
                    sp.wait_ge(hi_done, e * NHALF + ends[i - RAW])
                    sp.wait_ge(lo_done, e * NHALF + ends[i - RAW])
                    sp.dma_start(raw[:, r % RAW, :, :], panel_dram(*panel, e=e)).then_inc(raw_in[r % RAW], 16)
            sp.wait_ge(flag_set, 1)
            some = sp.value_load(flag[0:1, 0:1], min_val=0, max_val=1)
            with sp.If(some != 0):
                sp.wait_ge(hi_done, ends[base + NE * NEXP - 1])
                sp.wait_ge(lo_done, ends[base + NE * NEXP - 1])
                for n in range(NEXP):
                    if n >= RAW:
                        sp.wait_ge(rest.hi_done, 2 * (n - RAW + 1))
                        sp.wait_ge(rest.lo_done, 2 * (n - RAW + 1))
                    sp.dma_start(raw[:, n % RAW, :, :], panel_dram(*order[n], e=0)).then_inc(rest.raw_in[n % RAW], 16)
                with sp.Fori(1, NE) as e:
                    for n in range(NEXP):
                        sp.wait_ge(rest.hi_done, e * NHALF + 2 * (n - RAW + 1))
                        sp.wait_ge(rest.lo_done, e * NHALF + 2 * (n - RAW + 1))
                        sp.dma_start(raw[:, n % RAW, :, :], panel_dram(*order[n], e=e)).then_inc(
                            rest.raw_in[n % RAW], 16)
                sp.wait_ge(rest.hi_done, NE * NHALF)
                sp.wait_ge(rest.lo_done, NE * NHALF)
            for i in range(base + NE * NEXP, len(panels)):
                load(i, panels[i])
            for t in range(NT):
                sp.wait_ge(fin, t + 1)
                sp.dma_start(out[tok(t), :], hn[:, t, :]).then_inc(out_done, 16)
            sp.wait_ge(out_done, 16 * NT)

        @block.gpsimd
        def _(pool):
            steps = [0]

            def step(ins):
                steps[0] += 1
                ins.then_inc(pool_seq, 1)
                pool.wait_ge(pool_seq, steps[0])

            def unit_inputs(i):
                hs = slice(i * HPU, (i + 1) * HPU)

                def by_head(ap):
                    return ap.rearrange("p (h d) -> p h d", h=HPU)

                def spread(ap):
                    return ap.unsqueeze(2).to_broadcast([P, HPU, HD])

                if i % 2 == 0:
                    pool.wait_ge(bk_sb, i // 2 + 2)
                if i == 0:
                    pool.wait_ge(cum_exp, 1)
                if i >= 2:
                    pool.wait_ge(y_ps, i - 1)
                for c in range(NT):
                    ins = pool.tensor_tensor(by_head(xdt[:, i % 2, c, :]), by_head(xt[:, c, i * UW:(i + 1) * UW]),
                                             spread(dts[:, 0, c, hs]), ALU.mult)
                ins.then_inc(xdt_done, 1)
                pool.wait_ge(xdt_done, 2 * i + 1)
                pool.tensor_tensor(by_head(xtl[:, i % 2, :]), by_head(xdt[:, i % 2, 0, :]), spread(dec[:, 0, hs]),
                                   ALU.mult).then_inc(xdt_done, 1)
                if i == 0:
                    pool.wait_ge(cb_ps, 1)
                elif i >= 2:
                    pool.wait_ge(y_sb, i - 1)
                for c in range(NT):
                    ins = pool.tensor_tensor(by_head(dx[:, i % 2, c, :]), by_head(xt[:, c, i * UW:(i + 1) * UW]),
                                             spread(par("d_skip")[:, hs]), ALU.mult)
                ins.then_inc(dx_done, 1)

            pool.wait_ge(lt_sb, 2)
            ks = slice(CONV_DVE, LRU_K)
            shape = [P, LRU_K - CONV_DVE, SEQ]
            for j in (3, 0, 1, 2):
                wj = par("lru_w", a=LRU_K)[:, ks, j:j + 1].to_broadcast(shape)
                step(pool.tensor_tensor((xc if j == 3 else gi)[:, ks, :], xrT[:, ks, j:j + SEQ], wj, ALU.mult))
                add = gi[:, ks, :] if j != 3 else par("lru_b")[:, ks].unsqueeze(2).to_broadcast(shape)
                ins = pool.tensor_tensor(xc[:, ks, :], xc[:, ks, :], add, ALU.add)
                if j != 2:
                    step(ins)
            ins.then_inc(conv_pool, 1)

            for n, name in enumerate(("e_ffn_norm", "e_ple_gate_norm", "o_mix_norm", "o_moe_norm", "o_ple_gate_norm",
                                      "final_norm")):
                pool.wait_ge(hg_ready, 4 * (n + 1))
                pool.dma_start(gain[:, :], w[name].partition_broadcast(P)).then_inc(gain_in, 16)
                if name == "o_mix_norm":
                    pool.wait_ge(cv_raw, 6)
                    pool.dma_start(gn[:, :], w["o_gnorm"].partition_broadcast(P)).then_inc(gn_in, 16)
                if name == "o_moe_norm":
                    for i in range(UNITS):
                        unit_inputs(i)

        @block.scalar
        def _(a):
            sent = [0]
            steps = [0]

            def step(ins):
                steps[0] += 1
                ins.then_inc(act_seq, 1)
                a.wait_ge(act_seq, steps[0])

            def splits(upto):
                while sent[0] < min(upto, len(halves)) and panels[halves[sent[0]][0]] is not None:
                    q = sent[0]
                    i, k = halves[q]
                    n, width = min(HK, panels[i][2] - k), panels[i][4]
                    a.wait_ge(raw_in[ring(starts, i) % RAW], 16 * (ring(starts, i) // RAW + 1))
                    if q >= SPL:
                        a.wait_ge(half_used, q - SPL + 1)
                    a.activation(whi[:, q % SPL, 0:n, 0:width], raw[:, ring(starts, i) % RAW, k:k + n, 0:width], ACT.Copy).then_inc(
                        hi_done, 1)
                    sent[0] += 1

            def taken(name):
                c = chunks[name]
                splits(ends[c.last] + LAG)
                a.wait_ge(half_used, ends[c.last])
                return ps[:, c.banks:c.banks + 2, 0:c.width]

            preloads = [0]

            def preload(func):
                a.activation(warm[:, 8 + preloads[0]:9 + preloads[0]], eps, func)
                preloads[0] += 1

            def norm(n, scratch):
                a.activation(warm[:, 0:1], eps, ACT.Sqrt)
                summed = {0: (x_in, 16), 1: (chunk_dve, 2), 2: (dense.summed, 2), 3: (gate_ple, 2), 4: (chunk_dve, 4),
                          5: (gate_ple, 3)}
                a.wait_ge(*summed[n])
                for t in range(NT):
                    step(a.activation(scratch, h[:, t, :], ACT.Square, accum_out=stat[:, 0, t:t + 1]))
                a.activation(stat[:, 1, :], stat[:, 0, :], ACT.Sqrt, scale=1.0 / DM, bias=eps).then_inc(rms, 1)

            def normed(dst, src, func, n):
                a.wait_ge(rstd_ready, n + 1)
                for t in range(NT):
                    ins = a.activation(dst[:, t], src[:, t], func, scale=stat[:, 2, t:t + 1])
                return ins

            def group_hi(g, dst):
                a.wait_ge(tp_ps, g + 1)
                a.activation(dst, ps[:, bank(g), :].rearrange("p (k c) -> p k c", k=4), ACT.Copy).then_inc(tp_hi, 1)

            def turn_hi(n, half):
                for t in range(NT):
                    group_hi(GROUP[NORMS[n]] + 2 * half + t, left_of[n][0][:, 4 * half:4 * half + 4, tok(t)])

            a.dma_start(cst[:, :], const).then_inc(const_in, 16)
            a.dma_start(gain[:, :], w["e_mix_norm"].partition_broadcast(P)).then_inc(gain0_in, 16)
            a.dma_start(pin[:, :, :], p.rearrange("l (t p) d -> p (l t) d", p=P)).then_inc(p_in, 16)
            a.dma_start(sml[:, :], small).then_inc(small_in, 16)
            splits(1)
            a.wait_ge(const_in, 16)
            norm(0, scratch=u[:, 0, 0:DM])
            turn_hi(0, 0)
            turn_hi(0, 1)
            splits(SPL)
            for i in range(2):
                a.wait_ge(tp_ps, GROUP["ple"] + i + 1)
                a.activation(pT_hi[:, i].rearrange("p k (t c) -> p t k c", t=NT),
                             ps[:, bank(GROUP["ple"] + i), :].rearrange("p (t k c) -> p t k c", t=NT, k=PLE // P),
                             ACT.Copy).then_inc(tp_hi, 1)
            a.wait_ge(small_in, 16)
            a.activation(rt[:, :, 0:NE], par("router", a=DM // P), ACT.Copy).then_inc(rt_done, 1)
            a.wait_ge(setup, 2)
            a.activation(c8[:, 1, :], c8[:, 0, :], ACT.Exp, scale=-1.0).then_inc(setup, 1)
            a.wait_ge(setup, 4)
            a.activation(c8[:, 3, :], c8[:, 2, :], ACT.Ln).then_inc(setup, 1)

            def project(name):
                b = {"kv_qi": U_K, "ki_wi": U_KI, "q": U_Q, "xr": U_XR, "xg": U_XG}[name]
                normed(u[:, :, b:b + chunks[name].width], taken(name), ACT.Copy, 0).then_inc(chunk_act, 1)
                splits(ends[chunks[name].last] + SPL)

            def turned(ready, n, bank, dst, done):
                a.wait_ge(ready, n + 1)
                a.activation(dst, ps[:, bank, :].rearrange("p (k c) -> p k c", k=4), ACT.Copy).then_inc(done, 1)

            def indexed(t):
                if t:
                    a.wait_ge(ix_relu, t + 1)
                a.wait_ge(ix_ps, t + 1)
                keys = (t + 1) * P
                src = ps[:, 4, :].rearrange("p (h k) -> p h k", h=4) if t == 0 else \
                    ps[:, 5:7, :].rearrange("p b (h k) -> p (b h) k", h=2)
                a.activation(relu[:, :, 0:keys], src, ACT.Relu, scale=HD ** -0.5).then_inc(ix_relu, 1)

            project("ki_wi")
            project("kv_qi")
            project("xr")
            turned(at_ps, 0, 4, kqT[:, 4:8, tok(0)], at_sb)
            turned(at_ps, 1, 5, kqT[:, 4:8, tok(1)], at_sb)
            turned(at_ps, 2, 6, kqT[:, 0:4, tok(0)], at_sb)
            turned(at_ps, 3, 7, kqT[:, 0:4, tok(1)], at_sb)
            indexed(0)
            turned(lt_ps, 0, 7, xrT[:, :, 3:3 + P], lt_sb)
            indexed(1)
            project("q")
            turned(lt_ps, 1, 4, xrT[:, :, 3 + P:3 + 2 * P], lt_sb)
            turned(at_ps, 4, 5, qT[:, :, tok(0)], at_sb)
            turned(at_ps, 5, 6, qT[:, :, tok(1)], at_sb)
            project("xg")
            def exps(s):
                a.wait_ge(lg_sb, s + 1)
                keys = (s // 2 + 1) * P
                for j in range(4):
                    ins = a.activation(probs[:, s % 2, j, 0:keys], probs[:, s % 2, j, 0:keys], ACT.Exp,
                                       bias=nmax[:, s, j:j + 1], accum_out=rsum[:, s, j:j + 1])
                ins.then_inc(pr_sb, 1)

            def turned_probs(s):
                a.wait_ge(pt_ps, s + 1)
                n = 4 * (s // 2 + 1)
                if s == 0:
                    src = ps[:, 2, :]
                elif s == 1:
                    src = ps[:, 3, :]
                else:
                    src = ps[:, 2:4, :].rearrange("p b c -> p (b c)")
                if s:
                    a.wait_ge(o_ps, s)
                else:
                    a.wait_ge(ix_relu, 4)
                a.activation(prT[:, 0:n, :], src.rearrange("p (k c) -> p k c", k=n), ACT.Copy).then_inc(pt_sb, 1)

            for n, (dst, bias) in enumerate(((gr, par("lru_ba")), (gi, par("lru_bx")))):
                a.wait_ge(gate_ps, n + 1)
                for k in range(LRU_K):
                    ins = a.activation(dst[:, k, :], ps[:, 2 + 2 * n + k // 2, (k % 2) * SEQ:(k % 2 + 1) * SEQ], ACT.Sigmoid,
                                       bias=bias[:, k:k + 1])
                ins.then_inc(gate_sb, 1)
            exps(0)
            exps(1)
            turned(lt_ps, 2, 0, xgT[:, :, tok(0)], lt_sb)
            turned(lt_ps, 3, 1, xgT[:, :, tok(1)], lt_sb)
            a.wait_ge(gate_sb, 2)
            a.wait_ge(setup, 7)
            for k in range(LRU_K):
                ins = a.activation(la[:, k, :], gr[:, k, :], ACT.Exp, scale=c8[:, 6, k:k + 1])
            ins.then_inc(lru_a, 1)
            a.wait_ge(lru_a, 1)
            for k in range(LRU_K):
                ins = a.activation(gr[:, k, :], gr[:, k, :], ACT.Tanh, scale=c8[:, 7, k:k + 1])
            ins.then_inc(lru_a, 1)
            turned_probs(0)
            turned_probs(1)
            exps(2)
            turned_probs(2)
            exps(3)
            a.wait_ge(lru_b1, 1)
            a.activation(gr[:, :, :], gr[:, :, :], ACT.Sqrt).then_inc(lru_bs, 1)
            turned_probs(3)
            a.wait_ge(lt_sb, 4)
            a.activation(xgT[:, :, :], xgT[:, :, :], ACT.Gelu_apprx_tanh).then_inc(lru_gelu, 1)
            a.wait_ge(lru_y, 1)
            a.activation(xT_hi[:, 4:8, :], la[:, :, :], ACT.Copy).then_inc(lru_hi, 1)
            splits(ends[chunks["xg"].last] + SPL + 2)
            for t in range(NT):
                group_hi(GROUP["o_attn"] + t, xT_hi[:, 0:4, tok(t)])
            splits(ends[chunks["e_out0"].last] + LAG)
            turn_hi(1, 0)
            splits(ends[chunks["e_out1"].last] + LAG)

            def silu(s, nt, used, count, j):
                a.wait_ge(s.half_used, used)
                if j >= 2:
                    a.wait_ge(s.prod, count + (j - 1))
                if nt == NT:
                    normed(sg[:, j % 2], ps[:, 0:nt, :], ACT.Silu, 1).then_inc(s.silu, 1)
                else:
                    a.activation(sg[:, j % 2, 0:nt, :], ps[:, 0:nt, :], ACT.Silu).then_inc(s.silu, 1)

            def aT_part_hi(s, nt, count, j):
                a.wait_ge(s.aT_ps, count + (j + 1))
                bank = 0 if nt == 2 else 4 + j % 2
                dst = aT_hi[:, j % 2, :, 0:nt * P].rearrange("p k (t c) -> p t k c", t=nt)
                a.activation(dst, ps[:, bank:bank + nt, :].rearrange("p t (k c) -> p t k c", k=4),
                             ACT.Copy).then_inc(s.aT_hi, 1)

            norm(1, u[:, 0, 0:DM])
            turn_hi(1, 1)
            preload(ACT.Silu)
            base = starts["ffn"]
            for j in range(FCH):
                g1 = base + FFN_AT["g", j, 1]
                splits(ends[g1] + LAG)
                silu(dense, NT, ends[g1], 0, j)
                if j:
                    splits(ends[base + FFN_AT["u", j, 1]] + LAG)
                    aT_part_hi(dense, NT, 0, j - 1)
            splits(ends[base + FFN_AT["d", FCH - 2, 1]] + LAG)
            aT_part_hi(dense, NT, 0, FCH - 1)
            splits(ends[base + NEXP - 2] + LAG)
            turn_hi(2, 0)
            splits(ends[base + NEXP - 1] + LAG)

            def embed(layer, half):
                src = taken(f"{layer}_emb{half}")
                a.activation(emb[:, :, half * WC:(half + 1) * WC], src, ACT.Copy).then_inc(chunk_act, 1)

            def embed_gate(layer, n, half):
                normed(sg[:, half], taken(f"{layer}_gate{half}"), ACT.Sigmoid, n).then_inc(chunk_act, 1)

            scratch = act[:, :, :, :].rearrange("p a t n -> p (a t n)")[:, 0:DM]
            norm(2, scratch)
            embed("e", 0)
            turn_hi(2, 1)
            preload(ACT.Sigmoid)
            embed("e", 1)
            embed_gate("e", 2, 0)
            turn_hi(3, 0)
            embed_gate("e", 2, 1)

            norm(3, xt[:, 0, 0:DM])
            turn_hi(3, 1)
            preload(ACT.Exp)

            def stage_in(q, name):
                src = taken(name)
                if q >= 2:
                    a.wait_ge(fw_ps, q - 1)
                elif q == 0:
                    a.wait_ge(tp_ps, GROUP["o_mix"] + 4)
                normed(hn[:, :, (q % 2) * WC:(q % 2 + 1) * WC], src, ACT.Copy, 3).then_inc(chunk_act, 1)

            stage_in(0, "B")
            normed(dts[:, 0], taken("dt"), ACT.Copy, 3).then_inc(chunk_act, 1)
            splits(ends[chunks["dt"].last] + SPL)
            a.wait_ge(dt_abs, 1)
            a.activation(dts[:, 2, :, :], dts[:, 1, :, :], ACT.Exp, scale=-1.0).then_inc(dt_exp, 1)
            a.activation(dts[:, 5, 0, :], par("a_log"), ACT.Exp).then_inc(dt_exp, 1)
            a.wait_ge(dt_ln, 1)
            a.activation(dts[:, 3, :, :], dts[:, 1, :, :], ACT.Ln).then_inc(dt_ln, 1)

            def forward_out(q):
                a.wait_ge(fw_ps, q + 1)
                if q >= 2:
                    a.wait_ge(cv_raw, q - 1)
                dst = pre[:, q % 2, :, 3:3 + SEQ].rearrange("p k (t c) -> p t k c", t=NT)
                b = 4 + 2 * (q % 2)
                a.activation(dst, ps[:, b:b + 2, :].rearrange("p t (k c) -> p t k c", k=4), ACT.Copy).then_inc(fw_sb, 1)

            def conv_silu(q):
                a.wait_ge(cv_raw, q + 1)
                dst = BT if q == 0 else CT if q == 1 else cv[:, q % 2]
                dst = dst[:, :, :]
                a.activation(dst, cv[:, q % 2, :, :], ACT.Silu).then_inc(cv_done, 1)

            def backward_out(n):
                a.wait_ge(bk_ps, n + 1)
                if n == 0:
                    a.activation(Btok[:, :, :], ps[:, 4, :].rearrange("p (k c) -> p k c", k=4), ACT.Copy).then_inc(bk_sb, 1)
                else:
                    q = n + 1
                    b = 4 + 2 * (q % 2)
                    a.activation(xt[:, :, (n - 1) * WC:n * WC], ps[:, b:b + 2, :], ACT.Copy).then_inc(bk_sb, 1)

            def split_next(name, count=LAG):
                splits(ends[chunks[name].last] + count)

            def z_silu(j):
                src = taken(f"z{j}")
                normed(zt[:, :, j * WC:(j + 1) * WC], src, ACT.Silu, 3).then_inc(chunk_act, 1)

            a.wait_ge(dt_da, 1)
            following = ["C", "x0", "x1", "x2", "x3", "z0", "z1"]
            for q in range(6):
                split_next(following[q])
                if q:
                    conv_silu(q - 1)
                split_next(following[q], SPL)
                if q < 5:
                    stage_in(q + 1, following[q])
                else:
                    z_silu(0)
                forward_out(q)
                if q == 0:
                    a.wait_ge(cum_ps, 1)
                    a.activation(cumT[0:3 * SH, :], ps[0:3 * SH, 7, 0:SEQ], ACT.Copy).then_inc(cumT_part, 1)
                elif q == 1:
                    a.wait_ge(cumT_part, 2)
                    for r in (slice(SH, 2 * SH), slice(2 * SH, 3 * SH)):
                        ins = a.activation(cumT[r, :], cumT_rest[r, :], ACT.Copy)
                    ins.then_inc(cumT_part, 1)
                    a.wait_ge(cum_sb, 2)
                    a.activation(dec[:, 0, :], dec[:, 0, :], ACT.Exp).then_inc(cum_exp, 1)
                    a.activation(dec[:, 1, :], cum[:, 1, :], ACT.Exp).then_inc(cum_exp, 1)
                if q == 1:
                    backward_out(0)
                elif q >= 3:
                    backward_out(q - 2)
            split_next("z1")
            conv_silu(5)
            z_silu(1)
            backward_out(4)

            def decays(i):
                a.wait_ge(seg_ps, i + 1)
                if i == 0:
                    a.wait_ge(bk_ps, 5)
                elif i >= 2:
                    a.wait_ge(y_ps, i - 1)
                b = 2 + 2 * (i % 2)
                for j in range(HPU):
                    for c in range(NT):
                        hd = i * HPU + j
                        ins = a.activation(segs[:, i % 2, j, c, :],
                                           ps[:, b + j // 2, (j % 2) * SEQ + c * P:(j % 2) * SEQ + (c + 1) * P],
                                           ACT.Relu, scale=-1.0, bias=cum[:, c, hd:hd + 1])
                ins.then_inc(seg_relu, 1)
                a.wait_ge(seg_relu, i + 1)
                a.activation(segs[:, i % 2], segs[:, i % 2], ACT.Exp, scale=-1.0).then_inc(seg_exp, 1)

            def state_out(i):
                a.wait_ge(st_ps, i + 1)
                a.activation(st[:, i % 2, :], ps[:, 7, 0:UW], ACT.Copy).then_inc(st_sb, 1)

            def squares(g):
                a.wait_ge(y_done, 2 * g + 2)
                for c in range(NT):
                    step(a.activation(hn[:, 0, 0:WC], xt[:, c, g * WC:(g + 1) * WC], ACT.Square,
                                      accum_out=gss[:, 0, c, g:g + 1]))

            decays(0)
            z_silu(2)
            decays(1)
            for i in range(2, UNITS):
                if i == 4:
                    z_silu(3)
                state_out(i - 2)
                decays(i)
                if i >= 4 and i % 2 == 1:
                    squares((i - 5) // 2)
            split_next("z3")
            state_out(UNITS - 2)
            squares(2)

            def roots(gs):
                a.activation(gss[:, 1, :, gs], gss[:, 0, :, gs], ACT.Sqrt, scale=1.0 / WC, bias=eps).then_inc(grms, 1)

            def y_hi_part(n):
                x = (xT_hi if n // 2 < 2 else yT_hi)
                group_hi(GROUP["ssd"] + n, x[:, 4 * (n // 2 % 2):4 * (n // 2 % 2) + 4, tok(n % 2)])

            roots(slice(0, GROUPS - 1))
            state_out(UNITS - 1)
            y_hi_part(0)
            squares(3)
            roots(slice(GROUPS - 1, GROUPS))
            for n in range(1, 6):
                y_hi_part(n)
            splits(ends[chunks["o_out0"].first] + LAG)
            y_hi_part(6)
            y_hi_part(7)
            splits(ends[chunks["o_out1"].first] + LAG)
            turn_hi(4, 0)
            splits(ends[chunks["o_out1"].last] + LAG)
            norm(4, scratch)
            embed("o", 0)
            turn_hi(4, 1)
            normed(hn_hi, hn, ACT.Copy, 4).then_inc(hn_split, 1)
            preload(ACT.Exp)
            a.wait_ge(lw_max, 1)
            a.activation(gw[:, 1, :], gw[:, 0, :], ACT.Exp).then_inc(lw_exp, 1)
            preload(ACT.Silu)
            embed("o", 1)

            def expert_splits(s, base, e):
                first = ends[base - 1] if base else 0
                e_is_first = isinstance(e, int)
                done = [0]

                def ahead(upto):
                    while done[0] < min(upto, NHALF):
                        q = first + done[0]
                        i = base + done[0] // 2
                        k = HK * (done[0] % 2)
                        n = i - base
                        if s is main and e_is_first and n in AHEAD:
                            a.wait_ge(ahead_in[n], 16)
                        else:
                            r = place_of(s, e_is_first, i, n)
                            a.wait_ge(s.raw_in[r % RAW], (e * (NEXP // RAW) + (r // RAW + 1)) * 16)
                        if q >= SPL or not e_is_first:
                            a.wait_ge(s.half_used, e * NHALF + (q - SPL + 1))
                        a.activation(whi[:, q % SPL, :, :], landing(s, e_is_first, i, n)[:, k:k + HK, :],
                                     ACT.Copy).then_inc(s.hi_done, 1)
                        done[0] += 1
                return first, ahead

            def end(step_):
                return 2 * (FFN_AT[step_] + 1)

            def copy_tokens(s, count):
                a.wait_ge(s.xe_raw, count)
                a.activation(xe_tok[:, :], ps[:, 6:8, :].rearrange("p b c -> p (b c)"), ACT.Copy).then_inc(s.xe_tok, 1)

            def take_tokens_hi(s, count):
                a.wait_ge(s.xe_ps, count)
                a.activation(xT_hi[:, :, 0:P], ps[:, 6:8, :].rearrange("p b (k c) -> p (b k) c", k=4),
                             ACT.Copy).then_inc(s.xe_hi, 1)

            def result_hi(s, used, count):
                a.wait_ge(s.half_used, used)
                a.activation(y_hi[:, :], ps[:, 2:4, :].rearrange("p b c -> p (b c)"), ACT.Copy).then_inc(s.y_hi, 1)

            def expert(s, base, e, peeled):
                first, ahead = expert_splits(s, base, e)
                shift, count = e * NHALF + first, e * FCH
                ahead(SPL)
                if peeled:
                    copy_tokens(s, 1)
                    take_tokens_hi(s, 1)
                else:
                    result_hi(s, shift, e)
                ahead(end(("g", 0, 1)) + LAG)
                silu(s, 1, shift + end(("g", 0, 1)), count, 0)
                ahead(end(("u", 0, 1)) + LAG)
                a.wait_ge(s.selT_ps, e + 1)
                a.activation(selT[:, :], ps[:, 5, 0:NT * P], ACT.Copy).then_inc(s.selT_sb, 1)
                for j in range(1, FCH):
                    ahead(end(("g", j, 1)) + LAG)
                    silu(s, 1, shift + end(("g", j, 1)), count, j)
                    ahead(end(("u", j, 1)) + LAG)
                    aT_part_hi(s, 1, count, j - 1)
                ahead(end(("d", FCH - 3, 1)) + LAG)
                copy_tokens(s, e + 2)
                ahead(end(("d", FCH - 2, 1)) + LAG)
                aT_part_hi(s, 1, count, FCH - 1)
                take_tokens_hi(s, e + 2)
                ahead(NHALF)

            def experts_act(s, base):
                first = ends[base - 1] if base else 0
                expert(s, base, 0, True)
                with a.Fori(1, NE) as e:
                    expert(s, base, e, False)
                result_hi(s, NE * NHALF + first, NE)

            experts_act(main, starts["experts"])
            a.wait_ge(flag_set, 1)
            some = a.value_load(flag[0:1, 0:1], min_val=0, max_val=1)
            with a.If(some != 0):
                experts_act(rest, 0)
            sent[0] = ends[starts["experts"] + NE * NEXP - 1]
            splits(ends[chunks["o_gate0"].first])
            norm(5, scratch)
            turn_hi(5, 0)
            turn_hi(5, 1)
            preload(ACT.Sigmoid)
            embed_gate("o", 5, 0)
            embed_gate("o", 5, 1)
            a.activation(warm[:, 0:1], eps, ACT.Sqrt)
            for t in range(NT):
                a.wait_ge(gate_ple, 5 + t)
                step(a.activation(scratch, h[:, t, :], ACT.Square, accum_out=stat[:, 0, t:t + 1]))
                a.activation(stat[:, 1, t:t + 1], stat[:, 0, t:t + 1], ACT.Sqrt, scale=1.0 / DM, bias=eps).then_inc(rms, 1)

        @block.vector
        def _(v):
            sent = [0]
            steps = [0]

            def step(ins):
                steps[0] += 1
                ins.then_inc(dve_seq, 1)
                v.wait_ge(dve_seq, steps[0])

            def splits(upto):
                while sent[0] < min(upto, len(halves)) and panels[halves[sent[0]][0]] is not None:
                    q = sent[0]
                    i, k = halves[q]
                    n, width = min(HK, panels[i][2] - k), panels[i][4]
                    v.wait_ge(hi_done, q + 1)
                    v.tensor_tensor(wlo[:, q % SPL, 0:n, 0:width], raw[:, ring(starts, i) % RAW, k:k + n, 0:width],
                                    whi[:, q % SPL, 0:n, 0:width], ALU.subtract).then_inc(lo_done, 1)
                    sent[0] += 1

            def taken(name):
                c = chunks[name]
                splits(ends[c.last] + LAG)
                v.wait_ge(half_used, ends[c.last])
                return ps[:, c.banks:c.banks + 2, 0:c.width]

            def scaled(n, half, used=0):
                v.wait_ge(*((gain_in, 16 * n) if n else (gain0_in, 16)))
                if used:
                    v.wait_ge(tp_ps, used)
                cols = slice(half * WC, (half + 1) * WC)
                for t in range(NT):
                    v.tensor_tensor(hn[:, t, cols], h[:, t, cols], gain[:, cols], ALU.mult).then_inc(hg_ready, 1)

            def factor(n):
                v.wait_ge(rms, n + 1)
                v.reciprocal(stat[:, 2, :], stat[:, 1, :]).then_inc(rstd_ready, 1)

            def group_lo(g, dst, high):
                v.wait_ge(tp_hi, g + 1)
                v.tensor_tensor(dst, ps[:, bank(g), :].rearrange("p (k c) -> p k c", k=4), high,
                                ALU.subtract).then_inc(tp_lo, 1)

            def turn_lo(n, half):
                for t in range(NT):
                    hi, lo = (x[:, 4 * half:4 * half + 4, tok(t)] for x in left_of[n])
                    group_lo(GROUP[NORMS[n]] + 2 * half + t, lo, hi)

            v.wait_ge(x_in, 16)
            scaled(0, 0)
            scaled(0, 1)
            factor(0)
            turn_lo(0, 0)
            turn_lo(0, 1)
            splits(SPL)
            step(v.memset(xrT[:, :, 0:3], 0.0))
            step(v.memset(bd[:, :, :, :], 0.0))
            step(v.memset(kdup[:, :, :, :, :, :], 0.0))
            v.tensor_copy(ident_r[:, :], ident).then_inc(setup, 1)
            v.wait_ge(small_in, 16)
            for n, name in enumerate(("lru_wa", "lru_wx")):
                src = par(name, a=LRU_K)
                v.tensor_copy(bd[0:HD, n, :, 0:HD], src[0:HD])
                step(v.tensor_copy(bd[HD:P, n, :, HD:P], src[HD:P]))
            step(v.tensor_scalar(c8[:, 4, :], par("lam"), -1.0, None, ALU.mult))
            v.tensor_tensor(c8[:, 0, :], c8[:, 4, :], par("lam"), ALU.max).then_inc(setup, 1)
            for i in range(2):
                v.wait_ge(tp_hi, GROUP["ple"] + i + 1)
                v.tensor_tensor(pT_lo[:, i].rearrange("p k (t c) -> p t k c", t=NT),
                                ps[:, bank(GROUP["ple"] + i), :].rearrange("p (t k c) -> p t k c", t=NT, k=PLE // P),
                                pT_hi[:, i].rearrange("p k (t c) -> p t k c", t=NT), ALU.subtract).then_inc(tp_lo, 1)
            v.wait_ge(rt_done, 1)
            v.tensor_tensor(rt[:, :, NE:2 * NE], par("router", a=DM // P), rt[:, :, 0:NE], ALU.subtract).then_inc(rt_done, 1)
            v.wait_ge(setup, 3)
            v.tensor_scalar(c8[:, 2, :], c8[:, 1, :], 1.0, None, ALU.add).then_inc(setup, 1)
            v.wait_ge(setup, 5)
            step(v.tensor_scalar(c8[:, 5, :], c8[:, 2, :], -1.0, 1e-30, ALU.add, ALU.max))
            step(v.tensor_scalar(c8[:, 6, :], c8[:, 2, :], 1.0, None, ALU.is_equal))
            step(v.reciprocal(c8[:, 5, :], c8[:, 5, :]))
            step(v.tensor_tensor(c8[:, 3, :], c8[:, 3, :], c8[:, 1, :], ALU.mult))
            step(v.tensor_tensor(c8[:, 3, :], c8[:, 3, :], c8[:, 5, :], ALU.mult))
            step(v.tensor_tensor(c8[:, 6, :], c8[:, 6, :], c8[:, 1, :], ALU.mult))
            step(v.tensor_tensor(c8[:, 3, :], c8[:, 3, :], c8[:, 6, :], ALU.add))
            step(v.tensor_scalar(c8[:, 4, :], c8[:, 4, :], 0.0, None, ALU.max))
            step(v.tensor_tensor(c8[:, 3, :], c8[:, 3, :], c8[:, 4, :], ALU.add))
            v.memset(warm[:, 4:5], 0.0).then_inc(setup, 1)
            step(v.tensor_scalar(c8[:, 6, :], c8[:, 3, :], -8.0, None, ALU.mult))
            v.tensor_scalar(c8[:, 7, :], c8[:, 3, :], 8.0, None, ALU.mult).then_inc(setup, 1)
            splits(ends[chunks["kv_qi"].last] + LAG)

            def rope(base, nh):
                head = u[:, :, base:base + nh * HD].rearrange("p t (h d) -> p t h d", h=nh)
                for t in range(NT):
                    x1, x2 = head[:, t, :, 0:ROT], head[:, t, :, ROT:2 * ROT]
                    r = [rot[:, i, t, 0:nh, :] for i in range(4)]
                    c = cos[:, t, :].unsqueeze(1).to_broadcast([P, nh, ROT])
                    s = sin[:, t, :].unsqueeze(1).to_broadcast([P, nh, ROT])
                    v.tensor_tensor(r[0], x1, c, ALU.mult)
                    v.tensor_tensor(r[1], x2, s, ALU.mult)
                    v.tensor_tensor(r[2], x1, s, ALU.mult)
                    step(v.tensor_tensor(r[3], x2, c, ALU.mult))
                    v.tensor_tensor(x1, r[0], r[1], ALU.subtract)
                    ins = v.tensor_tensor(x2, r[2], r[3], ALU.add)
                    if t == 0:
                        step(ins)
                return ins

            v.wait_ge(chunk_act, 2)
            step(rope(U_QI, IDXH + 1))
            step(rope(U_K, KVH))
            for t in range(NT):
                for r in range(2):
                    v.tensor_copy(kdup[:, t, 0:KVH, r, r, :], u[:, t, U_K:U_V].rearrange("p (g d) -> p g d", g=KVH))
                    ins = v.tensor_copy(kdup[:, t, KVH, r, r, :], u[:, t, U_KI:U_WI])
            ins.then_inc(roped, 1)
            step(v.tensor_scalar(wi2[:, :, :], u[:, :, U_WI:U_XG], IDXH ** -0.5, None, ALU.mult))
            splits(ends[chunks["xr"].last] + LAG)

            def scores(t):
                keys = (t + 1) * P
                v.wait_ge(ix_relu, 2 * t + 1)
                step(v.tensor_scalar(score[:, t, 0:keys], relu[:, 0, 0:keys], wi2[:, t, 0:1], None, ALU.mult))
                for j in range(1, IDXH):
                    ins = v.scalar_tensor_tensor(score[:, t, 0:keys], relu[:, j, 0:keys], wi2[:, t, j:j + 1],
                                                 score[:, t, 0:keys], ALU.mult, ALU.add)
                    if j < IDXH - 1:
                        step(ins)
                ins.then_inc(ix_relu, 1)
                v.wait_ge(ix_relu, 2 * t + 2)
                step(v.tensor_tensor(score[:, t, t * P:keys], score[:, t, t * P:keys], cmask, ALU.add))

            def best(t, rounds):
                keys = (t + 1) * P
                for n in rounds:
                    cur = work[:, 0:keys] if n else score[:, t, 0:keys]
                    step(v.max(top8[:, :], cur))
                    step(v.match_replace(work[:, 0:keys], top8[:, :], cur, REPLACED))

            def kept(t):
                keys = (t + 1) * P
                step(v.tensor_tensor(keep[:, t, 0:keys], work[:, 0:keys], score[:, t, 0:keys], ALU.is_equal))
                step(v.tensor_scalar(keep[:, t, 0:keys], keep[:, t, 0:keys], NEG, None, ALU.mult))
                step(v.tensor_tensor(keep[:, t, t * P:keys], keep[:, t, t * P:keys], cmask, ALU.add))

            def masked(s):
                t, keys = s // 2, (s // 2 + 1) * P
                v.wait_ge(lg_ps, s + 1)
                if s >= 2:
                    v.wait_ge(pt_ps, s - 1)
                src = (ps[:, 6, :], ps[:, 7, :], ps[:, 0:2, :], ps[:, 6:8, :])[s]
                src = src.rearrange("p (h k) -> p h k", h=4) if t == 0 else src.rearrange("p b (h k) -> p (b h) k", h=2)
                dst = probs[:, s % 2, :, 0:keys]
                step(v.scalar_tensor_tensor(dst, src, HD ** -0.5, keep[:, t, 0:keys].unsqueeze(1).to_broadcast([P, 4, keys]),
                                            ALU.mult, ALU.add))
                v.tensor_reduce(nmax[:, s, :], dst, AX, ALU.max, negate=True).then_inc(lg_sb, 1)

            def attended(t):
                v.wait_ge(pr_sb, 2 * t + 2)
                v.wait_ge(o_ps, 2 * t + 2)
                step(v.reciprocal(rinv[:, 2 * t:2 * t + 2, :], rsum[:, 2 * t:2 * t + 2, :]))
                r = rinv[:, 2 * t:2 * t + 2, :].rearrange("p a b -> p (a b)").unsqueeze(2).to_broadcast([P, HEADS, HD])
                v.tensor_tensor(hn[:, t, 0:HEADS * HD].rearrange("p (h d) -> p h d", h=HEADS),
                                ps[:, 4 + t, :].rearrange("p (h d) -> p h d", h=HEADS), r, ALU.mult).then_inc(o_sb, 1)

            rounds = NSEL // 8
            splits(ends[chunks["q"].last])
            scores(0)
            best(0, range(rounds // 2))
            splits(ends[chunks["q"].last] + 1)
            best(0, range(rounds // 2, rounds))
            kept(0)
            splits(ends[chunks["q"].last] + 3)
            v.wait_ge(chunk_act, 4)
            rope(U_Q, HEADS).then_inc(roped, 1)
            splits(ends[chunks["xg"].last])
            v.wait_ge(lt_sb, 2)
            cw = par("lru_w", a=LRU_K)
            for j in (3, 0, 1, 2):
                for k in range(CONV_DVE):
                    if j == 3:
                        ins = v.tensor_scalar(xc[:, k, :], xrT[:, k, 3:3 + SEQ], cw[:, k, 3:4], par("lru_b")[:, k:k + 1],
                                              ALU.mult, ALU.add)
                    else:
                        ins = v.scalar_tensor_tensor(xc[:, k, :], xrT[:, k, j:j + SEQ], cw[:, k, j:j + 1], xc[:, k, :],
                                                     ALU.mult, ALU.add)
                if j != 2:
                    step(ins)
            ins.then_inc(conv_done, 1)
            scores(1)
            best(1, range(rounds // 2))
            masked(0)
            masked(1)
            best(1, range(rounds // 2, rounds))
            kept(1)
            masked(2)
            splits(ends[chunks["xg"].last] + SPL)
            masked(3)

            v.wait_ge(lru_a, 2)
            v.wait_ge(gate_ps, 2)
            aa = xrT[:, :, 0:SEQ]
            step(v.tensor_tensor(aa, la[:, :, :], la[:, :, :], ALU.mult))
            v.scalar_tensor_tensor(gr[:, :, :], aa, 1.0, gr[:, :, :], ALU.add, ALU.mult).then_inc(lru_b1, 1)
            step(v.tensor_tensor(gi[:, :, :], gi[:, :, :], xc[:, :, :], ALU.mult))
            v.wait_ge(lru_bs, 1)
            step(v.tensor_tensor(gi[:, :, :], gi[:, :, :], gr[:, :, :], ALU.mult))
            for k in range(LRU_K):
                ins = v.tensor_tensor_scan(aa[:, k, :], la[:, k, :], gi[:, k, :], 0.0, ALU.mult, ALU.add)
            step(ins)
            v.wait_ge(lru_gelu, 1)
            v.tensor_tensor(la[:, :, :], aa, xgT[:, :, :], ALU.mult).then_inc(lru_y, 1)
            v.wait_ge(lru_y, 1)
            attended(0)
            v.wait_ge(lru_hi, 1)
            v.tensor_tensor(xT_lo[:, 4:8, :], la[:, :, :], xT_hi[:, 4:8, :], ALU.subtract).then_inc(lru_lo, 1)

            attended(1)
            splits(ends[chunks["xg"].last] + SPL + 2)
            for t in range(NT):
                group_lo(GROUP["o_attn"] + t, xT_lo[:, 0:4, tok(t)], xT_hi[:, 0:4, tok(t)])

            def add_out(name, half):
                src = taken(name)
                dst = h[:, :, half * WC:(half + 1) * WC]
                v.tensor_tensor(dst, dst, src, ALU.add).then_inc(chunk_dve, 1)

            add_out("e_out0", 0)
            v.wait_ge(chunk_dve, 1)
            scaled(1, 0, GROUP["o_attn"] + 2)
            turn_lo(1, 0)
            add_out("e_out1", 1)

            def prod(s, nt, count_used, count, j):
                v.wait_ge(s.half_used, count_used)
                v.wait_ge(s.silu, count + 1)
                ub = 2 if nt == 2 else 1
                if nt == NT:
                    for t in range(NT):
                        ins = v.scalar_tensor_tensor(act[:, j % 2, t, :], ps[:, ub + t, :], stat[:, 2, t:t + 1],
                                                     sg[:, j % 2, t, :], ALU.mult, ALU.mult)
                    ins.then_inc(s.prod, 1)
                else:
                    v.tensor_tensor(act[:, j % 2, 0:nt, :], sg[:, j % 2, 0:nt, :], ps[:, ub:ub + nt, :],
                                    ALU.mult).then_inc(s.prod, 1)

            def aT_part_lo(s, nt, count, j):
                v.wait_ge(s.aT_hi, count + 1)
                bank = 0 if nt == 2 else 4 + j % 2
                view = [b[:, j % 2, :, 0:nt * P].rearrange("p k (t c) -> p t k c", t=nt) for b in (aT_lo, aT_hi)]
                v.tensor_tensor(view[0], ps[:, bank:bank + nt, :].rearrange("p t (k c) -> p t k c", k=4), view[1],
                                ALU.subtract).then_inc(s.aT_lo, 1)

            v.wait_ge(chunk_dve, 2)
            scaled(1, 1)
            factor(1)
            turn_lo(1, 1)
            base = starts["ffn"]
            for j in range(FCH):
                u1 = base + FFN_AT["u", j, 1]
                splits(ends[u1] + LAG)
                if j >= 2:
                    v.wait_ge(dense.aT_ps, j - 1)
                prod(dense, NT, ends[u1], j, j)
                if j:
                    aT_part_lo(dense, NT, j - 1, j - 1)
            splits(ends[base + FFN_AT["d", FCH - 2, 1]] + LAG)
            aT_part_lo(dense, NT, FCH - 1, FCH - 1)
            for half in range(2):
                last = base + NEXP - 2 + half
                cols = slice(half * WC, (half + 1) * WC)
                splits(ends[last] + LAG)
                v.wait_ge(half_used, ends[last])
                for t in range(NT):
                    ins = v.tensor_tensor(h[:, t, cols], h[:, t, cols], ps[:, 4 + 2 * t + half, :], ALU.add)
                ins.then_inc(dense.summed, 1)
                v.wait_ge(dense.summed, half + 1)
                scaled(2, half, GROUP["e_ffn"] + 4)
                if half == 0:
                    turn_lo(2, 0)

            def ple(layer, half):
                c = chunks[f"{layer}_gate{half}"]
                splits(ends[c.last] + LAG)
                v.wait_ge(*evacuated(c.number))
                cols = slice(half * WC, (half + 1) * WC)
                step(v.tensor_tensor(emb[:, :, cols], emb[:, :, cols], sg[:, half, :, :], ALU.mult))
                v.tensor_tensor(h[:, :, cols], h[:, :, cols], emb[:, :, cols], ALU.add).then_inc(gate_ple, 1)

            splits(ends[chunks["e_emb0"].last] + LAG)
            factor(2)
            turn_lo(2, 1)
            splits(ends[chunks["e_emb1"].last] + LAG)
            ple("e", 0)
            v.wait_ge(gate_ple, 1)
            scaled(3, 0, GROUP["e_ple"] + 4)
            turn_lo(3, 0)
            ple("e", 1)

            v.wait_ge(gate_ple, 2)
            scaled(3, 1)
            factor(3)
            turn_lo(3, 1)
            c = chunks["dt"]
            splits(ends[c.last] + LAG)
            v.memset(pre[:, :, :, 0:3], 0.0)
            v.wait_ge(*evacuated(c.number))
            raw_dt, d1, d2, d3, d4, d5 = (dts[:, i, :, :] for i in range(6))
            step(v.tensor_tensor(raw_dt, raw_dt, par("dt_bias").unsqueeze(1).to_broadcast([P, NT, SH]), ALU.add))
            step(v.tensor_scalar(d3, raw_dt, -1.0, None, ALU.mult))
            v.tensor_tensor(d1, raw_dt, d3, ALU.max).then_inc(dt_abs, 1)
            v.wait_ge(dt_abs, 1)
            v.wait_ge(dt_exp, 1)
            v.tensor_scalar(d1, d2, 1.0, None, ALU.add).then_inc(dt_ln, 1)
            v.wait_ge(dt_ln, 2)
            step(v.tensor_scalar(d4, d1, -1.0, 1e-30, ALU.add, ALU.max))
            step(v.reciprocal(d4, d4))
            step(v.tensor_tensor(d3, d3, d2, ALU.mult))
            step(v.tensor_tensor(d3, d3, d4, ALU.mult))
            step(v.tensor_scalar(d4, d1, 1.0, None, ALU.is_equal))
            step(v.tensor_tensor(d4, d4, d2, ALU.mult))
            step(v.tensor_tensor(d3, d3, d4, ALU.add))
            step(v.tensor_scalar(raw_dt, raw_dt, 0.0, None, ALU.max))
            step(v.tensor_tensor(raw_dt, raw_dt, d3, ALU.add))
            v.wait_ge(dt_exp, 2)
            step(v.tensor_scalar(dts[:, 5, 0, :], dts[:, 5, 0, :], -1.0, None, ALU.mult))
            step(v.tensor_tensor(d1, raw_dt, dts[:, 5, 0, :].unsqueeze(1).to_broadcast([P, NT, SH]), ALU.mult))
            v.tensor_copy(da3[:, :, :, :], d1.unsqueeze(2).to_broadcast([P, NT, 3, SH])).then_inc(dt_da, 1)

            def convolve(q):
                v.wait_ge(fw_sb, q + 1)
                if q >= 2:
                    if q < 4:
                        v.wait_ge(cv_done, q - 1)
                    else:
                        v.wait_ge(bk_ps, q - 2)
                k0 = {0: 16, 1: 20}.get(q, 4 * (q - 2))
                cw_ = par("conv_w", a=24)
                for k in range(4):
                    dst = cv[:, q % 2, k, :]
                    step(v.tensor_scalar(dst, pre[:, q % 2, k, 3:3 + SEQ], cw_[:, k0 + k, 3:4],
                                         par("conv_b")[:, k0 + k:k0 + k + 1], ALU.mult, ALU.add))
                    for j in range(3):
                        ins = v.scalar_tensor_tensor(dst, pre[:, q % 2, k, j:j + SEQ], cw_[:, k0 + k, j:j + 1], dst,
                                                     ALU.mult, ALU.add)
                        if j < 2:
                            step(ins)
                ins.then_inc(cv_raw, 1)

            for q in range(6):
                following = ["C", "x0", "x1", "x2", "x3", "z0"][q]
                splits(ends[chunks[following].last] + SPL)
                convolve(q)
                if q == 0:
                    v.wait_ge(cum_ps, 1)
                    v.tensor_copy(cum[:, :, :], ps[:, 6, 0:3 * SH].rearrange("p (a b) -> p a b", a=3)).then_inc(cum_sb, 1)
                    v.wait_ge(cumT_part, 1)
                    v.tensor_tensor(cumT_rest[0:3 * SH, :], ps[0:3 * SH, 7, 0:SEQ], cumT[0:3 * SH, :],
                                    ALU.subtract).then_inc(cumT_part, 1)
                    v.wait_ge(cum_sb, 1)
                    v.tensor_tensor(dec[:, 0, :], cum[:, 2, :], cum[:, 0, :], ALU.subtract).then_inc(cum_sb, 1)
                elif q == 1:
                    low = slice(2 * SH, 3 * SH)
                    v.wait_ge(cumT_part, 3)
                    v.tensor_tensor(cumT[low, :], cumT_rest[low, :], cumT[low, :], ALU.subtract).then_inc(cumT_part, 1)
                    step(v.tensor_tensor(yt[:, 0:SH], ident[:, 0:SH], ident[:, SH:2 * SH], ALU.add))
                    v.tensor_tensor(pick[:, :], yt[:, 0:SH], ident[:, 2 * SH:3 * SH], ALU.add).then_inc(picked, 1)
            splits(ends[chunks["z1"].last] + SPL)
            v.wait_ge(cb_ps, 1)
            v.tensor_tensor(cbm[:, :, :], ps[:, 4:6, :].rearrange("p b (n c) -> p (b n) c", c=P),
                            tri.unsqueeze(1).to_broadcast([P, GROUPS * NT, P]), ALU.mult).then_inc(cb_sb, 1)
            splits(ends[chunks["z2"].last] + LAG)

            def masked_decays(i):
                g = i // 2
                if i == 0:
                    v.wait_ge(cb_sb, 1)
                v.wait_ge(seg_exp, i + 1)
                v.tensor_tensor(segs[:, i % 2], segs[:, i % 2],
                                cbm[:, NT * g:NT * (g + 1), :].unsqueeze(1).to_broadcast([P, HPU, NT, P]),
                                ALU.mult).then_inc(m_done, 1)

            def y_out(i):
                cols = slice(i * UW, (i + 1) * UW)
                v.wait_ge(y_ps, i + 1)
                v.wait_ge(dx_done, i + 1)
                off = yt[:, :].rearrange("p (h d) -> p h d", h=HPU)
                step(v.tensor_tensor(off, ps[:, 7, UW:2 * UW].rearrange("p (h d) -> p h d", h=HPU),
                                     dec[:, 1, i * HPU:(i + 1) * HPU].unsqueeze(2).to_broadcast([P, HPU, HD]), ALU.mult))
                v.tensor_tensor(xt[:, :, cols], dx[:, i % 2], ps[:, 6, :].rearrange("p (c d) -> p c d", c=NT),
                                ALU.add).then_inc(y_sb, 1)
                v.wait_ge(y_sb, i + 1)
                step(v.tensor_tensor(xt[:, 1, cols], xt[:, 1, cols], yt[:, :], ALU.add))
                v.wait_ge(*evacuated(chunks[f"z{i // 2}"].number))
                v.tensor_tensor(xt[:, :, cols], xt[:, :, cols], zt[:, :, cols], ALU.mult).then_inc(y_done, 1)

            v.wait_ge(cum_exp, 2)
            masked_decays(0)
            for i in range(1, UNITS):
                masked_decays(i)
                if i == 3:
                    splits(ends[chunks["z3"].last] + LAG)
                y_out(i - 1)

            def y_normed(gs):
                step(v.reciprocal(gss[:, 2, :, gs], gss[:, 1, :, gs]))
                for g in range(GROUPS)[gs]:
                    for c in range(NT):
                        y = xt[:, c, g * WC:(g + 1) * WC]
                        v.scalar_tensor_tensor(y, y, gss[:, 2, c, g:g + 1], gn[:, g * WC:(g + 1) * WC], ALU.mult,
                                               ALU.mult).then_inc(yn_ready, 1)

            def y_lo_part(n):
                at = (slice(None), slice(4 * (n // 2 % 2), 4 * (n // 2 % 2) + 4), tok(n % 2))
                group_lo(GROUP["ssd"] + n, *((xT_lo[at], xT_hi[at]) if n // 2 < 2 else (yT_lo[at], yT_hi[at])))

            v.wait_ge(gn_in, 16)
            v.wait_ge(grms, 1)
            y_normed(slice(0, GROUPS - 1))
            y_out(UNITS - 1)
            y_lo_part(0)
            v.wait_ge(grms, 2)
            y_normed(slice(GROUPS - 1, GROUPS))
            for n in range(1, 6):
                y_lo_part(n)
            splits(ends[chunks["o_out0"].first] + LAG)
            y_lo_part(6)
            y_lo_part(7)
            add_out("o_out0", 0)
            v.wait_ge(chunk_dve, 3)
            scaled(4, 0, GROUP["ssd"] + 8)
            splits(ends[chunks["o_out1"].first] + LAG)
            turn_lo(4, 0)
            add_out("o_out1", 1)

            v.wait_ge(chunk_dve, 4)
            scaled(4, 1)
            splits(ends[starts["experts"] - 1])
            factor(4)
            turn_lo(4, 1)
            v.wait_ge(hn_split, 1)
            for t in range(NT):
                ins = v.scalar_tensor_tensor(hn_lo[:, t, :], hn[:, t, :], stat[:, 2, t:t + 1], hn_hi[:, t, :], ALU.mult,
                                             ALU.subtract)
            ins.then_inc(hn_split, 1)
            v.wait_ge(rt_ps, 1)
            v.wait_ge(rstd_ready, 5)
            for t in range(NT):
                parts = ps[:, 4 + 2 * t, 0:2 * NE]
                step(v.tensor_scalar(lg[:, t, :], parts[:, 0:NE], stat[:, 2, t:t + 1], None, ALU.mult))
                step(v.scalar_tensor_tensor(lg[:, t, :], parts[:, NE:2 * NE], stat[:, 2, t:t + 1], lg[:, t, :], ALU.mult,
                                            ALU.add))
            for t in range(NT):
                step(v.max(lmax[:, t, :], lg[:, t, :]))
                step(v.max_index(lidx[:, t, :], lmax[:, t, :], lg[:, t, :]))
                step(v.tensor_copy(lidf[:, t, :], lidx[:, t, :]))
                for n in range(2):
                    step(v.tensor_scalar(oh[:, n, t, :], iota[:, 0:NE], lidf[:, t, n:n + 1], None, ALU.is_equal))
            v.tensor_tensor(gw[:, 0, :], lmax[:, :, 1], lmax[:, :, 0], ALU.subtract).then_inc(lw_max, 1)
            v.tensor_tensor(routed[:, :, :], oh[:, 0, :, :], oh[:, 1, :, :], ALU.add).then_inc(routed_sb, 1)
            v.wait_ge(lw_exp, 1)
            step(v.tensor_scalar(gw[:, 2, :], gw[:, 1, :], 1.0, None, ALU.add))
            step(v.reciprocal(gw[:, 2, :], gw[:, 2, :]))
            step(v.tensor_tensor(gw[:, 3, :], gw[:, 1, :], gw[:, 2, :], ALU.mult))
            for t in range(NT):
                step(v.tensor_scalar(gates[:, t, :], oh[:, 0, t, :], gw[:, 2, t:t + 1], None, ALU.mult))
                step(v.scalar_tensor_tensor(gates[:, t, :], oh[:, 1, t, :], gw[:, 3, t:t + 1], gates[:, t, :], ALU.mult,
                                            ALU.add))
            v.wait_ge(slot_ps, 1)
            v.wait_ge(routed_sb, 1)
            pos = ps[:, 5, 0:NT * NE].rearrange("p (t e) -> p t e", t=NT)
            step(v.memset(slot[:, :, :, NE:NE + 1], -1.0))
            step(v.tensor_tensor(slot[:, 0, :, 0:NE], pos, routed[:, :, :], ALU.mult))
            step(v.tensor_scalar(slot[:, 0, :, 0:NE], slot[:, 0, :, 0:NE], -1.0, None, ALU.add))
            step(v.tensor_scalar(slot[:, 1, :, :], slot[:, 0, :, :], -float(P), None, ALU.add))
            step(v.tensor_reduce(most[:, 0:1], ps[:, 5, NT * NE:(NT + 1) * NE], AX, ALU.max))
            step(v.tensor_scalar(most[:, 1:2], most[:, 0:1], P + 0.5, None, ALU.is_gt))
            v.tensor_copy(flag[:, 0:1], most[:, 1:2]).then_inc(flag_set, 1)
            def end(step_):
                return 2 * (FFN_AT[step_] + 1)

            def select(s, turn, e):
                for t in range(NT):
                    at = slice(e, e + 1) if isinstance(e, int) else bass.ds(e, 1)
                    ins = v.tensor_scalar(sel[:, t, :], iota, slot[:, turn, t, at], None, ALU.is_equal)
                ins.then_inc(s.sel, 1)

            def take_tokens_lo(s, count):
                v.wait_ge(s.xe_hi, count)
                v.tensor_tensor(xT_lo[:, :, 0:P], ps[:, 6:8, :].rearrange("p b (k c) -> p (b k) c", k=4),
                                xT_hi[:, :, 0:P], ALU.subtract).then_inc(s.xe_lo, 1)

            def result_lo(s, count):
                v.wait_ge(s.y_hi, count)
                v.tensor_tensor(y_lo[:, :], ps[:, 2:4, :].rearrange("p b c -> p (b c)"), y_hi[:, :],
                                ALU.subtract).then_inc(s.y_lo, 1)

            def add_result(s, count, e):
                v.wait_ge(s.back_ps, count)
                at = slice(e, e + 1) if isinstance(e, int) else bass.ds(e, 1)
                for t in range(NT):
                    ins = v.scalar_tensor_tensor(h[:, t, :], ps[:, 4 + 2 * t:6 + 2 * t, :].rearrange("p b c -> p (b c)"),
                                                 gates[:, t, at], h[:, t, :], ALU.mult, ALU.add)
                ins.then_inc(s.summed, 1)

            def expert(s, base, turn, e, peeled):
                first = ends[base - 1] if base else 0
                shift, count = e * NHALF + first, e * FCH
                done = [0]

                def ahead(upto):
                    while done[0] < min(upto, NHALF):
                        q = first + done[0]
                        i = base + done[0] // 2
                        k = HK * (done[0] % 2)
                        v.wait_ge(s.hi_done, e * NHALF + (q + 1))
                        v.tensor_tensor(wlo[:, q % SPL, :, :], landing(s, peeled, i, i - base)[:, k:k + HK, :],
                                        whi[:, q % SPL, :, :], ALU.subtract).then_inc(s.lo_done, 1)
                        done[0] += 1

                ahead(SPL)
                if peeled:
                    take_tokens_lo(s, 1)
                else:
                    result_lo(s, e)
                    ahead(end(("g", 0, 1)) + LAG)
                    add_result(s, e, e - 1)
                ahead(end(("u", 0, 1)) + LAG)
                prod(s, 1, shift + end(("u", 0, 1)), count, 0)
                v.wait_ge(s.selT_ps, e + 1)
                select(s, turn, e + 1)
                for j in range(1, FCH):
                    ahead(end(("u", j, 1)) + LAG)
                    if j >= 2:
                        v.wait_ge(s.aT_ps, count + (j - 1))
                    prod(s, 1, shift + end(("u", j, 1)), count + j, j)
                    aT_part_lo(s, 1, count + (j - 1), j - 1)
                ahead(end(("d", FCH - 2, 1)) + LAG)
                aT_part_lo(s, 1, count + (FCH - 1), FCH - 1)
                take_tokens_lo(s, e + 2)
                ahead(NHALF)
                if not peeled:
                    v.wait_ge(s.summed, e)

            def experts_dve(s, base, turn):
                select(s, turn, 0)
                expert(s, base, turn, 0, True)
                with v.Fori(1, NE) as e:
                    expert(s, base, turn, e, False)
                result_lo(s, NE)
                add_result(s, NE, NE - 1)
                v.wait_ge(s.summed, NE)

            experts_dve(main, starts["experts"], 0)
            v.wait_ge(flag_set, 1)
            some = v.value_load(flag[0:1, 0:1], min_val=0, max_val=1)
            with v.If(some != 0):
                experts_dve(rest, 0, 1)
            v.sem_inc(gate_ple, 1)
            sent[0] = ends[starts["experts"] + NE * NEXP - 1]
            v.wait_ge(gate_ple, 3)
            scaled(5, 0)
            scaled(5, 1)
            splits(ends[chunks["o_gate0"].first])
            factor(5)
            turn_lo(5, 0)
            turn_lo(5, 1)
            ple("o", 0)
            c = chunks["o_gate1"]
            splits(ends[c.last] + LAG)
            v.wait_ge(*evacuated(c.number))
            for t in range(NT):
                step(v.tensor_tensor(emb[:, t, WC:], emb[:, t, WC:], sg[:, 1, t, :], ALU.mult))
                v.tensor_tensor(h[:, t, WC:], h[:, t, WC:], emb[:, t, WC:], ALU.add).then_inc(gate_ple, 1)
            v.wait_ge(gain_in, 16 * 6)
            for t in range(NT):
                v.wait_ge(rms, 7 + t)
                step(v.reciprocal(stat[:, 2, t:t + 1], stat[:, 1, t:t + 1]))
                v.scalar_tensor_tensor(hn[:, t, :], h[:, t, :], stat[:, 2, t:t + 1], gain[:, :], ALU.mult,
                                       ALU.mult).then_inc(fin, 1)

        @block.tensor
        def _(pe):
            def turn(g, srcs):
                if g >= 4:
                    pe.wait_ge(tp_hi, g - 3)
                    pe.wait_ge(tp_lo, g - 3)
                for n, src in enumerate(srcs):
                    ins = pe.transpose(ps[:, bank(g), n * P:(n + 1) * P], src, ident)
                ins.then_inc(tp_ps, 1)

            def turn_hn(n, half):
                for t in range(NT):
                    pe.wait_ge(hg_ready, 4 * n + 2 * half + t + 1)
                    turn(GROUP[NORMS[n]] + 2 * half + t,
                         [hn[:, t, (4 * half + k) * P:(4 * half + k + 1) * P] for k in range(4)])

            def parts_ready(n, half):
                pe.wait_ge(tp_hi, GROUP[NORMS[n]] + 2 * half + 2)
                pe.wait_ge(tp_lo, GROUP[NORMS[n]] + 2 * half + 2)

            def three(out_ap, left, right, first, last):
                (lh, ll), (rh, rl) = left, right
                pe.matmul(out_ap, lh, rh, start=first, stop=False)
                pe.matmul(out_ap, lh, rl, start=False, stop=False)
                return pe.matmul(out_ap, ll, rh, start=False, stop=last)

            def left(x):
                return lambda k, t: (x[0][:, k, tok(t)], x[1][:, k, tok(t)])

            left_xT = left(in_xT)

            def left_y(k, t):
                return left_xT(k, t) if k < 8 else (yT_hi[:, k - 8, tok(t)], yT_lo[:, k - 8, tok(t)])

            def panel_mm(s, shift, half0, outs, left, k0, n, width, first, last, midway=None):
                for k in range(n):
                    q = half0 + k // HK
                    if k == HK and midway:
                        midway()
                    if k % HK == 0:
                        pe.wait_ge(s.lo_done, shift + (q + 1) if shift is not None else q + 1)
                    for t, o in enumerate(outs):
                        ins = three(o, left(k0 + k, t),
                                    (whi[:, q % SPL, k % HK, 0:width], wlo[:, q % SPL, k % HK, 0:width]),
                                    first and k == 0, last and k == n - 1)
                    if k % HK == HK - 1 or k == n - 1:
                        ins.then_inc(s.half_used, 1)

            def chunk(name, left=left_xT, between=None):
                c = chunks[name]
                if c.number >= 2:
                    pe.wait_ge(*evacuated(c.before))
                for n in range(c.panels):
                    if between and n in between:
                        between[n]()
                    i = c.first + n
                    k = min(KS, c.ksubs - n * KS)
                    outs = [ps[:, c.banks + t, 0:c.width] for t in range(NT)]
                    panel_mm(dense, None, ends[i] - -(-k // HK), outs, left, n * KS, k, c.width, n == 0,
                             n == c.panels - 1)

            def blocks(ap, n):
                return [ap[:, k * P:(k + 1) * P] for k in range(n)]

            pe.wait_ge(const_in, 16)
            turn_hn(0, 0)
            turn_hn(0, 1)
            parts_ready(0, 0)
            pe.wait_ge(p_in, 16)
            for i in range(2):
                turn(GROUP["ple"] + i, [pin[:, i * NT + t, k * P:(k + 1) * P] for t in range(NT) for k in range(PLE // P)])

            def turn_heads(bank, srcs):
                for k, src in enumerate(srcs):
                    ins = pe.transpose(ps[:, bank, k * P:(k + 1) * P], src, ident)
                ins.then_inc(at_ps, 1)

            def turn_lru(base, t, bank):
                for k, src in enumerate(blocks(u[:, t, base:base + LRU], 4)):
                    ins = pe.transpose(ps[:, bank, k * P:(k + 1) * P], src, ident)
                ins.then_inc(lt_ps, 1)

            def index_products():
                pe.wait_ge(at_sb, 4)
                for t in range(NT):
                    for j in range(IDXH):
                        o = ps[:, 4, j * P:(j + 1) * P] if t == 0 else \
                            ps[:, 5 + j // 2, (j % 2) * SEQ:(j % 2 + 1) * SEQ]
                        ins = pe.matmul(o, kqT[:, 6 + j // 2, tok(t)], kqT[:, 4 + j % 2, 0:(t + 1) * P], start=True, stop=True)
                    ins.then_inc(ix_ps, 1)
                pe.wait_ge(*evacuated(chunks["xr"].number))
                turn_lru(U_XR, 0, 7)

            def turn_q():
                pe.wait_ge(roped, 2)
                pe.wait_ge(ix_relu, 3)
                for t in range(NT):
                    turn_heads(5 + t, blocks(u[:, t, U_Q:U_K], 4))

            chunk("ki_wi", between={1: lambda: parts_ready(0, 1)})
            chunk("kv_qi")
            chunk("xr")
            pe.wait_ge(roped, 1)
            pe.wait_ge(tp_lo, GROUP["ple"] + 2)
            for t in range(NT):
                turn_heads(4 + t, [kdup[:, t, KVH, r].rearrange("p a d -> p (a d)") for r in range(2)] +
                           blocks(u[:, t, U_QI:U_KI], 2))
            for t in range(NT):
                turn_heads(6 + t,
                           [kdup[:, t, g, r].rearrange("p a d -> p (a d)") for g in range(KVH) for r in range(2)])
            chunk("q", between={1: index_products})
            pe.wait_ge(ix_relu, 1)
            turn_lru(U_XR, 1, 4)
            chunk("xg", between={1: turn_q})

            def gates_of_recurrence():
                pe.wait_ge(lt_sb, 2)
                pe.wait_ge(at_sb, 6)
                pe.wait_ge(*evacuated(chunks["q"].number))
                pe.wait_ge(conv_done, 1)
                pe.wait_ge(conv_pool, 1)
                for n in range(2):
                    for k in range(LRU_K):
                        ins = pe.matmul(ps[:, 2 + 2 * n + k // 2, (k % 2) * SEQ:(k % 2 + 1) * SEQ], bd[:, n, k, :], xc[:, k, :],
                                        start=True, stop=True)
                    ins.then_inc(gate_ps, 1)

            def logits(s):
                t, g, keys = s // 2, s % 2, (s // 2 + 1) * P
                if s == 0:
                    pe.wait_ge(at_sb, 6)
                elif s == 1:
                    pe.wait_ge(lt_sb, 1)
                elif s == 2:
                    pe.wait_ge(lt_sb, 4)
                elif s == 3:
                    pe.wait_ge(lg_sb, 2)
                for j in range(4):
                    hd = 4 * g + j
                    o = ps[:, 6 + s, j * P:(j + 1) * P] if t == 0 else \
                        ps[:, (0 if s == 2 else 6) + j // 2, (j % 2) * SEQ:(j % 2 + 1) * SEQ]
                    ins = pe.matmul(o, qT[:, hd // 2, tok(t)], kqT[:, 2 * g + hd % 2, 0:keys], start=True, stop=True)
                ins.then_inc(lg_ps, 1)

            def turn_probs(s):
                t = s // 2
                pe.wait_ge(pr_sb, s + 1)
                if s >= 2:
                    pe.wait_ge(pt_sb, s)
                for j in range(4):
                    for kb in range(t + 1):
                        n = j * (t + 1) + kb
                        bank = 2 + s if t == 0 else 2 + n // 4
                        ins = pe.transpose(ps[:, bank, (n % 4) * P:(n % 4 + 1) * P], probs[:, s % 2, j, tok(kb)], ident)
                ins.then_inc(pt_ps, 1)

            def attend(s):
                t, g = s // 2, s % 2
                pe.wait_ge(pt_sb, s + 1)
                for j in range(4):
                    hd = 4 * g + j
                    for kb in range(t + 1):
                        ins = pe.matmul(ps[:, 4 + t, hd * HD:(hd + 1) * HD], prT[:, j * (t + 1) + kb, :],
                                        u[:, kb, U_V + g * HD:U_V + (g + 1) * HD], start=(kb == 0), stop=(kb == t))
                ins.then_inc(o_ps, 1)

            logits(0)
            logits(1)
            gates_of_recurrence()
            pe.wait_ge(*evacuated(chunks["xg"].number))
            for t in range(NT):
                turn_lru(U_XG, t, t)
            pe.wait_ge(gate_sb, 2)
            turn_probs(0)
            turn_probs(1)
            logits(2)
            logits(3)
            attend(0)
            attend(1)
            turn_probs(2)
            attend(2)
            turn_probs(3)
            attend(3)

            def out_part(half, k0, midway=None):
                c = chunks[f"e_out{half}"]
                i = c.first if k0 else c.last
                outs = [ps[:, c.banks + t, 0:WC] for t in range(NT)]
                panel_mm(dense, None, ends[i] - KS // HK, outs, left_xT, k0, KS, WC, k0 != 0, k0 == 0, midway)

            pe.wait_ge(lru_lo, 1)
            pe.wait_ge(lg_sb, 4)
            out_part(0, KS)
            pe.wait_ge(o_sb, NT)
            for t in range(NT):
                turn(GROUP["o_attn"] + t, blocks(hn[:, t, 0:HEADS * HD], 4))
            out_part(1, KS)
            pe.wait_ge(tp_lo, GROUP["o_attn"] + 2)
            out_part(0, 0)
            out_part(1, 0, midway=lambda: turn_hn(1, 0))

            def ffn(s, nt, base, e, left_x, after_g0=None, after_u0=None, before_end=None, before_last=None, midway={}, ahead={}):
                shift = e * NHALF if e is not None else None
                count = e * FCH if e is not None else 0
                first = ends[base - 1] if base else 0
                ub = nt
                db = 4 if nt == 2 else 2

                def panel(step_, outs, left_, k0, start, stop):
                    if step_ in ahead:
                        ahead[step_]()
                    panel_mm(s, shift, first + 2 * FFN_AT[step_], outs, left_, k0, KS, WC, start, stop, midway.get(step_))

                def turn_act(j):
                    pe.wait_ge(s.prod, count + (j + 1))
                    if nt == 2:
                        pe.wait_ge(s.silu, min(j + 2, FCH))
                    elif j >= 2:
                        pe.wait_ge(s.aT_lo, count + (j - 1))
                    else:
                        pe.wait_ge(s.selT_sb, e + 1)
                    for t in range(nt):
                        bank = t if nt == 2 else 4 + j % 2
                        for k in range(4):
                            ins = pe.transpose(ps[:, bank, k * P:(k + 1) * P], act[:, j % 2, t, k * P:(k + 1) * P], ident)
                    ins.then_inc(s.aT_ps, 1)

                def down(j):
                    pe.wait_ge(s.aT_lo, count + (j + 1))
                    for half in range(2):
                        outs = [ps[:, db + 2 * t + half, :] for t in range(nt)]
                        panel(("d", j, half), outs, lambda k, t: (aT_hi[:, j % 2, k, tok(t)], aT_lo[:, j % 2, k, tok(t)]),
                              0, j == 0, j == FCH - 1)

                for j in range(FCH):
                    if j:
                        pe.wait_ge(s.silu, count + j)
                        if nt == 2 and j >= 2:
                            pe.wait_ge(s.aT_lo, j - 1)
                    for half in range(2):
                        panel(("g", j, half), [ps[:, t, :] for t in range(nt)], left_x, KS * half, half == 0, half == 1)
                    if j == 0 and after_g0:
                        after_g0()
                    if j:
                        pe.wait_ge(s.prod, count + j)
                    for half in range(2):
                        panel(("u", j, half), [ps[:, ub + t, :] for t in range(nt)], left_x, KS * half, half == 0,
                              half == 1)
                    if j == 0 and after_u0:
                        after_u0()
                    if j:
                        turn_act(j - 1)
                    if j >= 2:
                        down(j - 2)
                if before_end:
                    before_end()
                down(FCH - 2)
                turn_act(FCH - 1)
                if before_last:
                    before_last()
                down(FCH - 1)

            parts_ready(1, 0)
            pe.wait_ge(chunk_dve, 1)
            ffn(dense, NT, starts["ffn"], None, left(left_of[1]),
                midway={("g", 0, 0): lambda: turn_hn(1, 1), ("d", FCH - 1, 1): lambda: turn_hn(2, 0)},
                ahead={("g", 0, 1): lambda: parts_ready(1, 1)})

            def embed(layer, index, half):
                chunk(f"{layer}_emb{half}", lambda k, t: (pT_hi[:, index, k, tok(t)], pT_lo[:, index, k, tok(t)]))

            embed("e", 0, 0)
            turn_hn(2, 1)
            embed("e", 0, 1)
            parts_ready(2, 0)
            chunk("e_gate0", left(left_of[2]), between={1: lambda: parts_ready(2, 1)})
            chunk("e_gate1", left(left_of[2]), between={1: lambda: turn_hn(3, 0)})

            parts_ready(3, 0)
            stage = ["B", "C", "x0", "x1", "x2", "x3", "z0"]

            def forward(q):
                pe.wait_ge(*evacuated(chunks[stage[q]].number))
                if q >= 2:
                    pe.wait_ge(fw_sb, q - 1)
                    if q != 3:
                        pe.wait_ge(bk_sb, 1 if q == 2 else q - 2)
                for t in range(NT):
                    for k, src in enumerate(blocks(hn[:, t, (q % 2) * WC:(q % 2 + 1) * WC], 4)):
                        ins = pe.transpose(ps[:, 4 + 2 * (q % 2) + t, k * P:(k + 1) * P], src, ident)
                ins.then_inc(fw_ps, 1)

            def backward(q):
                pe.wait_ge(cv_done, q + 1)
                if q == 1:
                    return
                src = BT if q == 0 else cv[:, q % 2]
                for t in range(1 if q == 0 else NT):
                    for k in range(4):
                        ins = pe.transpose(ps[:, 4 + 2 * (q % 2) + t, k * P:(k + 1) * P], src[:, k, tok(t)], ident)
                ins.then_inc(bk_ps, 1)

            def second_half():
                turn_hn(3, 1)
                parts_ready(3, 1)

            chunk("B", between={1: second_half})
            chunk("dt")
            for q in range(6):
                chunk(stage[q + 1])
                if q == 1:
                    pe.wait_ge(cum_sb, 1)
                    pe.wait_ge(cumT_part, 2)
                forward(q)
                if q:
                    backward(q - 1)
                else:
                    pe.wait_ge(dt_da, 1)
                    for c in range(NT):
                        pe.matmul(ps[:, 6, c * SH:(c + 1) * SH], tri, da3[:, c, 0, :], start=True, stop=True)
                        pe.matmul(ps[0:3 * SH, 7, tok(c)], da3[:, c].rearrange("p r h -> p (r h)"), tri, start=True,
                                  stop=True)
                    pe.matmul(ps[:, 6, 2 * SH:3 * SH], ones, da3[:, 0, 0, :], start=True, stop=True).then_inc(cum_ps, 1)
            chunk("z1")
            backward(5)

            pe.wait_ge(bk_sb, 4)
            pe.wait_ge(cv_done, 2)
            for n in range(GROUPS * NT):
                ins = pe.matmul(ps[:, 4 + n // 4, (n % 4) * P:(n % 4 + 1) * P], BT[:, n // NT, tok(n % NT)],
                                CT[:, n // NT, tok(n % NT)], start=True, stop=True)
            ins.then_inc(cb_ps, 1)

            def spread_sums(i):
                if i == 0:
                    pe.wait_ge(cumT_part, 4)
                    pe.wait_ge(picked, 1)
                    pe.wait_ge(*evacuated(chunks["z1"].number))
                elif i == 1:
                    pe.wait_ge(cb_sb, 1)
                else:
                    pe.wait_ge(seg_relu, i - 1)
                for j in range(HPU):
                    hd = i * HPU + j
                    ins = pe.matmul(ps[:, 2 + 2 * (i % 2) + j // 2, (j % 2) * SEQ:(j % 2 + 1) * SEQ],
                                    pick[0:3 * SH, hd:hd + 1].to_broadcast([3 * SH, P]), cumT[0:3 * SH, :], start=True,
                                    stop=True)
                ins.then_inc(seg_ps, 1)

            def ssd(i):
                g = i // 2
                pe.wait_ge(xdt_done, 2 * i + 2)
                if i:
                    pe.wait_ge(y_sb, i)
                else:
                    pe.wait_ge(bk_sb, 5)
                pe.matmul(ps[:, 7, 0:UW], Btok[:, g, :], xtl[:, i % 2, :], start=True, stop=True).then_inc(st_ps, 1)
                pe.wait_ge(m_done, i + 1)
                for j in range(HPU):
                    for c in range(NT):
                        pe.matmul(ps[:, 6, c * UW + j * HD:c * UW + (j + 1) * HD], segs[:, i % 2, j, c, :],
                                  xdt[:, i % 2, c, j * HD:(j + 1) * HD], start=True, stop=True)
                pe.wait_ge(st_sb, i + 1)
                pe.matmul(ps[:, 7, UW:2 * UW], CT[:, g, tok(1)], st[:, i % 2, :], start=True, stop=True).then_inc(y_ps, 1)

            spread_sums(0)
            chunk("z2")
            spread_sums(1)
            for i in range(UNITS):
                if i == 2:
                    chunk("z3")
                ssd(i)
                if i + 2 < UNITS:
                    spread_sums(i + 2)
            def turn_y(ns):
                for n in ns:
                    g, t = n // 2, n % 2
                    pe.wait_ge(yn_ready, n + 1)
                    if n == 1:
                        pe.wait_ge(y_sb, UNITS)
                    turn(GROUP["ssd"] + n, blocks(xt[:, t, g * WC:(g + 1) * WC], 4))

            def y_parts_ready(g):
                pe.wait_ge(tp_lo, GROUP["ssd"] + NT * (g + 1))

            def last_group():
                turn_y(range(6, 8))
                y_parts_ready(1)

            turn_y(range(6))
            y_parts_ready(0)
            chunk("o_out0", left_y, between={1: last_group, 2: lambda: y_parts_ready(2), 3: lambda: y_parts_ready(3)})
            chunk("o_out1", left_y, between={1: lambda: turn_hn(4, 0)})

            def route(half):
                for t in range(NT):
                    for k in range(4 * half, 4 * half + 4):
                        high, low = left(left_of[4])(k, t)
                        o = ps[:, 4 + 2 * t, 0:2 * NE]
                        steps = [(o, high, rt[:, k, :]), (o[:, 0:NE], low, rt[:, k, 0:NE])]
                        last = k == DM // P - 1
                        for n, (dst, lhs, rhs) in enumerate(reversed(steps) if last else steps):
                            ins = pe.matmul(dst, lhs, rhs, start=(k == 0 and n == 0), stop=(last and n == 1))
                return ins

            embed("o", 1, 0)
            turn_hn(4, 1)
            parts_ready(4, 0)
            pe.wait_ge(rt_done, 2)
            route(0)
            parts_ready(4, 1)
            route(1).then_inc(rt_ps, 1)
            embed("o", 1, 1)
            pe.wait_ge(routed_sb, 1)
            pe.matmul(ps[:, 5, 0:NE], tri, routed[:, 0, :], start=True, stop=True)
            pe.matmul(ps[:, 5, NE:2 * NE], tri, routed[:, 1, :], start=True, stop=False)
            pe.matmul(ps[:, 5, NE:2 * NE], ones, routed[:, 0, :], start=False, stop=True)
            pe.matmul(ps[:, 5, 2 * NE:3 * NE], ones, routed[:, 0, :], start=True, stop=False)
            pe.matmul(ps[:, 5, 2 * NE:3 * NE], ones, routed[:, 1, :], start=False, stop=True).then_inc(slot_ps, 1)
            pe.wait_ge(flag_set, 1)
            pe.wait_ge(hn_split, 2)
            pe.wait_ge(setup, 1)

            def gather(s, count):
                pe.wait_ge(s.sel, count)
                for half in range(2):
                    cols = slice(half * WC, (half + 1) * WC)
                    for n, (t, part) in enumerate(((0, hn_hi), (0, hn_lo), (1, hn_hi), (1, hn_lo))):
                        ins = pe.matmul(ps[:, 6 + half, :], sel[:, t, :], part[:, t, cols], start=(n == 0), stop=(n == 3))
                ins.then_inc(s.xe_raw, 1)

            def turn_tokens(s, count):
                pe.wait_ge(s.xe_tok, count)
                for k in range(DM // P):
                    ins = pe.transpose(ps[:, 6 + k // 4, (k % 4) * P:(k % 4 + 1) * P], xe_tok[:, k * P:(k + 1) * P], ident)
                ins.then_inc(s.xe_ps, 1)

            def scatter(s, count):
                pe.wait_ge(s.y_lo, count)
                pe.wait_ge(s.xe_lo, count + 1)
                for t in range(NT):
                    for half in range(2):
                        cols = slice(half * WC, (half + 1) * WC)
                        o = ps[:, 4 + 2 * t + half, :]
                        pe.matmul(o, selT[:, tok(t)], y_hi[:, cols], start=True, stop=False)
                        ins = pe.matmul(o, selT[:, tok(t)], y_lo[:, cols], start=False, stop=True)
                ins.then_inc(s.back_ps, 1)

            def turn_selection(s, e, peeled):
                if not peeled:
                    pe.wait_ge(s.summed, e)
                for t in range(NT):
                    ins = pe.matmul(ps[:, 5, tok(t)], sel[:, t, :], ident_r[:, :], start=True, stop=True)
                ins.then_inc(s.selT_ps, 1)

            def experts_pe(s, base):
                def expert(e, peeled):
                    pe.wait_ge(s.xe_lo, e + 1)
                    ffn(s, 1, base, e, left_xT, after_g0=None if peeled else lambda: scatter(s, e),
                        after_u0=lambda: turn_selection(s, e, peeled), before_end=lambda: gather(s, e + 2),
                        before_last=lambda: turn_tokens(s, e + 2))

                gather(s, 1)
                turn_tokens(s, 1)
                expert(0, True)
                with pe.Fori(1, NE) as e:
                    expert(e, False)
                scatter(s, NE)

            experts_pe(main, starts["experts"])
            some = pe.value_load(flag[0:1, 0:1], min_val=0, max_val=1)
            with pe.If(some != 0):
                experts_pe(rest, 0)
            turn_hn(5, 0)
            turn_hn(5, 1)
            parts_ready(5, 0)
            chunk("o_gate0", between={1: lambda: parts_ready(5, 1)})
            chunk("o_gate1")


_WEIGHTS = ["e_mix_norm", "e_w_in", "e_w_out", "e_ffn_norm", "e_ffn_wg", "e_ffn_wu", "e_ffn_wd", "e_ple_proj",
            "e_ple_gate_norm", "e_ple_gate", "o_mix_norm", "o_w_in", "o_gnorm", "o_w_out", "o_moe_norm", "o_exp_wg",
            "o_exp_wu", "o_exp_wd", "o_ple_proj", "o_ple_gate_norm", "o_ple_gate", "final_norm"]


def kernel(**inputs):
    import concourse.bacc as _bacc
    from concourse.bass_utils import run_bass_kernel_spmd as _run

    nc = _bacc.Bacc("TRN2", target_bir_lowering=False, num_devices=1)
    arrays = {}

    def dram(name, a):
        a = np.ascontiguousarray(a)
        arrays[f"in_{name}_dram"] = a
        return nc.dram_tensor(f"in_{name}_dram", a.shape, mybir.dt.from_np(a.dtype), kind="ExternalInput").ap()

    r = np.arange(P)
    inv = np.float32(500000.0) ** (-np.arange(ROT, dtype=np.float32) / np.float32(ROT))
    ang = np.arange(SEQ, dtype=np.float32)[:, None] * inv[None, :].astype(np.float32)
    by_tile = lambda a: a.reshape(NT, P, ROT).transpose(1, 0, 2).reshape(P, NT * ROT)
    const = np.concatenate([
        np.eye(P), np.where(r[None, :] <= r[:, None], 0.0, NEG), r[:, None] <= r[None, :], np.ones((P, P)),
        np.broadcast_to(r[None, :], (P, P)), by_tile(np.cos(ang)), by_tile(np.sin(ang)), np.full((P, 1), EPS)],
        axis=1).astype(np.float32)

    f = {k: np.asarray(v) for k, v in inputs.items()}
    chan = lambda a: a.reshape(-1, P).T
    taps = lambda a: a.T.reshape(-1, P, 4).transpose(1, 0, 2).reshape(P, -1)
    blocks = lambda a: a.reshape(LRU_K, 2, HD, HD).transpose(1, 2, 0, 3).reshape(P, -1)
    row = lambda a: np.broadcast_to(a[None, :], (P, a.shape[0]))
    small = np.concatenate([
        taps(f["e_lru_conv_w"]), chan(f["e_lru_conv_b"]), chan(f["e_lru_ba"]), chan(f["e_lru_bx"]),
        chan(f["e_lru_lambda"]), blocks(f["e_lru_wa"]), blocks(f["e_lru_wx"]), taps(f["o_conv_w"]),
        chan(f["o_conv_b"]), row(f["o_dt_bias"]), row(f["o_a_log"]), row(f["o_d_skip"]),
        f["o_router"].reshape(DM // P, P, NE).transpose(1, 0, 2).reshape(P, -1)], axis=1)

    w = {name: dram(name, f[name]) for name in _WEIGHTS}
    x = dram("x", f["x"].reshape(SEQ, DM))
    p = dram("p", f["p"].reshape(2, SEQ, PLE))
    cst, sml = dram("const", const), dram("small", small)
    out = nc.dram_tensor("out_0_dram", (SEQ, DM), F32, kind="ExternalOutput").ap()
    build(nc, w, x, p, cst, sml, out)
    r = _run(nc, [arrays], core_ids=[0])
    return r.results[0]["out_0_dram"].reshape(1, SEQ, DM)
```
